# Optimizing a Trainium2 kernel written in Bass

```python
import math
import jax, jax.numpy as jnp
from jax import lax
import numpy as np

D_MODEL = 1024
BATCH = 1
SEQ = 512
DEPTH = 2

N_MIXERS = 2
N_NSA_LAYERS = (DEPTH + N_MIXERS - 1) // N_MIXERS
N_SSD_LAYERS = DEPTH // N_MIXERS

NSA_HEADS = 16
NSA_HEAD_DIM = 64
NSA_KV_GROUPS = 4
NSA_HEADS_PER_GROUP = NSA_HEADS // NSA_KV_GROUPS
COMP_BLOCK = 32
COMP_STRIDE = 16
COMP_HIDDEN = 256
SEL_BLOCK = 64
N_SELECT = 16
N_LOCAL_BLOCKS = 2
WINDOW = 512
N_BRANCHES = 3
WIN_Q_BLOCK = 128
SEL_Q_BLOCK = 16
NSA_Q_DIM = NSA_HEADS * NSA_HEAD_DIM
NSA_KV_DIM = NSA_KV_GROUPS * NSA_HEAD_DIM
NSA_PROJ_DIM = NSA_Q_DIM + 2 * N_BRANCHES * NSA_KV_DIM + NSA_HEADS * N_BRANCHES

SSD_EXPAND = 2
SSD_D_INNER = SSD_EXPAND * D_MODEL
SSD_HEAD_DIM = 64
SSD_HEADS = SSD_D_INNER // SSD_HEAD_DIM
SSD_GROUPS = 4
SSD_STATE = 128
SSD_CONV = 4
SSD_CHUNK = 128
SSD_CONV_DIM = SSD_D_INNER + 2 * SSD_GROUPS * SSD_STATE
SSD_PROJ_DIM = SSD_D_INNER + SSD_CONV_DIM + SSD_HEADS

FFN_HIDDEN = 2816
FFN_CONV = 3

RMS_EPS = 1e-6
NEG_INF = -1e30
SEL_FORCE = 1e9


def rms_norm(x, gain):
    xf = x.astype(jnp.float32)
    y = xf * lax.rsqrt(jnp.mean(xf * xf, axis=-1, keepdims=True) + RMS_EPS)
    return (y * gain.astype(jnp.float32)).astype(x.dtype)

def causal_dwconv(x, w, b):
    width, ch = w.shape
    y = lax.conv_general_dilated(
        x, w.astype(x.dtype)[:, None, :], window_strides=(1,),
        padding=[(width - 1, 0)], dimension_numbers=("NWC", "WIO", "NWC"),
        feature_group_count=ch)
    return y + b.astype(x.dtype)

def masked_softmax(scores, mask):
    return jax.nn.softmax(jnp.where(mask, scores, NEG_INF), axis=-1)

def compress_tokens(t, pos, w1, w2):
    b, s, g, d = t.shape
    nc = (s - COMP_BLOCK) // COMP_STRIDE + 1
    idx = np.arange(nc)[:, None] * COMP_STRIDE + np.arange(COMP_BLOCK)[None, :]
    blocks = t[:, idx] + pos.astype(t.dtype)[None, None, :, None, :]
    flat = blocks.transpose(0, 1, 3, 2, 4).reshape(b, nc, g, COMP_BLOCK * d)
    return jax.nn.gelu(flat @ w1) @ w2

def cmp_to_sel_overlap(nc, nsb):
    cs = np.arange(nc) * COMP_STRIDE
    ss = np.arange(nsb) * SEL_BLOCK
    ov = (np.minimum(cs[:, None] + COMP_BLOCK, ss[None, :] + SEL_BLOCK)
          - np.maximum(cs[:, None], ss[None, :]))
    return np.clip(ov, 0, None).astype(np.float32) / COMP_BLOCK

def nsa_mixer(h, w_in, cmp_pos, cmp_w1, cmp_w2, w_out):
    b, s, _ = h.shape
    g, hpg, hd = NSA_KV_GROUPS, NSA_HEADS_PER_GROUP, NSA_HEAD_DIM
    scale = hd ** -0.5
    kv_end = NSA_Q_DIM + 2 * N_BRANCHES * NSA_KV_DIM
    proj = h @ w_in
    q = proj[..., :NSA_Q_DIM].reshape(b, s, g, hpg, hd)
    kv = proj[..., NSA_Q_DIM:kv_end].reshape(b, s, 2 * N_BRANCHES, g, hd)
    gates = jax.nn.sigmoid(proj[..., kv_end:].astype(jnp.float32)).reshape(b, s, g, hpg, N_BRANCHES)
    k_cmp, v_cmp = kv[:, :, 0], kv[:, :, 1]
    k_sel, v_sel = kv[:, :, 2], kv[:, :, 3]
    k_win, v_win = kv[:, :, 4], kv[:, :, 5]
    pos = np.arange(s)

    kc = compress_tokens(k_cmp, cmp_pos[0], cmp_w1[0], cmp_w2[0])
    vc = compress_tokens(v_cmp, cmp_pos[1], cmp_w1[1], cmp_w2[1])
    nc = kc.shape[1]
    cmp_mask = (np.arange(nc)[None, :] * COMP_STRIDE + COMP_BLOCK - 1) <= pos[:, None]
    sc = jnp.einsum("bsghd,bcgd->bghsc", q, kc).astype(jnp.float32) * scale
    p_cmp = jnp.where(cmp_mask, masked_softmax(sc, cmp_mask), 0.0)
    o_cmp = jnp.einsum("bghsc,bcgd->bsghd", p_cmp.astype(vc.dtype), vc)

    nsb = s // SEL_BLOCK
    p_slc = jnp.einsum("bgsc,cj->bgsj", p_cmp.sum(axis=2),
                       jnp.asarray(cmp_to_sel_overlap(nc, nsb)))
    blk = np.arange(nsb)[None, :]
    cur = (pos // SEL_BLOCK)[:, None]
    allowed = blk * SEL_BLOCK <= pos[:, None]
    forced = (blk == 0) | ((blk <= cur) & (blk > cur - N_LOCAL_BLOCKS))
    sel_score = jnp.where(forced, SEL_FORCE, jnp.where(allowed, p_slc, NEG_INF))
    n_sel = min(N_SELECT, nsb)
    _, sel_idx = lax.top_k(sel_score, n_sel)
    ks_blocks = k_sel.reshape(b, nsb, SEL_BLOCK, g, hd).transpose(0, 3, 1, 2, 4).reshape(b, g, nsb, SEL_BLOCK * hd)
    vs_blocks = v_sel.reshape(b, nsb, SEL_BLOCK, g, hd).transpose(0, 3, 1, 2, 4).reshape(b, g, nsb, SEL_BLOCK * hd)
    n_qc = s // SEL_Q_BLOCK
    q_ch = q.reshape(b, n_qc, SEL_Q_BLOCK, g, hpg, hd).transpose(1, 0, 3, 4, 2, 5)
    idx_ch = sel_idx.reshape(b, g, n_qc, SEL_Q_BLOCK, n_sel).transpose(2, 0, 1, 3, 4)
    pos_ch = jnp.arange(s).reshape(n_qc, SEL_Q_BLOCK)
    n_keys = n_sel * SEL_BLOCK

    def sel_chunk(args):
        qc, ic, pc = args
        flat_idx = ic.reshape(b, g, SEL_Q_BLOCK * n_sel)[..., None]
        kg = jnp.take_along_axis(ks_blocks, flat_idx, axis=2).reshape(b, g, SEL_Q_BLOCK, n_keys, hd)
        vg = jnp.take_along_axis(vs_blocks, flat_idx, axis=2).reshape(b, g, SEL_Q_BLOCK, n_keys, hd)
        kpos = (ic[..., None] * SEL_BLOCK + jnp.arange(SEL_BLOCK)).reshape(b, g, SEL_Q_BLOCK, n_keys)
        mask = (kpos <= pc[None, None, :, None])[:, :, None]
        scs = jnp.einsum("bghqd,bgqkd->bghqk", qc, kg).astype(jnp.float32) * scale
        p = masked_softmax(scs, mask)
        return jnp.einsum("bghqk,bgqkd->bghqd", p.astype(vg.dtype), vg)

    o_sel = lax.map(sel_chunk, (q_ch, idx_ch, pos_ch)).transpose(1, 0, 4, 2, 3, 5).reshape(b, s, g, hpg, hd)

    n_wb = s // WIN_Q_BLOCK
    span = WIN_Q_BLOCK + WINDOW
    kp = jnp.pad(k_win, ((0, 0), (WINDOW, 0), (0, 0), (0, 0)))
    vp = jnp.pad(v_win, ((0, 0), (WINDOW, 0), (0, 0), (0, 0)))
    q_wb = q.reshape(b, n_wb, WIN_Q_BLOCK, g, hpg, hd).transpose(1, 0, 3, 4, 2, 5)

    def win_block(args):
        qb, i = args
        start = i * WIN_Q_BLOCK
        kb = lax.dynamic_slice_in_dim(kp, start, span, axis=1)
        vb = lax.dynamic_slice_in_dim(vp, start, span, axis=1)
        qpos = start + jnp.arange(WIN_Q_BLOCK)
        kpos = start - WINDOW + jnp.arange(span)
        mask = ((kpos[None, :] >= 0) & (kpos[None, :] <= qpos[:, None])
                & (kpos[None, :] > qpos[:, None] - WINDOW))
        scs = jnp.einsum("bghqd,bkgd->bghqk", qb, kb).astype(jnp.float32) * scale
        p = masked_softmax(scs, mask)
        return jnp.einsum("bghqk,bkgd->bghqd", p.astype(vb.dtype), vb)

    o_win = lax.map(win_block, (q_wb, jnp.arange(n_wb))).transpose(1, 0, 4, 2, 3, 5).reshape(b, s, g, hpg, hd)

    o = (gates[..., 0:1] * o_cmp + gates[..., 1:2] * o_sel + gates[..., 2:3] * o_win).astype(h.dtype)
    return o.reshape(b, s, NSA_Q_DIM) @ w_out

def ssd_scan(x, dt, a, bm, cm):
    b, s, nh, p = x.shape
    g, n = bm.shape[2], bm.shape[3]
    hg = nh // g
    L = SSD_CHUNK
    nc = s // L
    xc = x.reshape(b, nc, L, g, hg, p).transpose(1, 0, 2, 3, 4, 5)
    dtc = dt.reshape(b, nc, L, g, hg).transpose(1, 0, 2, 3, 4)
    bc = bm.reshape(b, nc, L, g, n).transpose(1, 0, 2, 3, 4)
    cc = cm.reshape(b, nc, L, g, n).transpose(1, 0, 2, 3, 4)
    a_g = a.reshape(g, hg)
    causal = np.tril(np.ones((L, L), dtype=bool))[None, :, :, None, None]

    def step(state, inp):
        x_k, dt_k, b_k, c_k = inp
        acs = jnp.cumsum(dt_k * a_g, axis=1)
        seg = acs[:, :, None] - acs[:, None, :]
        lmat = jnp.exp(jnp.where(causal, seg, -jnp.inf))
        cb = jnp.einsum("blgn,bsgn->blsg", c_k, b_k)
        w = cb[..., None] * lmat * dt_k[:, None]
        y = jnp.einsum("blsgh,bsghp->blghp", w, x_k)
        y = y + jnp.einsum("blgn,bghpn->blghp", c_k, state) * jnp.exp(acs)[..., None]
        decay = jnp.exp(acs[:, -1:] - acs) * dt_k
        state = (state * jnp.exp(acs[:, -1])[..., None, None]
                 + jnp.einsum("bsgn,bsgh,bsghp->bghpn", b_k, decay, x_k))
        return state, y

    state0 = jnp.zeros((b, g, hg, p, n), jnp.float32)
    _, ys = lax.scan(step, state0, (xc, dtc, bc, cc))
    return ys.transpose(1, 0, 2, 3, 4, 5).reshape(b, s, nh, p)

def ssd_mixer(h, w_in, conv_w, conv_b, dt_bias, a_log, d_skip, norm_w, w_out):
    b, s, _ = h.shape
    f32 = jnp.float32
    gn = SSD_GROUPS * SSD_STATE
    proj = h @ w_in
    z = proj[..., :SSD_D_INNER]
    xbc = jax.nn.silu(causal_dwconv(proj[..., SSD_D_INNER:SSD_D_INNER + SSD_CONV_DIM], conv_w, conv_b))
    dt_raw = proj[..., SSD_D_INNER + SSD_CONV_DIM:]
    x_ssm = xbc[..., :SSD_D_INNER].astype(f32).reshape(b, s, SSD_HEADS, SSD_HEAD_DIM)
    bm = xbc[..., SSD_D_INNER:SSD_D_INNER + gn].astype(f32).reshape(b, s, SSD_GROUPS, SSD_STATE)
    cm = xbc[..., SSD_D_INNER + gn:].astype(f32).reshape(b, s, SSD_GROUPS, SSD_STATE)
    dt = jax.nn.softplus(dt_raw.astype(f32) + dt_bias.astype(f32))
    a = -jnp.exp(a_log.astype(f32))
    y = ssd_scan(x_ssm, dt, a, bm, cm) + d_skip.astype(f32)[:, None] * x_ssm
    y = y.reshape(b, s, SSD_D_INNER) * jax.nn.silu(z.astype(f32))
    yg = y.reshape(b, s, SSD_GROUPS, SSD_D_INNER // SSD_GROUPS)
    yg = yg * lax.rsqrt(jnp.mean(yg * yg, axis=-1, keepdims=True) + RMS_EPS)
    y = (yg.reshape(b, s, SSD_D_INNER) * norm_w.astype(f32)).astype(h.dtype)
    return y @ w_out

def conv_ffn(h, w_up, conv_w, conv_b, w_down):
    u = causal_dwconv(h @ w_up, conv_w, conv_b)
    val, gate = u[..., :FFN_HIDDEN], u[..., FFN_HIDDEN:]
    return (jax.nn.silu(gate) * val) @ w_down

def first_inputs(seed: int = 0) -> dict:
    key = jax.random.key(seed)
    ks = jax.random.split(key, 19)
    f32 = jnp.float32

    def dense(k, shape, fan_in):
        return jax.random.normal(k, shape, f32) * fan_in ** -0.5

    x = jax.random.normal(ks[0], (BATCH, SEQ, D_MODEL), f32)
    norm_gains = 1.0 + 0.05 * jax.random.normal(ks[1], (DEPTH, 4, D_MODEL), f32)
    nsa_w_in = dense(ks[2], (N_NSA_LAYERS, D_MODEL, NSA_PROJ_DIM), D_MODEL)
    nsa_cmp_pos = 0.1 * jax.random.normal(ks[3], (N_NSA_LAYERS, 2, COMP_BLOCK, NSA_HEAD_DIM), f32)
    nsa_cmp_w1 = dense(ks[4], (N_NSA_LAYERS, 2, COMP_BLOCK * NSA_HEAD_DIM, COMP_HIDDEN), COMP_BLOCK * NSA_HEAD_DIM)
    nsa_cmp_w2 = dense(ks[5], (N_NSA_LAYERS, 2, COMP_HIDDEN, NSA_HEAD_DIM), COMP_HIDDEN)
    nsa_w_out = dense(ks[6], (N_NSA_LAYERS, NSA_Q_DIM, D_MODEL), NSA_Q_DIM)
    ssd_w_in = dense(ks[7], (N_SSD_LAYERS, D_MODEL, SSD_PROJ_DIM), D_MODEL)
    ssd_conv_w = dense(ks[8], (N_SSD_LAYERS, SSD_CONV, SSD_CONV_DIM), SSD_CONV)
    ssd_conv_b = 0.02 * jax.random.normal(ks[9], (N_SSD_LAYERS, SSD_CONV_DIM), f32)
    dt0 = jnp.exp(jax.random.uniform(ks[10], (N_SSD_LAYERS, SSD_HEADS), f32,
                                     minval=math.log(1e-3), maxval=math.log(1e-1)))
    ssd_dt_bias = dt0 + jnp.log(-jnp.expm1(-dt0))
    ssd_a_log = jnp.log(jax.random.uniform(ks[11], (N_SSD_LAYERS, SSD_HEADS), f32, minval=1.0, maxval=16.0))
    ssd_d = 1.0 + 0.05 * jax.random.normal(ks[12], (N_SSD_LAYERS, SSD_HEADS), f32)
    ssd_norm_w = 1.0 + 0.05 * jax.random.normal(ks[13], (N_SSD_LAYERS, SSD_D_INNER), f32)
    ssd_w_out = dense(ks[14], (N_SSD_LAYERS, SSD_D_INNER, D_MODEL), SSD_D_INNER)
    ffn_w_up = dense(ks[15], (DEPTH, D_MODEL, 2 * FFN_HIDDEN), D_MODEL)
    ffn_conv_w = dense(ks[16], (DEPTH, FFN_CONV, 2 * FFN_HIDDEN), FFN_CONV)
    ffn_conv_b = 0.02 * jax.random.normal(ks[17], (DEPTH, 2 * FFN_HIDDEN), f32)
    ffn_w_down = dense(ks[18], (DEPTH, FFN_HIDDEN, D_MODEL), FFN_HIDDEN)
    return {
        "x": x, "norm_gains": norm_gains,
        "nsa_w_in": nsa_w_in, "nsa_cmp_pos": nsa_cmp_pos, "nsa_cmp_w1": nsa_cmp_w1,
        "nsa_cmp_w2": nsa_cmp_w2, "nsa_w_out": nsa_w_out,
        "ssd_w_in": ssd_w_in, "ssd_conv_w": ssd_conv_w, "ssd_conv_b": ssd_conv_b,
        "ssd_dt_bias": ssd_dt_bias, "ssd_a_log": ssd_a_log, "ssd_d": ssd_d,
        "ssd_norm_w": ssd_norm_w, "ssd_w_out": ssd_w_out,
        "ffn_w_up": ffn_w_up, "ffn_conv_w": ffn_conv_w, "ffn_conv_b": ffn_conv_b,
        "ffn_w_down": ffn_w_down,
    }

def first_block(x, norm_gains, nsa_w_in, nsa_cmp_pos, nsa_cmp_w1, nsa_cmp_w2, nsa_w_out,
              ssd_w_in, ssd_conv_w, ssd_conv_b, ssd_dt_bias, ssd_a_log, ssd_d, ssd_norm_w,
              ssd_w_out, ffn_w_up, ffn_conv_w, ffn_conv_b, ffn_w_down):
    h = x
    for i in range(DEPTH):
        gains = norm_gains[i]
        slot = i // N_MIXERS
        hn = rms_norm(h, gains[0])
        if i % N_MIXERS == 0:
            m = nsa_mixer(hn, nsa_w_in[slot], nsa_cmp_pos[slot], nsa_cmp_w1[slot],
                          nsa_cmp_w2[slot], nsa_w_out[slot])
        else:
            m = ssd_mixer(hn, ssd_w_in[slot], ssd_conv_w[slot], ssd_conv_b[slot],
                          ssd_dt_bias[slot], ssd_a_log[slot], ssd_d[slot],
                          ssd_norm_w[slot], ssd_w_out[slot])
        h = h + rms_norm(m, gains[1])
        f = conv_ffn(rms_norm(h, gains[2]), ffn_w_up[i], ffn_conv_w[i], ffn_conv_b[i], ffn_w_down[i])
        h = h + rms_norm(f, gains[3])
    return h


DEPTH_2 = 1

CHUNK = 64
CONV_WIDTH = 3
N_HEADS = 16
HEAD_DIM = D_MODEL // N_HEADS
LEFT_CHUNKS = 8
BAND = (LEFT_CHUNKS + 1) * CHUNK
MAX_REL_DIST = 256
N_REL = 2 * MAX_REL_DIST + 1
D_FF = (((8 * D_MODEL + 2) // 3 + 255) // 256) * 256
N_CONV_LAYERS = (DEPTH_2 + N_MIXERS - 1) // N_MIXERS
N_ATTN_LAYERS = DEPTH_2 // N_MIXERS
N_ADA = 6
NEG_INF_2 = -1e30


def rms_norm_2(x, g):
    xf = x.astype(jnp.float32)
    y = xf * lax.rsqrt(jnp.mean(xf * xf, axis=-1, keepdims=True) + RMS_EPS)
    return (y * g.astype(jnp.float32)).astype(x.dtype)

def modulate(h, shift, scale):
    return h * (1.0 + scale[:, None, :]) + shift[:, None, :]

def short_conv_mixer(h, w_in, w_conv, w_out):
    d = h.shape[-1]
    bcv = h @ w_in
    gate_b, gate_c, v = jnp.split(bcv, 3, axis=-1)
    u = gate_c * v
    conv = lax.conv_general_dilated(
        u, w_conv[:, None, :].astype(u.dtype),
        window_strides=(1,), padding=[(CONV_WIDTH - 1, 0)],
        dimension_numbers=("NWC", "WIO", "NWC"), feature_group_count=d)
    return (gate_b * conv) @ w_out

def _rel_bias_index():
    qi = np.arange(CHUNK)[:, None]
    kj = np.arange(BAND)[None, :]
    dist = qi + LEFT_CHUNKS * CHUNK - kj
    return (np.clip(dist, -MAX_REL_DIST, MAX_REL_DIST) + MAX_REL_DIST).astype(np.int32)

def chunked_rel_attention(h, w_qkv, rel_bias, w_out):
    b, s, d = h.shape
    n_chunks = s // CHUNK
    qkv = (h @ w_qkv).reshape(b, s, 3, N_HEADS, HEAD_DIM)
    q = qkv[:, :, 0] * (HEAD_DIM ** -0.5)
    k = qkv[:, :, 1]
    v = qkv[:, :, 2]
    pad = ((0, 0), (LEFT_CHUNKS * CHUNK, 0), (0, 0), (0, 0))
    k_pad = jnp.pad(k, pad)
    v_pad = jnp.pad(v, pad)
    q_chunks = q.reshape(b, n_chunks, CHUNK, N_HEADS, HEAD_DIM).transpose(1, 0, 2, 3, 4)
    bias = rel_bias.astype(jnp.float32)[:, jnp.asarray(_rel_bias_index())]
    key_slot = jnp.arange(BAND)

    def one_chunk(args):
        n, qc = args
        kb = lax.dynamic_slice_in_dim(k_pad, n * CHUNK, BAND, axis=1)
        vb = lax.dynamic_slice_in_dim(v_pad, n * CHUNK, BAND, axis=1)
        scores = jnp.einsum("bqhd,bkhd->bhqk", qc, kb).astype(jnp.float32) + bias[None]
        valid = key_slot >= (LEFT_CHUNKS - n) * CHUNK
        scores = jnp.where(valid[None, None, None, :], scores, NEG_INF_2)
        p = jax.nn.softmax(scores, axis=-1).astype(vb.dtype)
        return jnp.einsum("bhqk,bkhd->bqhd", p, vb)

    out = lax.map(one_chunk, (jnp.arange(n_chunks, dtype=jnp.int32), q_chunks))
    out = out.transpose(1, 0, 2, 3, 4).reshape(b, s, d)
    return out @ w_out

def swiglu(h, w_gate_up, w_down):
    g, u = jnp.split(h @ w_gate_up, 2, axis=-1)
    return (jax.nn.silu(g) * u) @ w_down

def second_inputs(seed: int = 0) -> dict:
    key = jax.random.key(seed)
    ks = jax.random.split(key, 14)
    f32 = jnp.float32
    sd = D_MODEL ** -0.5
    x = jax.random.normal(ks[0], (BATCH, SEQ, D_MODEL), f32)
    c = jax.random.normal(ks[1], (BATCH, D_MODEL), f32)
    ada_w = jax.random.normal(ks[2], (DEPTH_2, D_MODEL, N_ADA * D_MODEL), f32) * (0.5 * sd)
    ada_b = jax.random.normal(ks[3], (DEPTH_2, N_ADA * D_MODEL), f32) * 0.02
    norm_gains = 1.0 + 0.02 * jax.random.normal(ks[4], (DEPTH_2, 4, D_MODEL), f32)
    conv_w_in = jax.random.normal(ks[5], (N_CONV_LAYERS, D_MODEL, 3 * D_MODEL), f32) * sd
    conv_w = jax.random.normal(ks[6], (N_CONV_LAYERS, CONV_WIDTH, D_MODEL), f32) * (CONV_WIDTH ** -0.5)
    conv_w_out = jax.random.normal(ks[7], (N_CONV_LAYERS, D_MODEL, D_MODEL), f32) * sd
    attn_w_qkv = jax.random.normal(ks[8], (N_ATTN_LAYERS, D_MODEL, 3 * D_MODEL), f32) * sd
    attn_rel_bias = jax.random.normal(ks[9], (N_ATTN_LAYERS, N_HEADS, N_REL), f32) * 0.1
    attn_w_out = jax.random.normal(ks[10], (N_ATTN_LAYERS, D_MODEL, D_MODEL), f32) * sd
    ffn_w_gate_up = jax.random.normal(ks[11], (DEPTH_2, D_MODEL, 2 * D_FF), f32) * sd
    ffn_w_down = jax.random.normal(ks[12], (DEPTH_2, D_FF, D_MODEL), f32) * (D_FF ** -0.5)
    return {"x": x, "c": c, "ada_w": ada_w, "ada_b": ada_b, "norm_gains": norm_gains,
            "conv_w_in": conv_w_in, "conv_w": conv_w, "conv_w_out": conv_w_out,
            "attn_w_qkv": attn_w_qkv, "attn_rel_bias": attn_rel_bias, "attn_w_out": attn_w_out,
            "ffn_w_gate_up": ffn_w_gate_up, "ffn_w_down": ffn_w_down}

def second_block(x, c, ada_w, ada_b, norm_gains, conv_w_in, conv_w, conv_w_out,
              attn_w_qkv, attn_rel_bias, attn_w_out, ffn_w_gate_up, ffn_w_down):
    c_act = jax.nn.silu(c)
    for i in range(DEPTH_2):
        mod = c_act @ ada_w[i] + ada_b[i]
        sh_m, sc_m, g_m, sh_f, sc_f, g_f = jnp.split(mod, N_ADA, axis=-1)
        h = modulate(rms_norm_2(x, norm_gains[i, 0]), sh_m, sc_m)
        j = i // N_MIXERS
        if i % N_MIXERS == 0:
            h = short_conv_mixer(h, conv_w_in[j], conv_w[j], conv_w_out[j])
        else:
            h = chunked_rel_attention(h, attn_w_qkv[j], attn_rel_bias[j], attn_w_out[j])
        x = x + g_m[:, None, :] * rms_norm_2(h, norm_gains[i, 1])
        h = modulate(rms_norm_2(x, norm_gains[i, 2]), sh_f, sc_f)
        h = swiglu(h, ffn_w_gate_up[i], ffn_w_down[i])
        x = x + g_f[:, None, :] * rms_norm_2(h, norm_gains[i, 3])
    return x


def setup_inputs(seed=0):
    out = dict(first_inputs(seed))
    for name, value in second_inputs(seed + 1).items():
        if name != "x":
            out[name + "_2"] = value
    return out


def reference(
    x, norm_gains, nsa_w_in, nsa_cmp_pos, nsa_cmp_w1, nsa_cmp_w2, nsa_w_out, ssd_w_in,
    ssd_conv_w, ssd_conv_b, ssd_dt_bias, ssd_a_log, ssd_d, ssd_norm_w, ssd_w_out, ffn_w_up,
    ffn_conv_w, ffn_conv_b, ffn_w_down, c_2, ada_w_2, ada_b_2, norm_gains_2, conv_w_in_2,
    conv_w_2, conv_w_out_2, attn_w_qkv_2, attn_rel_bias_2, attn_w_out_2, ffn_w_gate_up_2,
    ffn_w_down_2,
):
    x = first_block(
        x, norm_gains, nsa_w_in, nsa_cmp_pos, nsa_cmp_w1, nsa_cmp_w2, nsa_w_out, ssd_w_in,
        ssd_conv_w, ssd_conv_b, ssd_dt_bias, ssd_a_log, ssd_d, ssd_norm_w, ssd_w_out, ffn_w_up,
        ffn_conv_w, ffn_conv_b, ffn_w_down,
    )
    return second_block(
        x, c_2, ada_w_2, ada_b_2, norm_gains_2, conv_w_in_2, conv_w_2, conv_w_out_2,
        attn_w_qkv_2, attn_rel_bias_2, attn_w_out_2, ffn_w_gate_up_2, ffn_w_down_2,
    )


_drawn_inputs = setup_inputs


def setup_inputs(seed=0):
    import zlib

    import numpy as np

    out = dict(_drawn_inputs(seed))
    spreads = {}
    factors = {'ssd_conv_b': 3.601, 'ssd_d': 3.685, 'ada_b_2': 3.679, 'norm_gains_2': 8.0}
    for name, (base, spread) in spreads.items():
        noise = np.random.default_rng([zlib.crc32(name.encode()), seed]).standard_normal(out[name].shape)
        drawn = base * np.exp(spread * noise) if base else spread * noise
        out[name] = __import__('jax').numpy.asarray(drawn.astype(out[name].dtype))
    for name, factor in factors.items():
        out[name] = (out[name] * factor).astype(out[name].dtype)
    return out
```

```python
from contextlib import ExitStack

import numpy as np

import concourse.bass as bass
from concourse import mybir

F32 = mybir.dt.float32
F32R = mybir.dt.float32r
ALU = mybir.AluOpType
ACT = mybir.ActivationFunctionType
AX = mybir.AxisListType

P = 128
S = 512
NT = S // P
D = 1024
KD = D // P
FH = 2816
KF = FH // P
HALF_F = KF // 2
HD = 64
NQ = 8
NC = (S - 32) // 16 + 1
SH = 32
CH = 24
NZ = 16
EPS = 1e-6
NEG = -1e30
QSCALE = HD ** -0.5
ADA_SLICE = 768
ADA_SLICES = 6 * D // ADA_SLICE

PHASES = [
    ("NSA_IN", 21, 8, 1), ("NSA_OUT", 8, 8, 1), ("UP1", 44, 8, 1), ("DOWN1", 16, HALF_F, 2),
    ("SSD_IN", 41, 8, 1), ("SSD_OUT", 16, 8, 2), ("UP2", 44, 8, 1), ("DOWN2", 16, HALF_F, 2),
    ("CONV_IN", 24, 8, 1), ("CONV_OUT", 8, 8, 1), ("UP3", 44, 8, 1), ("DOWN3", 16, HALF_F, 2),
]
START, COUNT, BLOCKS, PER_TILE, DRAM_AT = {}, {}, {}, {}, {}
PANEL_BLOCKS = []
_at8 = _at11 = 0
for _name, _n, _nb, _pt in PHASES:
    START[_name], COUNT[_name], BLOCKS[_name], PER_TILE[_name] = len(PANEL_BLOCKS), _n, _nb, _pt
    if _nb == 8:
        DRAM_AT[_name] = _at8
        _at8 += _n
    else:
        DRAM_AT[_name] = _at11
        _at11 += _n
    PANEL_BLOCKS += [_nb] * _n
TOTAL = len(PANEL_BLOCKS)
N8, N11 = _at8, _at11

OPERANDS = [("NSA_IN", 8), ("NSA_OUT", 8), ("UP1", 8), ("DOWN1", KF), ("SSD_IN", 8), ("SSD_OUT", NZ),
            ("UP2", 8), ("DOWN2", KF), ("CONV_IN", 8), ("CONV_OUT", 8), ("UP3", 8), ("DOWN3", KF)]
XT = {}
_n = 0
for _name, _k in OPERANDS:
    XT[_name] = _n
    _n += _k
EV, MV = {}, {}
_n = 0
for _name, _k in [("NSA_IN", 17), ("UP1", 44), ("SSD_IN", 41), ("UP2", 44), ("CONV_IN", 24), ("UP3", 44)]:
    EV[_name] = _n
    _n += _k
_n = 0
for _name in ["NSA_OUT", "DOWN1", "SSD_OUT", "DOWN2", "CONV_OUT", "DOWN3"]:
    MV[_name] = _n
    _n += 8
(Q_NSA_PRE, Q_NSA_POST, Q_F1_PRE, Q_F1_POST, Q_SSD_PRE, Q_GROUP, _a, _b, _c, Q_SSD_POST, Q_F2_PRE, Q_F2_POST,
 Q_CONV_PRE, Q_CONV_POST, Q_F3_PRE, Q_F3_POST) = range(16)

PARAMS = [("gains", 64), ("gains2", 32), ("ssd_w", CH * 4), ("ssd_b", CH), ("ffn_w", 2 * 44 * 3), ("ffn_b", 2 * 44),
          ("dskip", NZ), ("norm_w", NZ), ("c", KD), ("ada_b", 48), ("pos", 32), ("w2", 256), ("cw", 8 * 3)]
COL = {}
_n = 0
for _name, _k in PARAMS:
    COL[_name] = _n
    _n += _k
NPAR = _n


class Chain:

    def __init__(self, eng, sem):
        self.eng, self.sem, self.n, self.off = eng, sem, 0, 0

    def __call__(self, ins):
        ins.then_inc(self.sem, 1)
        self.n += 1
        return self.n + self.off

    def wait(self, value=None):
        self.eng.wait_ge(self.sem, self.n + self.off if value is None else value)


def static(i):
    return isinstance(i, int)


def walk(eng, n, step, chain=None, per=0):
    groups = n // 4
    for c in range(4):
        step(c, 0)
    if groups > 2:
        before = chain.n if chain else 0
        with eng.Fori(1, groups - 1) as i:
            if chain:
                chain.off = (i - 1) * per
            for c in range(4):
                step(c, i)
        if chain:
            assert chain.n - before == per, (chain.n - before, per)
            chain.n = before + per * (groups - 2)
            chain.off = 0
    for c in range(4 * (groups - 1), n):
        step(c, 0)


def ssd_walk(eng, step, zone, chain=None, per_conv=0, per_z=0):
    for c in range(4):
        step(c, 0)
    for is_z, (a, b), per in ((False, (1, 6), per_conv), (True, (6, 10), per_z)):
        zone["z"] = is_z
        before = chain.n if chain else 0
        with eng.Fori(a, b) as i:
            if chain:
                chain.off = (i - a) * per
            for c in range(4):
                step(c, i)
        if chain:
            assert chain.n - before == per, (chain.n - before, per)
            chain.n, chain.off = before + per * (b - a), 0
    zone["z"] = False
    step(40, 0)


def build(nc, w8, w11, xT, params, heads, w_cmp, w_ada, out, stop=None):
    with ExitStack() as ctx:
        def sem(name):
            return ctx.enter_context(nc.semaphore(name))

        base = [16512]

        def sb(name, shape, dt=F32, at=None):
            size = 4 * int(np.prod(shape[1:]))
            size = (size + 31) // 32 * 32
            if at is None:
                at = base[0]
                base[0] += size
            assert at + size <= 229344, (name, at + size)
            t = nc.alloc_sbuf_tensor_at(name, shape, dt, offset=at)
            ends[name] = at + size
            return t

        ends = {}
        h = sb("h", [P, KD, S])
        RAWW = HALF_F * P
        raw = [sb(f"raw{k}", [P, RAWW]) for k in range(4)]
        whi = [sb(f"whi{k}", [P, RAWW], F32R) for k in range(2)]
        wlo = [sb(f"wlo{k}", [P, RAWW], F32R) for k in range(2)]
        rstd_b = sb("rstd_b", [P, S])
        ssum = sb("ssum", [P, S])
        sqr = sb("sqr", [P, 2, S])
        tmp = sb("tmp", [P, 2, S])
        ident = sb("ident", [P, P])
        ones = sb("ones", [P, P])
        par = sb("par", [P, NPAR])
        hpar = sb("hpar", [SH, 4])
        small = sb("small", [P, 32])
        csil = sb("csil", [P, KD])
        mod = sb("mod", [P, 48])
        gmod = sb("gmod", [P, 4, KD])
        epsc = sb("epsc", [P, 1])
        ms, root, rt = small[:, 0:4], small[:, 4:8], small[:, 8:12]
        arena = base[0]

        def at(kb):
            return arena + int(kb * 1024)

        xhi = sb("xhi", [P, KD, S], F32R, at(0))
        xlo = sb("xlo", [P, KD, S], F32R, at(16))
        m_x = sb("m_x", [P, KD, S], F32, at(0))
        hid_hi = sb("hid_hi", [P, KF, S], F32R, at(32))
        hid_lo = sb("hid_lo", [P, KF, S], F32R, at(76))
        UP = 516
        upad = sb("upad", [P, 2, UP], F32, at(120))
        sg = sb("sg", [P, S], F32, at(124.125))
        hid = sb("hid", [P, S], F32, at(126.125))
        qkv = sb("qkv", [P, 16, S], F32, at(32))
        m_alt = sb("m_alt", [P, KD, S], F32, at(32))
        vtok = sb("vtok", [P, NT, S], F32, at(64))
        swp = sb("swp", [P, 4, S], F32, at(72))
        flat = sb("flat", [P, 16, 4, NC], F32, at(80))
        w1st = sb("w1st", [P, 16, 256], F32, at(88))
        pbuf = sb("pbuf", [P, 2, 2, S], F32, at(80))
        pt = sb("pt", [P, 2, 2, S], F32, at(88))
        qst = sb("qst", [P, S], F32, at(96))
        hg = sb("hg", [P, 2, 4 * NC], F32, at(104))
        kct = sb("kct", [P, 2, NC], F32, at(105))
        vct = sb("vct", [NC, 4, HD], F32, at(105.5))
        pcmp = sb("pcmp", [P, 2, 32], F32, at(106.5))
        ptc = sb("ptc", [NC, 2, P], F32, at(107))
        gt = sb("gt", [48, S], F32, at(108))
        gtok = sb("gtok", [P, NT, 48], F32, at(110))
        mbig = sb("mbig", [P, S], F32, at(111))
        mcmp = sb("mcmp", [P, NT, NC], F32, at(113))
        stat = sb("stat", [P, 2, 32], F32, at(113.75))
        ada_acc = sb("ada_acc", [P, ADA_SLICE], F32, at(114))
        ada_w = sb("ada_w", [P, 2, ADA_SLICE], F32, at(117))
        rowok = sb("rowok", [P, 1], F32, at(123))
        cv = sb("cv", [P, CH, S], F32, at(32))
        zb = sb("zb", [P, NZ, S], F32, at(80))
        yhi = sb("yhi", [P, NZ, S], F32R, at(48))
        ylo = sb("ylo", [P, NZ, S], F32R, at(16))
        xdt = sb("xdt", [P, SH, HD], F32, at(0))
        xdec = sb("xdec", [P, SH, HD], F32, at(8))
        state = sb("state", [P, SH, HD], F32, at(16))
        btok = sb("btok", [P, 4, P], F32, at(24))
        ebuf = sb("ebuf", [P, 2, S], F32, at(26))
        usum = sb("usum", [P, P], F32, at(30))
        smask = sb("smask", [P, P], F32, at(30.5))
        cbuf = sb("cbuf", [P, P], F32, at(31))
        xbuf = sb("xbuf", [P, 2, S], F32, at(112))
        spad = sb("spad", [P, UP], F32, at(116))
        cacc = sb("cacc", [P, 2, S], F32, at(118.25))
        dtt = sb("dtt", [SH, 2, S], F32, at(122.25))
        dtk = sb("dtk", [P, NT, 2, SH], F32, at(126.25))
        acs = sb("acs", [P, 3, SH], F32, at(127.25))
        dw = sb("dw", [SH, 5, S], F32, at(0))
        cc = sb("cc", [P, KD, S], F32, at(32))
        cy = sb("cy", [P, KD, S], F32, at(48))
        yc_hi = sb("yc_hi", [P, KD, S], F32R, at(64))
        yc_lo = sb("yc_lo", [P, KD, S], F32R, at(80))
        m_conv = sb("m_conv", [P, KD, S], F32, at(96))
        cpad = sb("cpad", [P, UP], F32, at(112))
        cyt = sb("cyt", [P, 2, S], F32, at(115))

        bank = [ctx.enter_context(nc.psum_tensor(f"bank{k}", [P, 512], F32)) for k in range(8)]
        stat_ps, bc_ps = bank[5], bank[4]

        s_raw = [sem(f"raw_landed{k}") for k in range(4)]
        s_in = sem("inputs_landed")
        s_const = sem("constants_made")
        s_carry = [sem(f"waits_taken_{e}") for e in ("sp", "dve", "pool")]
        s_hi = sem("weight_hi_made")
        s_lo = sem("weight_lo_made")
        s_pe = sem("panels_multiplied")
        s_ev = sem("in_tiles_taken")
        s_m = sem("out_tiles_taken")
        s_xh = sem("operand_hi_made")
        s_xt = sem("operand_lo_made")
        s_h = sem("residual_updated")
        s_sa = sem("squares_made")
        s_pa = sem("squares_added")
        s_sq = sem("square_sums_made")
        s_stat = sem("token_sums_made")
        s_ms = sem("mean_squares_made")
        s_sqrt = sem("roots_made")
        s_diag = sem("diagonals_made")
        s_bc = sem("rstd_spread")
        s_rb = sem("rstd_kept")
        s_dve = sem("dve_chain")
        s_act = sem("act_chain")
        s_pool = sem("pool_chain")
        s_cg = sem("gates_convolved")
        s_sg = sem("gates_silu")
        s_hid = sem("hidden_made")
        s_gate = sem("gates_sigmoid")
        s_gtp = sem("gates_turned")
        s_v = sem("v_panels_taken")
        s_swp = sem("halves_swapped")
        s_w1 = sem("compress_w1_landed")
        s_flat = sem("blocks_flattened")
        s_cm = sem("compress_matmuls")
        s_gelu = sem("compress_gelu")
        s_kv = sem("compressed_kept")
        s_qst = sem("q_staged")
        s_S = sem("scores_made")
        s_sc = sem("scores_masked")
        s_nb = sem("negative_max_made")
        s_e = sem("exps_made")
        s_P = sem("probs_scaled")
        s_T = sem("probs_turned")
        s_tv = sem("turned_kept_dve")
        s_ta = sem("turned_kept_act")
        s_pv = sem("pv_made")
        s_ada_w = [sem(f"ada_w_landed{k}") for k in range(2)]
        s_ada = sem("ada_slices_summed")
        s_adap = sem("ada_slices_spread")
        s_csil = sem("c_silu")
        s_cacc = sem("conv_sums_made")
        s_cv = sem("conv_silu_made")
        s_dt = sem("dt_steps")
        s_dta = sem("dt_act_steps")
        s_dtp = sem("dt_turned")
        s_dtk = sem("dt_kept")
        s_xtp = sem("x_turned")
        s_xd = sem("x_dt_made")
        s_bt = sem("b_kept")
        s_ac = sem("cumsums_made")
        s_acv = sem("cumsums_kept")
        s_dec = sem("decays_made")
        s_xdec = sem("x_decayed")
        s_cb = sem("cb_made")
        s_cbk = sem("cb_kept")
        s_lb = sem("cumsums_spread")
        s_ein = sem("segments_made")
        s_ee = sem("segment_exps")
        s_xe = sem("spread_exps")
        s_w = sem("ssd_weights_made")
        s_cx = sem("c_scaled")
        s_y = sem("y_made")
        s_yk = sem("y_kept")
        s_st = sem("state_products")
        s_stk = sem("state_kept")
        s_out = sem("out_stored")

        def col(name, k=0, rows=P):
            c = COL[name] + k
            return par[0:rows, c:c + 1]

        block = ctx.enter_context(nc.Block())

        def psum_ap(t):
            return bank[t][:, :]

        @block.sync
        def _(sp):
            sp.dma_start(h[:, 0:4, :], xT[:, 0:4, :]).then_inc(s_in, 16)
            sp.dma_start(h[:, 4:8, :], xT[:, 4:8, :]).then_inc(s_in, 16)
            sp.dma_start(par[:, :], params).then_inc(s_in, 16)
            sp.dma_start(hpar[:, 0:2], heads).then_inc(s_in, 16)

            def load(name, c, i):
                g = START[name] + c
                nb = BLOCKS[name]
                if g >= 4 or not static(i):
                    sp.wait_ge(s_raw[g % 4], 16 * (g // 4) + 16 * i)
                    if not static(i):
                        sp.sem_inc(s_carry[0], 1)
                    sp.wait_ge(s_lo, g - 3 + 4 * i)
                    if not static(i):
                        sp.sem_inc(s_carry[0], 1)
                src = (w8 if nb == 8 else w11)[DRAM_AT[name] + c + 4 * i]
                sp.dma_start(raw[g % 4][:, 0:nb * P], src).then_inc(s_raw[g % 4], 16)

            for name, n, _, _ in PHASES:
                walk(sp, n, lambda c, i: load(name, c, i))
            sp.wait_ge(s_out, 16 * 8)

        @block.gpsimd
        def _(pool):
            chain = Chain(pool, s_pool)
            chain(pool.memset(ident[:, :], 0.0))
            chain(pool.memset(ones[:, :], 1.0))
            chain(pool.memset(epsc[:, :], EPS))
            chain(pool.memset(mbig[:, :], 0.0))
            chain(pool.memset(mcmp[:, :, :], 0.0))
            chain(pool.memset(rowok[:, :], 1.0))
            chain.wait()
            chain(pool.affine_select(out=ident[:, :], in_=ident[:, :], compare_op=ALU.not_equal, fill=1.0,
                                     base=0, pattern=[[-1, P]], channel_multiplier=1))
            chain(pool.affine_select(out=mbig[:, :], in_=mbig[:, :], compare_op=ALU.is_ge, fill=NEG,
                                     base=S - P, pattern=[[-1, S]], channel_multiplier=1))
            chain(pool.affine_select(out=mcmp[:, :, :], in_=mcmp[:, :, :], compare_op=ALU.is_ge, fill=NEG,
                                     base=-31, pattern=[[P, NT], [-16, NC]], channel_multiplier=1))
            chain(pool.affine_select(out=rowok[:, :], in_=rowok[:, :], compare_op=ALU.is_ge, fill=0.0,
                                     base=-31, pattern=[[0, 1]], channel_multiplier=1))
            chain.wait()
            pool.memset(small[:, 31:32], 0.0).then_inc(s_const, 1)

            squared, adds = [0], Chain(pool, s_pa)

            def add_squares(n):
                for j in range(1, n):
                    pool.wait_ge(s_sa, squared[0] + j + 1)
                    if j > 1:
                        adds.wait()
                    first = sqr[:, 0, :] if j == 1 else ssum[:, :]
                    adds(pool.tensor_tensor(ssum[:, :], first, sqr[:, j % 2, :], ALU.add))
                adds.wait()
                pool.memset(small[:, 31:32], 0.0).then_inc(s_sq, 1)
                squared[0] += n

            add_squares(KD)

            def ada_load(k, s):
                pool.dma_start(ada_w[:, k % 2, :], w_ada[s, k]).then_inc(s_ada_w[k % 2], 16)

            pool.wait_ge(s_csil, 1)
            before = chain.n
            per = 2 * KD - 1
            with pool.Fori(0, ADA_SLICES) as s:
                chain.off = s * per
                chain.wait()
                ada_load(0, s)
                ada_load(1, s)
                for k in range(KD):
                    pool.wait_ge(s_ada_w[k % 2], 16 * (k // 2 + 1) + 16 * (KD // 2) * s)
                    pool.sem_inc(s_carry[2], 1)
                    if k == 0:
                        done = chain(pool.tensor_scalar(ada_acc[:, :], ada_w[:, 0, :], csil[:, 0:1], 1.0,
                                                        ALU.mult, ALU.mult))
                    else:
                        chain(pool.tensor_scalar(ada_w[:, k % 2, :], ada_w[:, k % 2, :], csil[:, k:k + 1], 1.0,
                                                 ALU.mult, ALU.mult))
                        chain.wait()
                        ins = pool.tensor_tensor(ada_acc[:, :], ada_acc[:, :], ada_w[:, k % 2, :], ALU.add)
                        if k < KD - 1:
                            done = chain(ins)
                        else:
                            ins.then_inc(s_ada, 1)
                            pool.wait_ge(s_ada, s + 1)
                            pool.sem_inc(s_carry[2], 1)
                            chain(pool.memset(small[:, 31:32], 0.0))
                    if k + 2 < KD:
                        pool.wait_ge(s_pool, done)
                        ada_load(k + 2, s)
                pool.wait_ge(s_adap, s + 1)
            assert chain.n - before == per, (chain.n - before, per)
            chain.n = before + per * ADA_SLICES
            chain.off = 0

            add_squares(KD)
            add_squares(KD)

            pool.wait_ge(s_pe, START["SSD_IN"] + 41)
            chain(pool.memset(usum[:, :], 1.0))
            chain(pool.memset(smask[:, :], 0.0))
            chain.wait()
            chain(pool.affine_select(out=usum[:, :], in_=usum[:, :], compare_op=ALU.is_ge, fill=0.0,
                                     base=0, pattern=[[1, P]], channel_multiplier=-1))
            chain(pool.affine_select(out=smask[:, :], in_=smask[:, :], compare_op=ALU.is_ge, fill=NEG,
                                     base=0, pattern=[[1, P]], channel_multiplier=-1))
            chain.wait()
            pool.memset(small[:, 31:32], 0.0).then_inc(s_const, 1)

            for c in range(NT):
                tok = slice(c * P, (c + 1) * P)
                if c < NT - 1:
                    pool.wait_ge(s_xd, 4 * (c + 1))
                    pool.wait_ge(s_dec, c + 1)
                    if c > 0:
                        pool.wait_ge(s_st, 4 * c)
                    for k in range(4):
                        hs = slice(8 * k, 8 * k + 8)
                        pool.tensor_tensor(xdec[:, hs, :], xdt[:, hs, :],
                                           acs[:, 1, hs].unsqueeze(2).to_broadcast([P, 8, HD]),
                                           ALU.mult).then_inc(s_xdec, 1)
                if c > 0:
                    for u in range(8):
                        pool.wait_ge(s_xe, 8 * (c - 1) + u + 1)
                        pool.tensor_tensor(xbuf[:, u % 2, :].rearrange("p (a l) -> p a l", a=4),
                                           xbuf[:, u % 2, :].rearrange("p (a l) -> p a l", a=4),
                                           cv[:, 4 + u // 2, tok].unsqueeze(1).to_broadcast([P, 4, P]),
                                           ALU.mult).then_inc(s_cx, 1)
            for g in range(4):
                add_squares(4)
            add_squares(KD)
            add_squares(KD)
            add_squares(KD)

        @block.tensor
        def _(pe):
            def stats_a(q):
                pe.wait_ge(s_sq, q + 1)
                if q:
                    pe.wait_ge(s_ms, q)
                for t in range(NT):
                    mm = pe.matmul(stat_ps[:, t:t + 1], ssum[:, t * P:(t + 1) * P], ones[:, 0:1],
                                   start=True, stop=True)
                mm.then_inc(s_stat, 1)

            def stats_b(q):
                pe.wait_ge(s_diag, q + 1)
                if q:
                    pe.wait_ge(s_rb, q)
                pe.matmul(bc_ps[:, :], ones[:, :], tmp[:, 0, :], start=True, stop=True).then_inc(s_bc, 1)

            def gemm(name, hi, lo, taken, taken_at, q=None, panels=None, others=()):
                st, nb, per = START[name], BLOCKS[name], PER_TILE[name]
                n = panels or COUNT[name]
                nbank = 4 if per == 1 else 2
                for s_, v in others:
                    pe.wait_ge(s_, v)

                def weights(c, i):
                    pe.wait_ge(s_lo, st + c + 1 + 4 * i)

                def bank_free(c, i):
                    t = c // per
                    if not static(i) or t >= nbank:
                        pe.wait_ge(taken, taken_at + t - nbank + 1 + (4 // per) * i)

                def block_of(c, kb, bk):
                    w = (st + c) % 2
                    k = kb + nb * (c % per)
                    first, last = k == 0, k == nb * per - 1
                    cols = slice(kb * P, (kb + 1) * P)
                    pe.matmul(bk, whi[w][:, cols], hi[:, k, :], start=first, stop=False)
                    pe.matmul(bk, whi[w][:, cols], lo[:, k, :], start=False, stop=False)
                    return pe.matmul(bk, wlo[w][:, cols], hi[:, k, :], start=False, stop=last)

                def step(c, i):
                    bk = psum_ap((c // per) % nbank)
                    if c in (0, 1) and static(i) and per == 1:
                        if c == 0:
                            weights(1, 0)
                            for kb in range(nb):
                                pe.wait_ge(s_xt, XT[name] + kb + 1)
                                for cc_ in (0, 1):
                                    mm = block_of(cc_, kb, psum_ap(cc_))
                                    if kb == nb - 1:
                                        mm.then_inc(s_pe, 1)
                            if q is not None:
                                stats_a(q)
                        return
                    weights(c, i)
                    if c % per == 0:
                        bank_free(c, i)
                    for kb in range(nb):
                        if static(i) and c < per:
                            pe.wait_ge(s_xt, XT[name] + kb + nb * c + 1)
                        mm = block_of(c, kb, bk)
                    mm.then_inc(s_pe, 1)
                    if static(i) and c == 2 and q is not None:
                        stats_b(q)

                walk(pe, n, step)

            pe.wait_ge(s_const, 1)
            pe.wait_ge(s_in, 64)
            gemm("NSA_IN", xhi, xlo, s_ev, EV["NSA_IN"], Q_NSA_PRE, panels=17)
            pe.wait_ge(s_rb, 1)
            for c in range(17, 21):
                pe.wait_ge(s_lo, START["NSA_IN"] + c + 1)
                w = (START["NSA_IN"] + c) % 2
                for kk in range(2):
                    k = 2 * (c - 17) + kk
                    cols = slice(kk * S, (kk + 1) * S)
                    for t in range(NT):
                        tk = slice(t * P, (t + 1) * P)
                        bk = bank[4 + t][:, :]
                        pe.matmul(bk, xhi[:, k, tk], whi[w][:, cols], start=k == 0, stop=False)
                        pe.matmul(bk, xhi[:, k, tk], wlo[w][:, cols], start=False, stop=False)
                        mm = pe.matmul(bk, xlo[:, k, tk], whi[w][:, cols], start=False, stop=k == KD - 1)
                mm.then_inc(s_pe, 1)
            pe.wait_ge(s_gate, 1)
            pe.wait_ge(s_ev, 17)
            for t in range(NT):
                mm = pe.transpose(bank[1][:, t * 48:(t + 1) * 48], gt[:, t * P:(t + 1) * P], ident[0:48, 0:48])
            mm.then_inc(s_gtp, 1)
            for kv in range(2):
                pe.wait_ge(s_w1, 16 * (kv + 1))
                pe.wait_ge(s_flat, kv + 1)
                if kv:
                    pe.wait_ge(s_gelu, 1)
                for hh in range(2):
                    for m in range(16):
                        mm = pe.matmul(bank[0][:, hh * P:hh * P + 4 * NC], w1st[:, m, hh * P:(hh + 1) * P],
                                       flat[:, m, :, :].rearrange("p g c -> p (g c)"), start=m == 0, stop=m == 15)
                mm.then_inc(s_cm, 1)
                pe.wait_ge(s_gelu, kv + 1)
                w2 = par[:, COL["w2"] + kv * P:COL["w2"] + (kv + 1) * P].rearrange("p (a d) -> p a d", a=2)
                for g in range(4):
                    cs = slice(g * NC, (g + 1) * NC)
                    for hh in range(2):
                        if kv == 0:
                            o = bank[2][(g % 2) * HD:(g % 2 + 1) * HD, (g // 2) * NC:(g // 2 + 1) * NC]
                            mm = pe.matmul(o, w2[:, hh, :], hg[:, hh, cs], start=hh == 0, stop=hh == 1)
                        else:
                            o = bank[3][0:NC, g * HD:(g + 1) * HD]
                            mm = pe.matmul(o, hg[:, hh, cs], w2[:, hh, :], start=hh == 0, stop=hh == 1)
                mm.then_inc(s_cm, 1)

            pe.wait_ge(s_kv, 2)
            pe.wait_ge(s_v, 1)
            pe.wait_ge(s_gtp, 1)
            for j in range(2):
                with pe.Fori(4 * j, 4 * j + 4) as t:
                    def scores(u):
                        qt, a = u // 2, u % 2
                        rows = slice(a * HD, (a + 1) * HD)
                        n = (qt + 1) * P
                        q_ = qst[rows, qt * P:(qt + 1) * P]
                        if u:
                            pe.wait_ge(s_sc, u + 8 * t)
                        pe.matmul(bank[0][:, 0:n], q_, qkv[rows, 12 + j, 0:n], start=True, stop=True)
                        pe.matmul(bank[1][:, 0:n], q_, qkv[rows, 14 + j, 0:n], start=True, stop=True)
                        pe.matmul(bank[2][:, 0:NC], q_, kct[rows, j, :], start=True, stop=True).then_inc(s_S, 1)

                    def turn(u):
                        qt = u // 2
                        pe.wait_ge(s_P, 1 + u + 8 * t)
                        if u:
                            pe.wait_ge(s_tv, u + 8 * t)
                            pe.wait_ge(s_ta, u + 8 * t)
                        for r in range(2):
                            for kb in range(qt + 1):
                                ks = slice(kb * P, (kb + 1) * P)
                                pe.transpose(bank[3 + r][:, ks], pbuf[:, u % 2, r, ks], ident[:, :])
                        pe.transpose(bank[5][0:NC, 0:P], pcmp[:, u % 2, 0:NC], ident[:, :]).then_inc(s_T, 1)

                    def pv(u):
                        qt, a = u // 2, u % 2
                        o = bank[6][a * HD:(a + 1) * HD, qt * P:(qt + 1) * P]
                        pe.wait_ge(s_tv, 1 + u + 8 * t)
                        pe.wait_ge(s_ta, 1 + u + 8 * t)
                        if u == 0:
                            pe.wait_ge(s_xt, XT["NSA_OUT"] + t)
                        g = 2 * j + a
                        for r in range(2):
                            for kb in range(qt + 1):
                                pe.matmul(o, vtok[:, kb, r * 256 + g * HD:r * 256 + (g + 1) * HD],
                                          pt[:, u % 2, r, kb * P:(kb + 1) * P], start=r == 0 and kb == 0, stop=False,
                                          skip_group_check=True)
                        pe.matmul(o, vct[:, g, :], ptc[:, u % 2, :], start=False, stop=True,
                                  skip_group_check=True).then_inc(s_pv, 1)

                    pe.wait_ge(s_qst, 1 + t)
                    scores(0)
                    for u in range(8):
                        if u < 7:
                            scores(u + 1)
                        turn(u)
                        if u:
                            pv(u - 1)
                    pv(7)
                    pe.wait_ge(s_ada, 1 + t)
                    for f in range(ADA_SLICE // P):
                        mm = pe.matmul(bank[7][:, f:f + 1], ada_acc[:, f * P:(f + 1) * P], ones[:, 0:1],
                                       start=True, stop=True)
                    mm.then_inc(s_adap, 1)

            outs = [(s_ev, EV["UP1"]), (s_sc, 64), (s_tv, 64), (s_ta, 64)]
            gemm("NSA_OUT", xhi, xlo, s_m, MV["NSA_OUT"], others=outs)
            stats_a(Q_NSA_POST)
            stats_b(Q_NSA_POST)
            gemm("UP1", xhi, xlo, s_ev, EV["UP1"], Q_F1_PRE, others=[(s_m, 8)])
            gemm("DOWN1", hid_hi, hid_lo, s_m, MV["DOWN1"], others=[(s_ev, EV["SSD_IN"])])
            stats_a(Q_F1_POST)
            stats_b(Q_F1_POST)
            gemm("SSD_IN", xhi, xlo, s_ev, EV["SSD_IN"], Q_SSD_PRE, others=[(s_m, 16)])
            pe.wait_ge(s_dt, 8)
            pe.wait_ge(s_rb, Q_SSD_PRE + 1)
            for t in range(NT):
                for r in range(2):
                    mm = pe.transpose(bank[5][:, (2 * t + r) * SH:(2 * t + r + 1) * SH],
                                      dtt[:, r, t * P:(t + 1) * P], ident[0:SH, 0:SH])
            mm.then_inc(s_dtp, 1)
            pe.wait_ge(s_const, 2)
            pe.wait_ge(s_cv, 40)
            pe.wait_ge(s_ev, EV["UP2"])
            for c in range(NT):
                tok = slice(c * P, (c + 1) * P)
                if c:
                    pe.wait_ge(s_yk, 4 * c)
                    pe.wait_ge(s_w, 8 * c)
                    if c > 1:
                        pe.wait_ge(s_xe, 8 * (c - 1))
                for k in range(4):
                    for r in range(4):
                        mm = pe.transpose(bank[k][:, r * P:(r + 1) * P], cv[:, 8 + 4 * k + r, tok], ident[:, :])
                    mm.then_inc(s_xtp, 1)
                if c:
                    pe.wait_ge(s_bt, c)
                if c < NT - 1:
                    for g in range(4):
                        mm = pe.transpose(bank[4][:, g * P:(g + 1) * P], cv[:, g, tok], ident[:, :])
                    mm.then_inc(s_xtp, 1)
                pe.wait_ge(s_dtk, 1)
                dta = dtk[:, c, 1, :]
                pe.matmul(bank[5][:, 0:SH], usum[:, :], dta, start=True, stop=True)
                pe.matmul(bank[5][:, SH:2 * SH], ones[:, :], dta, start=True, stop=True).then_inc(s_ac, 1)
                pe.wait_ge(s_xd, 4 * (c + 1))
                for g in range(4):
                    G = 4 * c + g
                    if G:
                        pe.wait_ge(s_cbk, G)
                    pe.matmul(bank[6][:, 0:P], cv[:, g, tok], cv[:, 4 + g, tok], start=True, stop=True)\
                        .then_inc(s_cb, 1)
                    for v in range(2):
                        U = 2 * G + v
                        if U >= 2:
                            pe.wait_ge(s_ein, U - 1)
                        if c and U - 8 >= 2:
                            pe.wait_ge(s_xe, U - 8 - 1)
                        for k in range(4):
                            hd = 8 * g + 4 * v + k
                            mm = pe.matmul(bank[v][:, k * P:(k + 1) * P],
                                           dtk[:, c, 1, hd:hd + 1].to_broadcast([P, P]), usum[:, :],
                                           start=True, stop=True)
                        mm.then_inc(s_lb, 1)
                    yb = 2 + g % 2
                    if G >= 2:
                        pe.wait_ge(s_yk, G - 1)
                    for v in range(2):
                        U = 2 * G + v
                        pe.wait_ge(s_w, U + 1)
                        if c:
                            pe.wait_ge(s_cx, U - 8 + 1)
                            pe.wait_ge(s_stk, 4 * (c - 1) + g + 1)
                        for k in range(4):
                            hd = 8 * g + 4 * v + k
                            o = bank[yb][(hd % 2) * HD:(hd % 2 + 1) * HD, (hd // 2 % 4) * P:(hd // 2 % 4 + 1) * P]
                            mm = pe.matmul(o, xdt[:, hd, :], ebuf[:, v, k * P:(k + 1) * P],
                                           start=True, stop=c == 0, skip_group_check=True)
                            if c:
                                mm = pe.matmul(o, state[:, hd, :], xbuf[:, v, k * P:(k + 1) * P],
                                               start=False, stop=True, skip_group_check=True)
                        mm.then_inc(s_y, 1)
                    if c < NT - 1:
                        pe.wait_ge(s_xdec, 4 * c + g + 1)
                        if G:
                            pe.wait_ge(s_stk, G)
                        pe.wait_ge(s_bt, c + 1)
                        pe.matmul(bank[7][:, :], btok[:, g, :],
                                  xdec[:, 8 * g:8 * g + 8, :].rearrange("p h d -> p (h d)"),
                                  start=True, stop=True).then_inc(s_st, 1)
            pe.wait_ge(s_acv, NT)
            for g in range(4):
                stats_a(Q_GROUP + g)
                stats_b(Q_GROUP + g)
            gemm("SSD_OUT", yhi, ylo, s_m, MV["SSD_OUT"], others=[(s_yk, 16)])
            stats_a(Q_SSD_POST)
            stats_b(Q_SSD_POST)
            gemm("UP2", xhi, xlo, s_ev, EV["UP2"], Q_F2_PRE, others=[(s_m, 24)])
            gemm("DOWN2", hid_hi, hid_lo, s_m, MV["DOWN2"], others=[(s_ev, EV["CONV_IN"])])
            stats_a(Q_F2_POST)
            stats_b(Q_F2_POST)
            stats_a(Q_CONV_PRE)
            stats_b(Q_CONV_PRE)
            gemm("CONV_IN", xhi, xlo, s_ev, EV["CONV_IN"], others=[(s_m, 32)])
            gemm("CONV_OUT", yc_hi, yc_lo, s_m, MV["CONV_OUT"], others=[(s_ev, EV["UP3"])])
            stats_a(Q_CONV_POST)
            stats_b(Q_CONV_POST)
            stats_a(Q_F3_PRE)
            stats_b(Q_F3_PRE)
            gemm("UP3", xhi, xlo, s_ev, EV["UP3"], others=[(s_m, 40)])
            gemm("DOWN3", hid_hi, hid_lo, s_m, MV["DOWN3"], others=[(s_ev, EV["UP3"] + 44)])
            stats_a(Q_F3_POST)
            stats_b(Q_F3_POST)

        @block.scalar
        def _(act):
            chain = Chain(act, s_act)

            def weight_hi(g, i):
                if g >= TOTAL:
                    return
                n = PANEL_BLOCKS[g] * P
                act.wait_ge(s_raw[g % 4], 16 * (g // 4 + 1) + 16 * i)
                if g >= 2:
                    act.wait_ge(s_pe, g - 1 + 4 * i)
                act.activation(whi[g % 2][:, 0:n], raw[g % 4][:, 0:n], ACT.Copy).then_inc(s_hi, 1)

            def stats_root(q):
                act.wait_ge(s_ms, q + 1)
                act.activation(root, ms, ACT.Sqrt).then_inc(s_sqrt, 1)

            def stats_keep(q):
                act.wait_ge(s_bc, q + 1)
                act.activation(rstd_b[:, :], bc_ps[:, :], ACT.Copy).then_inc(s_rb, 1)

            added = [0]

            def square(src, j, n):
                need = added[0] + (max(1, j - 2) if j >= 2 else 0)
                if need:
                    act.wait_ge(s_pa, need)
                act.activation(sqr[:, j % 2, :], src, ACT.Square).then_inc(s_sa, 1)
                if j == n - 1:
                    added[0] += n - 1

            def project_in(name, post, q=None, panels=None):
                st = START[name]

                def step(c, i):
                    weight_hi(st + c + 2, i)
                    if q is not None and static(i) and c == 0:
                        stats_root(q)
                        return
                    if q is not None and static(i) and c == 1:
                        stats_keep(q)
                        post(0, 0)
                    post(c, i)
                walk(act, COUNT[name], step)

            def project_out(name, m):
                st, per = START[name], PER_TILE[name]

                def step(c, i):
                    weight_hi(st + c + 2, i)
                    if c % per == per - 1:
                        t = c // per
                        act.wait_ge(s_pe, st + c + 1 + 4 * i)
                        act.activation(m[:, t + (4 // per) * i, :], psum_ap(t % (4 if per == 1 else 2)), ACT.Copy)\
                            .then_inc(s_m, 1)
                walk(act, COUNT[name], step)

            def operands(name, gain, updated):
                for j in range(KD):
                    if updated is not None:
                        act.wait_ge(s_h, updated + j + 1)
                    act.activation(xhi[:, j, :], h[:, j, :], ACT.Copy, scale=gain(j)).then_inc(s_xh, 1)
                    square(h[:, j, :], j, KD)

            def ffn_post(gates_before, hidden_before):
                def post(c, i):
                    t = c // 2 + 2 * i
                    if c % 2 == 0:
                        act.wait_ge(s_cg, gates_before + t + 1)
                        act.activation(sg[:, :], tmp[:, 0, :], ACT.Silu).then_inc(s_sg, 1)
                    else:
                        act.wait_ge(s_hid, hidden_before + t + 1)
                        act.activation(hid_hi[:, c // 2 + 2 * i, :], hid[:, :], ACT.Copy).then_inc(s_xh, 1)
                return post

            act.wait_ge(s_in, 64)
            act.wait_ge(s_const, 1)
            weight_hi(0, 0)
            weight_hi(1, 0)
            operands("NSA_IN", lambda j: col("gains", j), None)
            chain(act.activation(csil[:, :], par[:, COL["c"]:COL["c"] + KD], ACT.Silu))
            chain.wait()
            act.activation(csil[:, 0:1], csil[:, 0:1], ACT.Copy).then_inc(s_csil, 1)

            def nsa_post(c, i):
                if static(i) and c == 16:
                    act.wait_ge(s_ev, 12)
                    act.dma_start(swp[0:HD, :, :], qkv[HD:P, 8:12, :]).then_inc(s_swp, 16)
                    act.dma_start(swp[HD:P, :, :], qkv[0:HD, 8:12, :]).then_inc(s_swp, 16)
                    act.dma_start(w1st[:, :, :], w_cmp[0]).then_inc(s_w1, 16)
                if static(i) and c == 16:
                    act.wait_ge(s_ev, 17)
                    chain(act.activation(gt[:, :], gt[:, :], ACT.Sigmoid))
                    chain.wait()
                    act.activation(gt[0:1, 0:1], gt[0:1, 0:1], ACT.Copy).then_inc(s_gate, 1)

            project_in("NSA_IN", nsa_post, Q_NSA_PRE)
            for kv in range(2):
                act.wait_ge(s_cm, 2 * kv + 1)
                if kv == 0:
                    act.dma_start(w1st[:, :, :], w_cmp[1]).then_inc(s_w1, 16)
                else:
                    act.wait_ge(s_cm, 2)
                act.activation(hg[:, :, :], bank[0][:, 0:2 * P].rearrange("p (a c) -> p a c", a=2)[:, :, 0:4 * NC],
                               ACT.Gelu_apprx_tanh).then_inc(s_gelu, 1)
            act.wait_ge(s_cm, 4)
            for j in range(2):
                with act.Fori(4 * j, 4 * j + 4) as t:
                    def exps(u):
                        qt = u // 2
                        n = (qt + 1) * P
                        b = u % 2
                        act.wait_ge(s_nb, 1 + u + 8 * t)
                        for r in range(2):
                            act.activation(pbuf[:, b, r, 0:n], pbuf[:, b, r, 0:n], ACT.Exp, scale=QSCALE,
                                           bias=stat[:, b, 4 + r:5 + r], accum_out=stat[:, b, 8 + r:9 + r])\
                                .then_inc(s_e, 1)
                        act.activation(pcmp[:, b, 0:NC], pcmp[:, b, 0:NC], ACT.Exp, scale=QSCALE,
                                       bias=stat[:, b, 6:7], accum_out=stat[:, b, 10:11]).then_inc(s_e, 1)

                    def keep(u):
                        n = (u // 2 + 1) * P
                        act.wait_ge(s_T, 1 + u + 8 * t)
                        if u >= 2:
                            act.wait_ge(s_pv, u - 1 + 8 * t)
                        act.activation(ptc[:, u % 2, :], bank[5][0:NC, 0:P], ACT.Copy)
                        act.activation(pt[:, u % 2, 1, 0:n], bank[4][:, 0:n], ACT.Copy).then_inc(s_ta, 1)

                    exps(0)
                    for u in range(8):
                        if u < 7:
                            exps(u + 1)
                        keep(u)
                    act.wait_ge(s_pv, 8 + 8 * t)
                    act.activation(xhi[:, t, :], bank[6][:, :], ACT.Copy).then_inc(s_xh, 1)
            project_out("NSA_OUT", m_alt)
            stats_root(Q_NSA_POST)
            stats_keep(Q_NSA_POST)
            operands("UP1", lambda j: col("gains", 16 + j), 0)
            project_in("UP1", ffn_post(0, 0), Q_F1_PRE)
            project_out("DOWN1", m_x)
            stats_root(Q_F1_POST)
            stats_keep(Q_F1_POST)
            operands("SSD_IN", lambda j: col("gains", 32 + j), 8)

            def ssd_post(c, i):
                if c < 40:
                    act.wait_ge(s_cacc, c + 1 + 4 * i)
                    act.activation(ssd_dst(c, i), cacc[:, c % 2, :], ACT.Silu).then_inc(s_cv, 1)

            st = START["SSD_IN"]
            zone = {"z": False}

            def ssd_dst(c, i):
                return zb[:, c - 24 + 4 * i, :] if zone["z"] else cv[:, c + 4 * i, :]

            def ssd_step(c, i):
                weight_hi(st + c + 2, i)
                if static(i) and c == 0:
                    stats_root(Q_SSD_PRE)
                    return
                if static(i) and c == 1:
                    stats_keep(Q_SSD_PRE)
                    ssd_post(0, 0)
                ssd_post(c, i)

            ssd_walk(act, ssd_step, zone)
            act.wait_ge(s_dt, 1)
            act.activation(dw[:, 1, :], dw[:, 0, :], ACT.Abs).then_inc(s_dta, 1)
            act.wait_ge(s_dta, 1)
            act.activation(dw[:, 1, :], dw[:, 1, :], ACT.Exp, scale=-1.0).then_inc(s_dta, 1)
            act.activation(hpar[:, 2:3], hpar[:, 1:2], ACT.Exp).then_inc(s_dta, 1)
            act.wait_ge(s_dt, 2)
            act.activation(dw[:, 3, :], dw[:, 2, :], ACT.Ln).then_inc(s_dta, 1)
            for c in range(NT):
                if c < NT - 1:
                    act.wait_ge(s_xtp, 5 * (c + 1))
                    if c:
                        act.wait_ge(s_st, 4 * c)
                    act.activation(btok[:, :, :].rearrange("p g n -> p (g n)"), bank[4][:, :], ACT.Copy)\
                        .then_inc(s_bt, 1)
                act.wait_ge(s_acv, c + 1)
                if c:
                    act.wait_ge(s_stk, 4 * c)
                act.activation(acs[:, 1:3, :], acs[:, 1:3, :], ACT.Exp).then_inc(s_dec, 1)
                for g in range(4):
                    G = 4 * c + g
                    act.wait_ge(s_cb, G + 1)
                    if G:
                        act.wait_ge(s_w, 2 * G)
                    act.activation(cbuf[:, :], bank[6][:, 0:P], ACT.Copy).then_inc(s_cbk, 1)
                    for v in range(2):
                        U = 2 * G + v
                        if c:
                            act.wait_ge(s_ein, U + 1)
                            if U - 8 >= 2:
                                act.wait_ge(s_y, U - 1)
                            act.activation(xbuf[:, v, :], bank[v][:, :], ACT.Exp).then_inc(s_xe, 1)
                        act.wait_ge(s_ein, U + 1)
                        act.activation(ebuf[:, v, :], ebuf[:, v, :], ACT.Exp).then_inc(s_ee, 1)
            def group_squares(g):
                act.wait_ge(s_yk, 12 + g + 1)
                for j in range(4):
                    square(zb[:, 4 * g + j, :], j, 4)

            group_squares(0)
            for g in range(4):
                stats_root(Q_GROUP + g)
                stats_keep(Q_GROUP + g)
                if g < 3:
                    group_squares(g + 1)
                for j in range(4 * g, 4 * g + 4):
                    act.wait_ge(s_hid, KF + j + 1)
                    act.activation(yhi[:, j, :], zb[:, j, :], ACT.Copy).then_inc(s_xh, 1)
            project_out("SSD_OUT", m_x)
            stats_root(Q_SSD_POST)
            stats_keep(Q_SSD_POST)
            operands("UP2", lambda j: col("gains", 48 + j), 16)
            project_in("UP2", ffn_post(KF, KF + NZ), Q_F2_PRE)
            project_out("DOWN2", m_x)
            stats_root(Q_F2_POST)
            stats_keep(Q_F2_POST)

            def modulated(updated, shift, made):
                for j in range(KD):
                    act.wait_ge(s_h, updated + j + 1)
                    square(h[:, j, :], j, KD)
                q = Q_CONV_PRE if shift == 0 else Q_F3_PRE
                stats_root(q)
                stats_keep(q)
                for j in range(KD):
                    act.wait_ge(s_hid, made + j + 1)
                    act.activation(xhi[:, j, :], tmp[:, j % 2, :], ACT.Identity,
                                   bias=mod[:, shift * KD + j:shift * KD + j + 1]).then_inc(s_xh, 1)

            modulated(24, 0, 2 * KF + NZ)

            def conv_post(c, i):
                if c >= 16:
                    act.wait_ge(s_hid, 2 * KF + NZ + KD + c - 16 + 1)
                    act.activation(yc_hi[:, c - 16, :], cyt[:, c % 2, :], ACT.Copy).then_inc(s_xh, 1)

            st = START["CONV_IN"]
            for c in range(24):
                weight_hi(st + c + 2, 0)
                conv_post(c, 0)
            project_out("CONV_OUT", m_conv)
            stats_root(Q_CONV_POST)
            stats_keep(Q_CONV_POST)
            modulated(32, 3, 2 * KF + NZ + 2 * KD)
            base_t = 2 * KF + NZ + 3 * KD

            def up3_post(c, i):
                if c % 2 == 0:
                    act.wait_ge(s_pe, START["UP3"] + c + 1 + 4 * i)
                    if not static(i) or c >= 2:
                        act.wait_ge(s_hid, base_t + c // 2 + 2 * i)
                    act.activation(sg[:, :], psum_ap(c % 4), ACT.Silu).then_inc(s_sg, 1)
                else:
                    act.wait_ge(s_hid, base_t + c // 2 + 1 + 2 * i)
                    act.activation(hid_hi[:, c // 2 + 2 * i, :], hid[:, :], ACT.Copy).then_inc(s_xh, 1)
            project_in("UP3", up3_post)
            project_out("DOWN3", m_x)
            stats_root(Q_F3_POST)
            stats_keep(Q_F3_POST)
            for j in range(KD):
                act.wait_ge(s_h, 40 + j + 1)
                act.dma_start(out[:, j, :], h[:, j, :]).then_inc(s_out, 16)
            act.wait_ge(s_out, 16 * 8)

        @block.vector
        def _(dve):
            chain = Chain(dve, s_dve)

            def weight_lo(g, i):
                if g >= TOTAL:
                    return
                n = PANEL_BLOCKS[g] * P
                dve.wait_ge(s_hi, g + 1 + 4 * i)
                dve.tensor_tensor(wlo[g % 2][:, 0:n], raw[g % 4][:, 0:n], whi[g % 2][:, 0:n].bitcast(F32),
                                  ALU.subtract).then_inc(s_lo, 1)

            def stats(q, width):
                dve.wait_ge(s_stat, q + 1)
                dve.tensor_scalar(ms, stat_ps[:, 0:4], 1.0 / width, EPS, ALU.mult, ALU.add).then_inc(s_ms, 1)
                dve.wait_ge(s_sqrt, q + 1)
                chain(dve.reciprocal(rt, root))
                chain.wait()
                dve.tensor_tensor(tmp[:, 0, :].rearrange("p (a b) -> p a b", a=NT),
                                  ident[:, :].unsqueeze(1).to_broadcast([P, NT, P]),
                                  rt.unsqueeze(2).to_broadcast([P, NT, P]), ALU.mult).then_inc(s_diag, 1)

            def operand_lo(name, j, gain):
                dve.wait_ge(s_xh, XT[name] + j + 1)
                dve.scalar_tensor_tensor(out=xlo[:, j, :], in0=h[:, j, :], scalar=gain(j),
                                         in1=xhi[:, j, :].bitcast(F32), op0=ALU.mult, op1=ALU.subtract)\
                    .then_inc(s_xt, 1)

            def update(q, m, post_gain, name=None, pre_gain=None):
                dve.wait_ge(s_rb, q + 1)
                for j in range(KD):
                    chain(dve.scalar_tensor_tensor(out=tmp[:, j % 2, :], in0=m[:, j, :], scalar=post_gain(j),
                                                   in1=rstd_b[:, :], op0=ALU.mult, op1=ALU.mult))
                    v = chain.n
                    if name and j:
                        operand_lo(name, j - 1, pre_gain)
                    chain.wait(v)
                    dve.tensor_tensor(h[:, j, :], tmp[:, j % 2, :], h[:, j, :], ALU.add).then_inc(s_h, 1)
                if name:
                    operand_lo(name, KD - 1, pre_gain)

            def project_out(name, m):
                st, per = START[name], PER_TILE[name]
                mv = MV[name]

                def step(c, i):
                    weight_lo(st + c + 2, i)
                    if c % per == per - 1:
                        t, ti = c // per, (4 // per) * i
                        dve.wait_ge(s_m, mv + t + 1 + ti)
                        mt = m[:, t + ti, :]
                        if t == 0 and static(i):
                            chain(dve.tensor_tensor(ssum[:, :], mt, mt, ALU.mult))
                            return
                        chain.wait()
                        chain(dve.tensor_tensor(tmp[:, 0, :], mt, mt, ALU.mult))
                        chain.wait()
                        ins = dve.tensor_tensor(ssum[:, :], ssum[:, :], tmp[:, 0, :], ALU.add)
                        if static(i) and t == KD - 1:
                            ins.then_inc(s_sq, 1)
                        else:
                            chain(ins)
                walk(dve, COUNT[name], step, chain, per=8 // per)

            def ffn_up(name, layer, xt_at, tile_at, q):
                st, ev = START[name], EV[name]

                def lo_of(c, i):
                    dve.wait_ge(s_xh, xt_at + c // 2 + 1 + 2 * i)
                    dve.tensor_tensor(hid_lo[:, c // 2 + 2 * i, :], hid[:, :],
                                      hid_hi[:, c // 2 + 2 * i, :].bitcast(F32), ALU.subtract).then_inc(s_xt, 1)

                def step(c, i):
                    weight_lo(st + c + 2, i)
                    if static(i) and c == 0:
                        stats(q, D)
                    if static(i) and c == 0:
                        return
                    if static(i) and c == 1:
                        dve.wait_ge(s_rb, q + 1)
                        take(0, 0)
                    take(c, i)

                def take(c, i):
                    v = c % 2
                    dve.wait_ge(s_pe, st + c + 1 + 4 * i)
                    dve.tensor_tensor(upad[:, v, 2:2 + S], psum_ap(c % 4), rstd_b[:, :], ALU.mult).then_inc(s_ev, 1)
                    k = layer * 44 + c + 4 * i
                    w = par[:, COL["ffn_w"]:COL["ffn_w"] + 264]

                    def wc(tap):
                        return par[:, bass.ds(COL["ffn_w"] + 3 * k + tap, 1)]
                    dve.wait_ge(s_ev, ev + c + 1 + 4 * i)
                    chain(dve.tensor_scalar(tmp[:, v, :], upad[:, v, 2:2 + S], wc(2),
                                            par[:, bass.ds(COL["ffn_b"] + k, 1)], ALU.mult, ALU.add))
                    chain.wait()
                    chain(dve.scalar_tensor_tensor(out=tmp[:, v, :], in0=upad[:, v, 1:1 + S], scalar=wc(1),
                                                   in1=tmp[:, v, :], op0=ALU.mult, op1=ALU.add))
                    chain.wait()
                    ins = dve.scalar_tensor_tensor(out=tmp[:, v, :], in0=upad[:, v, 0:S], scalar=wc(0),
                                                   in1=tmp[:, v, :], op0=ALU.mult, op1=ALU.add)
                    if v == 0:
                        ins.then_inc(s_cg, 1)
                        if static(i) and c == 0:
                            return
                        lo_of(c - 2, i)
                    else:
                        chain(ins)
                        dve.wait_ge(s_sg, sg_at[0] + c // 2 + 1 + 2 * i)
                        chain.wait()
                        dve.tensor_tensor(hid[:, :], sg[:, :], tmp[:, 1, :], ALU.mult).then_inc(s_hid, 1)

                sg_at = [2 * 0 + (0 if layer == 0 else KF)]
                walk(dve, 44, step, chain, per=2 * (2 + 3))
                lo_of(42, 0)

            dve.wait_ge(s_in, 64)
            dve.wait_ge(s_const, 1)
            weight_lo(0, 0)
            weight_lo(1, 0)
            for j in range(KD):
                operand_lo("NSA_IN", j, lambda k: col("gains", k))

            def nsa_take(c, i):
                dve.wait_ge(s_pe, c + 1 + 4 * i)
                if static(i) and c == 16:
                    dve.tensor_tensor(gt[:, :], bank[0][0:48, :], rstd_b[0:48, :], ALU.mult).then_inc(s_ev, 1)
                else:
                    dve.tensor_tensor(qkv[:, c + 4 * i, :], psum_ap(c % 4), rstd_b[:, :], ALU.mult)\
                        .then_inc(s_ev, 1)

            def nsa_step(c, i):
                weight_lo(START["NSA_IN"] + c + 2, i)
                if static(i) and c == 0:
                    stats(Q_NSA_PRE, D)
                    return
                if static(i) and c == 1:
                    dve.wait_ge(s_rb, 1)
                    nsa_take(0, 0)
                if static(i) and c > 16:
                    return
                nsa_take(c, i)
            walk(dve, 21, nsa_step, chain, 0)
            dve.wait_ge(s_pe, 21)
            for t in range(NT):
                ins = dve.tensor_scalar(vtok[:, t, :], bank[4 + t][:, :], rt[:, t:t + 1], None, ALU.mult)
            ins.then_inc(s_v, 1)
            dve.wait_ge(s_swp, 32)
            dve.wait_ge(s_ev, 12)
            for kv in range(2):
                if kv:
                    dve.wait_ge(s_cm, 1)
                for a in range(2):
                    rows = slice(a * HD, (a + 1) * HD)
                    for b in range(2):
                        src = qkv[rows, 8 + 2 * kv:10 + 2 * kv, :] if a == b else swp[rows, 2 * kv:2 * kv + 2, :]
                        src = src.rearrange("p j (c r) -> p r j c", r=16)[:, a:16:2]
                        for mh in range(2):
                            pos = par[rows, COL["pos"] + 16 * kv + 8 * mh:COL["pos"] + 16 * kv + 8 * mh + 8]
                            for jt in range(2):
                                ins = dve.tensor_tensor(
                                    flat[rows, 8 * mh:8 * mh + 8, b + 2 * jt, :], src[:, :, jt, mh:mh + NC],
                                    pos.unsqueeze(2).to_broadcast([HD, 8, NC]), ALU.add)
                ins.then_inc(s_flat, 1)
            dve.wait_ge(s_gtp, 1)
            chain(dve.tensor_copy(gtok[:, :, :].rearrange("p t n -> p (t n)"), bank[1][:, 0:NT * 48]))
            dve.wait_ge(s_cm, 2)
            dve.tensor_copy(kct[:, :, :].rearrange("p j c -> p (j c)"), bank[2][:, 0:2 * NC]).then_inc(s_kv, 1)
            dve.wait_ge(s_cm, 4)
            dve.tensor_copy(vct[:, :, :].rearrange("p g d -> p (g d)"), bank[3][0:NC, 0:4 * HD]).then_inc(s_kv, 1)

            chain.wait()
            for j in range(2):
                before, per = chain.n, 8 * 3 + 2
                with dve.Fori(4 * j, 4 * j + 4) as t:
                    chain.off = (t - 4 * j) * per

                    def masked(u):
                        qt, b = u // 2, u % 2
                        n = (qt + 1) * P
                        dve.wait_ge(s_S, 1 + u + 8 * t)
                        if u >= 2:
                            dve.wait_ge(s_T, u - 1 + 8 * t)
                        dve.sem_inc(s_carry[1], 1)
                        for r in range(2):
                            dve.tensor_tensor_reduce(pbuf[:, b, r, 0:n], bank[r][:, 0:n], mbig[:, S - n:S], 1.0,
                                                     -3e38, ALU.add, ALU.max, stat[:, b, r:r + 1])
                        dve.tensor_tensor_reduce(pcmp[:, b, 0:NC], bank[2][:, 0:NC], mcmp[:, qt, :], 1.0,
                                                 -3e38, ALU.add, ALU.max, stat[:, b, 2:3]).then_inc(s_sc, 1)
                        dve.wait_ge(s_sc, 1 + u + 8 * t)
                        dve.tensor_scalar(stat[:, b, 4:7], stat[:, b, 0:3], -QSCALE, None, ALU.mult)\
                            .then_inc(s_nb, 1)

                    def scaled(u):
                        qt, b = u // 2, u % 2
                        n = (qt + 1) * P
                        dve.wait_ge(s_e, 3 + 3 * u + 24 * t)
                        chain(dve.reciprocal(stat[:, b, 12:15], stat[:, b, 8:11]))
                        hd = (8 * j + 4 * b) - 4 * j
                        gsel = gtok[:, qt, bass.ds(3 * hd + 3 * t + 1, 2)]
                        gcmp = gtok[:, qt, bass.ds(3 * hd + 3 * t, 1)]
                        chain.wait()
                        dve.tensor_tensor(stat[:, b, 16:18], stat[:, b, 12:14], gsel, ALU.mult)
                        if qt == 0:
                            chain(dve.scalar_tensor_tensor(out=stat[:, b, 18:19], in0=stat[:, b, 14:15],
                                                           scalar=rowok[:, 0:1], in1=gcmp,
                                                           op0=ALU.mult, op1=ALU.mult))
                        else:
                            chain(dve.tensor_tensor(stat[:, b, 18:19], stat[:, b, 14:15], gcmp, ALU.mult))
                        chain.wait()
                        chain(dve.tensor_scalar(pcmp[:, b, 0:NC], pcmp[:, b, 0:NC], stat[:, b, 18:19], None,
                                                ALU.mult))
                        dve.tensor_scalar(pbuf[:, b, 0, 0:n], pbuf[:, b, 0, 0:n], stat[:, b, 16:17], None, ALU.mult)
                        dve.tensor_scalar(pbuf[:, b, 1, 0:n], pbuf[:, b, 1, 0:n], stat[:, b, 17:18], None,
                                          ALU.mult).then_inc(s_P, 1)

                    def keep(u):
                        n = (u // 2 + 1) * P
                        dve.wait_ge(s_T, 1 + u + 8 * t)
                        if u >= 2:
                            dve.wait_ge(s_pv, u - 1 + 8 * t)
                        dve.tensor_copy(pt[:, u % 2, 0, 0:n], bank[3][:, 0:n]).then_inc(s_tv, 1)

                    dve.tensor_copy(qst[:, :], qkv[:, t, :]).then_inc(s_qst, 1)
                    masked(0)
                    for u in range(8):
                        if u < 7:
                            masked(u + 1)
                        if u:
                            keep(u - 1)
                        scaled(u)
                    keep(7)
                    dve.wait_ge(s_xh, XT["NSA_OUT"] + 1 + t)
                    chain(dve.tensor_tensor(xlo[:, t, :], bank[6][:, :], xhi[:, t, :].bitcast(F32), ALU.subtract))
                    dve.wait_ge(s_adap, 1 + t)
                    chain(dve.tensor_copy(mod[:, bass.ds(6 * t, 6)], bank[7][:, 0:6]))
                    chain.wait()
                    dve.tensor_copy(stat[:, 0, 31:32], stat[:, 0, 16:17]).then_inc(s_xt, 1)
                assert chain.n - before == per, (chain.n - before, per)
                chain.n, chain.off = before + 4 * per, 0
            chain(dve.tensor_tensor(mod[:, :], mod[:, :], par[:, COL["ada_b"]:COL["ada_b"] + 48], ALU.add))
            chain.wait()
            g2 = par[:, COL["gains2"]:COL["gains2"] + 32].rearrange("p (a k) -> p a k", a=4)
            md = mod[:, :].rearrange("p (a k) -> p a k", a=6)
            for f in range(2):
                chain(dve.tensor_scalar(gmod[:, 2 * f, :], md[:, 3 * f + 1, :], 1.0, None, ALU.add))
                chain.wait()
                chain(dve.tensor_tensor(gmod[:, 2 * f, :], gmod[:, 2 * f, :], g2[:, 2 * f, :], ALU.mult))
                chain(dve.tensor_tensor(gmod[:, 2 * f + 1, :], md[:, 3 * f + 2, :], g2[:, 2 * f + 1, :], ALU.mult))
                chain.wait()

            project_out("NSA_OUT", m_alt)
            stats(Q_NSA_POST, D)
            update(Q_NSA_POST, m_alt, lambda j: col("gains", 8 + j), "UP1", lambda j: col("gains", 16 + j))
            chain(dve.memset(upad[:, :, 0:2], 0.0))
            chain.wait()
            ffn_up("UP1", 0, XT["DOWN1"], 0, Q_F1_PRE)
            project_out("DOWN1", m_x)
            stats(Q_F1_POST, D)
            update(Q_F1_POST, m_x, lambda j: col("gains", 24 + j), "SSD_IN", lambda j: col("gains", 32 + j))
            st, ev = START["SSD_IN"], EV["SSD_IN"]
            chain(dve.memset(spad[:, 0:3], 0.0))
            chain.wait()
            zone = {"z": False}

            def ssd_take(c, i):
                dve.wait_ge(s_pe, st + c + 1 + 4 * i)
                if c == 40:
                    dve.tensor_tensor(dw[:, 0, :], bank[0][0:SH, :], rstd_b[0:SH, :], ALU.mult).then_inc(s_ev, 1)
                    return
                if not static(i) or c >= 2:
                    dve.wait_ge(s_cv, c - 1 + 4 * i)
                if zone["z"]:
                    ins = dve.tensor_tensor(cacc[:, c % 2, :], psum_ap(c % 4), rstd_b[:, :], ALU.mult)
                    chain(ins)
                    chain.wait()
                    dve.tensor_copy(small[:, 30:31], rt[:, 0:1]).then_inc(s_ev, 1)
                    dve.tensor_copy(small[:, 29:30], rt[:, 0:1]).then_inc(s_cacc, 1)
                    return
                dve.wait_ge(s_cacc, c + 4 * i)
                dve.tensor_tensor(spad[:, 3:3 + S], psum_ap(c % 4), rstd_b[:, :], ALU.mult).then_inc(s_ev, 1)
                dve.wait_ge(s_ev, ev + c + 1 + 4 * i)
                k = c + 4 * i
                for tap in (3, 2, 1, 0):
                    w = par[:, bass.ds(COL["ssd_w"] + 4 * k + tap, 1)]
                    if tap == 3:
                        ins = dve.tensor_scalar(cacc[:, c % 2, :], spad[:, 3:3 + S], w,
                                                par[:, bass.ds(COL["ssd_b"] + k, 1)], ALU.mult, ALU.add)
                    else:
                        ins = dve.scalar_tensor_tensor(out=cacc[:, c % 2, :], in0=spad[:, tap:tap + S], scalar=w,
                                                       in1=cacc[:, c % 2, :], op0=ALU.mult, op1=ALU.add)
                    if tap:
                        chain(ins)
                        chain.wait()
                    else:
                        ins.then_inc(s_cacc, 1)

            def ssd_step(c, i):
                weight_lo(st + c + 2, i)
                if static(i) and c == 0:
                    stats(Q_SSD_PRE, D)
                    return
                if static(i) and c == 1:
                    dve.wait_ge(s_rb, Q_SSD_PRE + 1)
                    ssd_take(0, 0)
                ssd_take(c, i)

            ssd_walk(dve, ssd_step, zone, chain, 12, 4)
            dve.wait_ge(s_ev, EV["UP2"])
            chain(dve.tensor_scalar(dw[:, 4, :], dw[:, 0, :], hpar[:, 0:1], None, ALU.add))
            chain.wait()
            dve.tensor_copy(dw[:, 0, :], dw[:, 4, :]).then_inc(s_dt, 1)
            dve.wait_ge(s_dta, 3)
            dve.tensor_scalar(dw[:, 2, :], dw[:, 1, :], 1.0, None, ALU.add).then_inc(s_dt, 1)
            dve.wait_ge(s_dt, 2)
            chain(dve.tensor_scalar(dw[:, 4, :], dw[:, 2, :], 1.0, 1e-30, ALU.subtract, ALU.max))
            chain.wait()
            chain(dve.reciprocal(dw[:, 4, :], dw[:, 4, :]))
            chain.wait()
            dve.tensor_tensor(dw[:, 4, :], dw[:, 4, :], dw[:, 1, :], ALU.mult).then_inc(s_dt, 1)
            dve.wait_ge(s_dt, 3)
            dve.wait_ge(s_dta, 4)
            chain(dve.tensor_tensor(dw[:, 3, :], dw[:, 3, :], dw[:, 4, :], ALU.mult))
            chain(dve.tensor_scalar(dw[:, 2, :], dw[:, 2, :], 1.0, None, ALU.is_equal))
            chain.wait()
            dve.tensor_tensor(dw[:, 2, :], dw[:, 2, :], dw[:, 1, :], ALU.mult).then_inc(s_dt, 1)
            dve.wait_ge(s_dt, 4)
            dve.tensor_tensor(dw[:, 3, :], dw[:, 3, :], dw[:, 2, :], ALU.add).then_inc(s_dt, 1)
            dve.wait_ge(s_dt, 5)
            dve.scalar_tensor_tensor(out=dtt[:, 0, :], in0=dw[:, 0, :], scalar=0.0, in1=dw[:, 3, :],
                                     op0=ALU.max, op1=ALU.add).then_inc(s_dt, 1)
            dve.tensor_scalar(hpar[:, 3:4], hpar[:, 2:3], -1.0, None, ALU.mult).then_inc(s_dt, 1)
            dve.wait_ge(s_dt, 7)
            dve.tensor_scalar(dtt[:, 1, :], dtt[:, 0, :], hpar[:, 3:4], None, ALU.mult).then_inc(s_dt, 1)
            dve.wait_ge(s_dtp, 1)
            dve.tensor_copy(dtk[:, :, :, :].rearrange("p t r h -> p (t r h)"), bank[5][:, 0:NT * 2 * SH])\
                .then_inc(s_dtk, 1)
            dve.wait_ge(s_dtk, 1)
            dve.wait_ge(s_cv, 40)
            dve.wait_ge(s_const, 2)
            for c in range(NT):
                tok = slice(c * P, (c + 1) * P)
                if c:
                    dve.wait_ge(s_xdec, 4 * c)
                for k in range(4):
                    dve.wait_ge(s_xtp, (5 * c if c < NT else 0) + k + 1)
                    if c:
                        dve.wait_ge(s_y, 8 * c)
                    dve.tensor_tensor(xdt[:, 8 * k:8 * k + 8, :], bank[k][:, :].rearrange("p (h d) -> p h d", h=8),
                                      dtk[:, c, 0, 8 * k:8 * k + 8].unsqueeze(2).to_broadcast([P, 8, HD]),
                                      ALU.mult).then_inc(s_xd, 1)
                dve.wait_ge(s_ac, c + 1)
                if c:
                    dve.wait_ge(s_xdec, 4 * c)
                chain(dve.tensor_copy(acs[:, 0, :], bank[5][:, 0:SH]))
                chain(dve.tensor_copy(acs[:, 2, :], bank[5][:, SH:2 * SH]))
                chain.wait()
                dve.tensor_tensor(acs[:, 1, :], acs[:, 2, :], acs[:, 0, :], ALU.subtract).then_inc(s_acv, 1)
                dve.wait_ge(s_dec, c + 1)

                def segments(g, v):
                    U = 8 * c + 2 * g + v
                    dve.wait_ge(s_lb, U + 1)
                    if U >= 2:
                        dve.wait_ge(s_y, U - 1)
                    for k in range(4):
                        hd = 8 * g + 4 * v + k
                        ins = dve.scalar_tensor_tensor(
                            out=ebuf[:, v, k * P:(k + 1) * P], in0=bank[v][:, k * P:(k + 1) * P],
                            scalar=acs[:, 0, hd:hd + 1], in1=smask[:, :], op0=ALU.subtract, op1=ALU.add)
                    ins.then_inc(s_ein, 1)

                def weights(g, v):
                    U = 8 * c + 2 * g + v
                    dve.wait_ge(s_ee, U + 1)
                    dve.wait_ge(s_cbk, 4 * c + g + 1)
                    dve.tensor_tensor(ebuf[:, v, :].rearrange("p (a l) -> p a l", a=4),
                                      ebuf[:, v, :].rearrange("p (a l) -> p a l", a=4),
                                      cbuf[:, :].unsqueeze(1).to_broadcast([P, 4, P]), ALU.mult).then_inc(s_w, 1)

                for g in range(4):
                    G = 4 * c + g
                    segments(g, 0)
                    segments(g, 1)
                    weights(g, 0)
                    weights(g, 1)
                    dve.wait_ge(s_y, 2 * G + 2)
                    for r in range(4):
                        chain(dve.scalar_tensor_tensor(
                            out=tmp[:, 0, r * P:(r + 1) * P], in0=cv[:, 8 + 4 * g + r, tok],
                            scalar=col("dskip", 4 * g + r), in1=bank[2 + g % 2][:, r * P:(r + 1) * P],
                            op0=ALU.mult, op1=ALU.add))
                    chain.wait()
                    dve.tensor_tensor(zb[:, 4 * g:4 * g + 4, tok], zb[:, 4 * g:4 * g + 4, tok],
                                      tmp[:, 0, :].rearrange("p (r l) -> p r l", r=4), ALU.mult).then_inc(s_yk, 1)
                    if c < NT - 1:
                        dve.wait_ge(s_st, G + 1)
                        hs = slice(8 * g, 8 * g + 8)
                        pr = bank[7][:, :].rearrange("p (h d) -> p h d", h=8)
                        if c == 0:
                            dve.tensor_copy(state[:, hs, :], pr).then_inc(s_stk, 1)
                        else:
                            chain(dve.tensor_tensor(state[:, hs, :], state[:, hs, :],
                                                    acs[:, 2, hs].unsqueeze(2).to_broadcast([P, 8, HD]), ALU.mult))
                            chain.wait()
                            dve.tensor_tensor(state[:, hs, :], state[:, hs, :], pr, ALU.add).then_inc(s_stk, 1)
            for g in range(4):
                stats(Q_GROUP + g, 4 * P)
                dve.wait_ge(s_rb, Q_GROUP + g + 1)
                for j in range(4 * g, 4 * g + 4):
                    dve.scalar_tensor_tensor(out=zb[:, j, :], in0=zb[:, j, :], scalar=col("norm_w", j),
                                             in1=rstd_b[:, :], op0=ALU.mult, op1=ALU.mult).then_inc(s_hid, 1)
                for j in range(4 * g, 4 * g + 4):
                    dve.wait_ge(s_xh, XT["SSD_OUT"] + j + 1)
                    dve.tensor_tensor(ylo[:, j, :], zb[:, j, :], yhi[:, j, :].bitcast(F32), ALU.subtract)\
                        .then_inc(s_xt, 1)
            project_out("SSD_OUT", m_x)
            stats(Q_SSD_POST, D)
            update(Q_SSD_POST, m_x, lambda j: col("gains", 40 + j), "UP2", lambda j: col("gains", 48 + j))
            chain(dve.memset(upad[:, :, 0:2], 0.0))
            chain.wait()
            ffn_up("UP2", 1, XT["DOWN2"], KF, Q_F2_PRE)
            project_out("DOWN2", m_x)
            stats(Q_F2_POST, D)
            update(Q_F2_POST, m_x, lambda j: col("gains", 56 + j))

            def modulated(q, f, name):
                stats(q, D)
                dve.wait_ge(s_rb, q + 1)

                def low(j):
                    dve.wait_ge(s_xh, XT[name] + j + 1)
                    dve.scalar_tensor_tensor(out=xlo[:, j, :], in0=tmp[:, j % 2, :],
                                             scalar=mod[:, 24 * f + j:24 * f + j + 1],
                                             in1=xhi[:, j, :].bitcast(F32), op0=ALU.add, op1=ALU.subtract)\
                        .then_inc(s_xt, 1)
                for j in range(KD):
                    if j >= 2:
                        dve.wait_ge(s_xt, XT[name] + j - 1)
                    dve.scalar_tensor_tensor(out=tmp[:, j % 2, :], in0=h[:, j, :], scalar=gmod[:, 2 * f, j:j + 1],
                                             in1=rstd_b[:, :], op0=ALU.mult, op1=ALU.mult).then_inc(s_hid, 1)
                    if j:
                        low(j - 1)
                low(KD - 1)

            modulated(Q_CONV_PRE, 0, "CONV_IN")
            chain(dve.memset(cpad[:, 0:2], 0.0))
            chain.wait()
            st, ev = START["CONV_IN"], EV["CONV_IN"]

            def conv_low(t):
                dve.wait_ge(s_xh, XT["CONV_OUT"] + t + 1)
                dve.tensor_tensor(yc_lo[:, t, :], cyt[:, t % 2, :], yc_hi[:, t, :].bitcast(F32), ALU.subtract)\
                    .then_inc(s_xt, 1)

            for c in range(24):
                weight_lo(st + c + 2, 0)
                dve.wait_ge(s_pe, st + c + 1)
                t = c % 8
                if c < 8:
                    dve.tensor_copy(cc[:, t, :], psum_ap(c % 4)).then_inc(s_ev, 1)
                elif c < 16:
                    dve.wait_ge(s_ev, ev + 8)
                    chain.wait()
                    dve.tensor_tensor(cpad[:, 2:2 + S], psum_ap(c % 4), cc[:, t, :], ALU.mult).then_inc(s_ev, 1)
                    dve.wait_ge(s_ev, ev + c + 1)
                    chain(dve.tensor_scalar(cy[:, t, :], cpad[:, 2:2 + S], col("cw", 3 * t + 2), None, ALU.mult))
                    for tap in (1, 0):
                        chain.wait()
                        chain(dve.scalar_tensor_tensor(out=cy[:, t, :], in0=cpad[:, tap:tap + S],
                                                       scalar=col("cw", 3 * t + tap), in1=cy[:, t, :],
                                                       op0=ALU.mult, op1=ALU.add))
                else:
                    chain.wait()
                    if t >= 2:
                        dve.wait_ge(s_xt, XT["CONV_OUT"] + t - 1)
                    chain(dve.tensor_tensor(cyt[:, t % 2, :], psum_ap(c % 4), cy[:, t, :], ALU.mult))
                    chain.wait()
                    dve.tensor_copy(small[:, 28:29], rt[:, 0:1]).then_inc(s_ev, 1)
                    dve.tensor_copy(small[:, 27:28], rt[:, 0:1]).then_inc(s_hid, 1)
                    if t:
                        conv_low(t - 1)
            conv_low(7)
            project_out("CONV_OUT", m_conv)
            stats(Q_CONV_POST, D)
            update(Q_CONV_POST, m_conv, lambda j: gmod[:, 1, j:j + 1])
            modulated(Q_F3_PRE, 1, "UP3")
            st, ev = START["UP3"], EV["UP3"]

            def low3(c, i):
                t = c // 2 + 2 * i
                dve.wait_ge(s_xh, XT["DOWN3"] + 1 + t)
                dve.tensor_tensor(hid_lo[:, t, :], hid[:, :], hid_hi[:, t, :].bitcast(F32), ALU.subtract)\
                    .then_inc(s_xt, 1)

            def step3(c, i):
                weight_lo(st + c + 2, i)
                if c % 2 == 0:
                    if not static(i) or c:
                        low3(c - 2, i)
                    dve.wait_ge(s_sg, 2 * KF + c // 2 + 1 + 2 * i)
                    dve.tensor_copy(small[:, 28:29], rt[:, 0:1]).then_inc(s_ev, 1)
                else:
                    dve.wait_ge(s_pe, st + c + 1 + 4 * i)
                    dve.wait_ge(s_xt, XT["DOWN3"] + c // 2 + 2 * i)
                    chain(dve.tensor_tensor(hid[:, :], psum_ap(c % 4), sg[:, :], ALU.mult))
                    chain.wait()
                    dve.tensor_copy(small[:, 28:29], rt[:, 0:1]).then_inc(s_ev, 1)
                    dve.tensor_copy(small[:, 27:28], rt[:, 0:1]).then_inc(s_hid, 1)
            walk(dve, 44, step3, chain, 2)
            low3(42, 0)
            project_out("DOWN3", m_x)
            stats(Q_F3_POST, D)
            update(Q_F3_POST, m_x, lambda j: gmod[:, 3, j:j + 1])


def pack(inputs):
    v = {k: np.asarray(a) for k, a in inputs.items()}

    def panels(w):
        k, f = w.shape
        return w.reshape(k // P, P, f // P, P).transpose(2, 1, 0, 3).reshape(f // P, P, k)

    def halves(w):
        k, f = w.shape
        w = w.reshape(2, k // 2 // P, P, f // P, P).transpose(3, 0, 2, 1, 4)
        return w.reshape(2 * f // P, P, k // 2)

    def paired(a, b):
        return np.stack([panels(a), panels(b)], 1).reshape(2 * a.shape[1] // P, P, a.shape[0])

    w = v["nsa_w_in"][0]
    q = w[:, :D].reshape(D, 2, 2, 4, HD).transpose(0, 1, 3, 2, 4).reshape(D, D)
    kv = w[:, D:D + 6 * 256].reshape(D, 6, 256)
    gates = w[:, D + 6 * 256:]
    vv = np.concatenate([kv[:, 3], kv[:, 5]], 1).reshape(4, 2, P, 512).transpose(0, 2, 1, 3).reshape(4, P, 1024)
    nsa_out = v["nsa_w_out"][0].reshape(2, 2, 4, HD, D).transpose(0, 2, 1, 3, 4).reshape(D, D)
    sw = v["ssd_w_in"][0]
    di = NZ * P
    order = np.concatenate([np.arange(di, di + 1024), np.arange(di)])
    dt = sw[:, 2 * di + 1024:]
    cw = v["conv_w_in_2"][0]
    up, down = v["ffn_w_up"], v["ffn_w_down"]
    gu = v["ffn_w_gate_up_2"][0]
    w8 = np.concatenate(
        [panels(q)] + [panels(kv[:, n]) for n in (0, 1, 2, 4)]
        + [panels(np.concatenate([gates, gates, gates[:, :32]], 1)), vv, panels(nsa_out),
           paired(up[0][:, FH:], up[0][:, :FH]),
           panels(sw[:, di:2 * di + 1024][:, order]), panels(sw[:, :di]), panels(np.concatenate([dt] * 4, 1)),
           halves(v["ssd_w_out"][0]), paired(up[1][:, FH:], up[1][:, :FH]),
           panels(cw[:, D:2 * D]), panels(cw[:, 2 * D:]), panels(cw[:, :D]), panels(v["conv_w_out_2"][0]),
           paired(gu[:, :FH], gu[:, FH:])])
    w11 = np.concatenate([halves(down[0]), halves(down[1]), halves(v["ffn_w_down_2"][0])])

    def cols(a):
        return a.reshape(-1, P).T

    def taps(a, tiles):
        return a.reshape(a.shape[0], tiles, P).transpose(2, 1, 0).reshape(P, -1)

    def pair_cols(a):
        return np.stack([a[..., FH:].reshape(-1, KF, P), a[..., :FH].reshape(-1, KF, P)], 2).reshape(-1, 2 * FH)

    par = np.concatenate(
        [cols(v["norm_gains"]), cols(v["norm_gains_2"]), taps(v["ssd_conv_w"][0][:, order], CH),
         cols(v["ssd_conv_b"][0][order])]
        + [taps(pair_cols(v["ffn_conv_w"][n]), 44) for n in range(2)]
        + [cols(pair_cols(v["ffn_conv_b"][n])) for n in range(2)]
        + [cols(np.repeat(v["ssd_d"][0], HD)), cols(v["ssd_norm_w"][0]), cols(v["c_2"][0]), cols(v["ada_b_2"][0]),
           v["nsa_cmp_pos"][0].reshape(2, 16, 2, HD).transpose(2, 3, 0, 1).reshape(P, 32),
           v["nsa_cmp_w2"][0].reshape(2, 2, P, HD).transpose(2, 0, 1, 3).reshape(P, 256),
           taps(v["conv_w_2"][0], KD)], 1)
    return {
        "w8": w8, "w11": w11, "xT": v["x"][0].T.reshape(KD, P, S).transpose(1, 0, 2), "params": par,
        "heads": np.stack([v["ssd_dt_bias"][0], v["ssd_a_log"][0]], 1),
        "w_cmp": v["nsa_cmp_w1"][0].reshape(2, 16, P, 256).transpose(0, 2, 1, 3),
        "w_ada": v["ada_w_2"][0].reshape(KD, P, ADA_SLICES, ADA_SLICE).transpose(2, 0, 1, 3),
    }


def kernel(**inputs):
    import concourse.bacc as bacc
    from concourse.bass_utils import run_bass_kernel_spmd as run

    nc = bacc.Bacc("TRN2", target_bir_lowering=False, num_devices=1)
    arrays, args = {}, []
    for name, a in pack(inputs).items():
        arrays[name] = np.ascontiguousarray(a)
        args.append(nc.dram_tensor(name, arrays[name].shape, F32, kind="ExternalInput").ap())
    out = nc.dram_tensor("out_t", (P, KD, S), F32, kind="ExternalOutput").ap()
    build(nc, *args, out)
    r = run(nc, [arrays], core_ids=[0])
    return r.results[0]["out_t"].transpose(2, 1, 0).reshape(1, S, D)
```

```python
from contextlib import ExitStack

import numpy as np

import concourse.bass as bass
from concourse import mybir

F32 = mybir.dt.float32
F32R = mybir.dt.float32r
ALU = mybir.AluOpType
ACT = mybir.ActivationFunctionType
AX = mybir.AxisListType

P = 128
S = 512
NT = S // P
D = 1024
KD = D // P
FH = 2816
KF = FH // P
HALF_F = KF // 2
HD = 64
NQ = 8
NC = (S - 32) // 16 + 1
SH = 32
CH = 24
NZ = 16
EPS = 1e-6
NEG = -1e30
QSCALE = HD ** -0.5
ADA_SLICE = 768
ADA_SLICES = 6 * D // ADA_SLICE

PHASES = [
    ("NSA_IN", 21, 8, 1), ("NSA_OUT", 8, 8, 1), ("UP1", 44, 8, 1), ("DOWN1", 16, HALF_F, 2),
    ("SSD_IN", 41, 8, 1), ("SSD_OUT", 16, 8, 2), ("UP2", 44, 8, 1), ("DOWN2", 16, HALF_F, 2),
    ("CONV_IN", 24, 8, 1), ("CONV_OUT", 8, 8, 1), ("UP3", 44, 8, 1), ("DOWN3", 16, HALF_F, 2),
]
START, COUNT, BLOCKS, PER_TILE, DRAM_AT = {}, {}, {}, {}, {}
PANEL_BLOCKS = []
_at8 = _at11 = 0
for _name, _n, _nb, _pt in PHASES:
    START[_name], COUNT[_name], BLOCKS[_name], PER_TILE[_name] = len(PANEL_BLOCKS), _n, _nb, _pt
    if _nb == 8:
        DRAM_AT[_name] = _at8
        _at8 += _n
    else:
        DRAM_AT[_name] = _at11
        _at11 += _n
    PANEL_BLOCKS += [_nb] * _n
TOTAL = len(PANEL_BLOCKS)
N8, N11 = _at8, _at11

OPERANDS = [("NSA_IN", 8), ("NSA_OUT", 8), ("UP1", 8), ("DOWN1", KF), ("SSD_IN", 8), ("SSD_OUT", NZ),
            ("UP2", 8), ("DOWN2", KF), ("CONV_IN", 8), ("CONV_OUT", 8), ("UP3", 8), ("DOWN3", KF)]
XT = {}
_n = 0
for _name, _k in OPERANDS:
    XT[_name] = _n
    _n += _k
EV, MV = {}, {}
_n = 0
for _name, _k in [("NSA_IN", 17), ("UP1", 44), ("SSD_IN", 41), ("UP2", 44), ("CONV_IN", 24), ("UP3", 44)]:
    EV[_name] = _n
    _n += _k
_n = 0
for _name in ["NSA_OUT", "DOWN1", "SSD_OUT", "DOWN2", "CONV_OUT", "DOWN3"]:
    MV[_name] = _n
    _n += 8
(Q_NSA_PRE, Q_NSA_POST, Q_F1_PRE, Q_F1_POST, Q_SSD_PRE, Q_GROUP, _a, _b, _c, Q_SSD_POST, Q_F2_PRE, Q_F2_POST,
 Q_CONV_PRE, Q_CONV_POST, Q_F3_PRE, Q_F3_POST) = range(16)

PARAMS = [("gains", 64), ("gains2", 32), ("ssd_w", CH * 4), ("ssd_b", CH), ("ffn_w", 2 * 44 * 3), ("ffn_b", 2 * 44),
          ("dskip", NZ), ("norm_w", NZ), ("c", KD), ("ada_b", 48), ("pos", 32), ("w2", 256), ("cw", 8 * 3)]
COL = {}
_n = 0
for _name, _k in PARAMS:
    COL[_name] = _n
    _n += _k
NPAR = _n


class Chain:

    def __init__(self, eng, sem):
        self.eng, self.sem, self.n, self.off = eng, sem, 0, 0

    def __call__(self, ins):
        ins.then_inc(self.sem, 1)
        self.n += 1
        return self.n + self.off

    def wait(self, value=None):
        self.eng.wait_ge(self.sem, self.n + self.off if value is None else value)


def static(i):
    return isinstance(i, int)


def walk(eng, n, step, chain=None, per=0):
    groups = n // 4
    for c in range(4):
        step(c, 0)
    if groups > 2:
        before = chain.n if chain else 0
        with eng.Fori(1, groups - 1) as i:
            if chain:
                chain.off = (i - 1) * per
            for c in range(4):
                step(c, i)
        if chain:
            assert chain.n - before == per, (chain.n - before, per)
            chain.n = before + per * (groups - 2)
            chain.off = 0
    for c in range(4 * (groups - 1), n):
        step(c, 0)


def ssd_walk(eng, step, zone, chain=None, per_conv=0, per_z=0, between=None):
    for c in range(4):
        step(c, 0)
    for is_z, (a, b), per in ((False, (1, 6), per_conv), (True, (6, 10), per_z)):
        zone["z"] = is_z
        before = chain.n if chain else 0
        with eng.Fori(a, b) as i:
            if chain:
                chain.off = (i - a) * per
            for c in range(4):
                step(c, i)
        if chain:
            assert chain.n - before == per, (chain.n - before, per)
            chain.n, chain.off = before + per * (b - a), 0
        if between and not is_z:
            between()
    zone["z"] = False
    step(40, 0)


def some(value):
    return not static(value) or value > 0


def unit(k, lag, t, j, jp):
    k -= lag
    if k < 0:
        return None if jp is None else (k + 8, jp, t - 1)
    return None if j is None else (k, j, t)


def tiles_of_q(eng, body, chain=None, per=0):
    body(0, 0, None)
    for j in range(2):
        a = 4 * j + 1
        before = chain.n if chain else 0
        with eng.Fori(a, a + 3) as t:
            if chain:
                chain.off = (t - a) * per
            body(t, j, j)
        if chain:
            assert chain.n - before == per, (chain.n - before, per)
            chain.n, chain.off = before + 3 * per, 0
        body(a + 3, 1 if j == 0 else None, j)


def build(nc, w8, w11, xT, params, heads, w_cmp, w_ada, out, stop=None):
    with ExitStack() as ctx:
        def sem(name):
            return ctx.enter_context(nc.semaphore(name))

        base = [16512]

        def sb(name, shape, dt=F32, at=None):
            size = 4 * int(np.prod(shape[1:]))
            size = (size + 31) // 32 * 32
            if at is None:
                at = base[0]
                base[0] += size
            assert at + size <= 229344, (name, at + size)
            t = nc.alloc_sbuf_tensor_at(name, shape, dt, offset=at)
            ends[name] = at + size
            return t

        ends = {}
        h = sb("h", [P, KD, S])
        RAWW = HALF_F * P
        raw = [sb(f"raw{k}", [P, RAWW]) for k in range(4)]
        whi = [sb(f"whi{k}", [P, RAWW], F32R) for k in range(2)]
        wlo = [sb(f"wlo{k}", [P, RAWW], F32R) for k in range(2)]
        rstd_b = sb("rstd_b", [P, S])
        ssum = sb("ssum", [P, S])
        sqr = sb("sqr", [P, 2, S])
        tmp = sb("tmp", [P, 2, S])
        ident = sb("ident", [P, P])
        ones = sb("ones", [P, P])
        par = sb("par", [P, NPAR])
        hpar = sb("hpar", [SH, 4])
        small = sb("small", [P, 32])
        csil = sb("csil", [P, KD])
        mod = sb("mod", [P, 48])
        gmod = sb("gmod", [P, 4, KD])
        epsc = sb("epsc", [P, 1])
        ms, root, rt = small[:, 0:4], small[:, 4:8], small[:, 8:12]
        arena = base[0]

        def at(kb):
            return arena + int(kb * 1024)

        xhi = sb("xhi", [P, KD, S], F32R, at(0))
        xlo = sb("xlo", [P, KD, S], F32R, at(16))
        m_x = sb("m_x", [P, KD, S], F32, at(0))
        hid_hi = sb("hid_hi", [P, KF, S], F32R, at(32))
        hid_lo = sb("hid_lo", [P, KF, S], F32R, at(76))
        UP = 516
        upad = sb("upad", [P, 2, UP], F32, at(120))
        sg = sb("sg", [P, S], F32, at(124.125))
        hid = sb("hid", [P, S], F32, at(126.125))
        qkv = sb("qkv", [P, 16, S], F32, at(32))
        m_alt = sb("m_alt", [P, KD, S], F32, at(32))
        vtok = sb("vtok", [P, NT, S], F32, at(64))
        swp = sb("swp", [P, 4, S], F32, at(72))
        flat = sb("flat", [P, 16, 4, NC], F32, at(80))
        w1st = sb("w1st", [P, 16, 256], F32, at(88))
        pbuf = sb("pbuf", [P, 4, 2, S], F32, at(80))
        pt = sb("pt", [P, 2, 2, S], F32, at(96))
        hg = sb("hg", [P, 2, 4 * NC], F32, at(104))
        kct = sb("kct", [P, 2, NC], F32, at(105))
        vct = sb("vct", [NC, 4, HD], F32, at(105.5))
        pcmp = sb("pcmp", [P, 4, 32], F32, at(106.5))
        ptc = sb("ptc", [NC, 2, P], F32, at(107))
        gt = sb("gt", [48, S], F32, at(108))
        qst = sb("qst", [P, S], F32, at(108))
        gtok = sb("gtok", [P, NT, 48], F32, at(110))
        mbig = sb("mbig", [P, S], F32, at(111))
        mcmp = sb("mcmp", [P, NT, NC], F32, at(113))
        stat = sb("stat", [P, 4, 32], F32, at(123.25))
        ada_acc = sb("ada_acc", [P, ADA_SLICE], F32, at(114))
        ada_w = sb("ada_w", [P, 2, ADA_SLICE], F32, at(117))
        rowok = sb("rowok", [P, 1], F32, at(123))
        cv = sb("cv", [P, CH, S], F32, at(32))
        zb = sb("zb", [P, NZ, S], F32, at(80))
        yhi = sb("yhi", [P, NZ, S], F32R, at(48))
        ylo = sb("ylo", [P, NZ, S], F32R, at(16))
        xdt = sb("xdt", [P, SH, HD], F32, at(0))
        xdec = sb("xdec", [P, SH, HD], F32, at(8))
        state = sb("state", [P, SH, HD], F32, at(16))
        btok = sb("btok", [P, 4, P], F32, at(24))
        ebuf = sb("ebuf", [P, 2, S], F32, at(26))
        usum = sb("usum", [P, P], F32, at(30))
        smask = sb("smask", [P, P], F32, at(30.5))
        cbuf = sb("cbuf", [P, P], F32, at(31))
        xbuf = sb("xbuf", [P, 2, S], F32, at(112))
        spad = sb("spad", [P, UP], F32, at(116))
        cacc = sb("cacc", [P, 2, S], F32, at(118.25))
        dtt = sb("dtt", [SH, 2, S], F32, at(122.25))
        dtk = sb("dtk", [P, NT, 2, SH], F32, at(126.25))
        acs = sb("acs", [P, 3, SH], F32, at(127.25))
        dw = sb("dw", [SH, 5, S], F32, at(0))
        cc = sb("cc", [P, KD, S], F32, at(32))
        cy = sb("cy", [P, KD, S], F32, at(48))
        yc_hi = sb("yc_hi", [P, KD, S], F32R, at(64))
        yc_lo = sb("yc_lo", [P, KD, S], F32R, at(80))
        m_conv = sb("m_conv", [P, KD, S], F32, at(96))
        cpad = sb("cpad", [P, UP], F32, at(112))
        cyt = sb("cyt", [P, 2, S], F32, at(115))

        bank = [ctx.enter_context(nc.psum_tensor(f"bank{k}", [P, 512], F32)) for k in range(8)]
        stat_ps, bc_ps = bank[5], bank[4]

        s_raw = [sem(f"raw_landed{k}") for k in range(4)]
        s_in = sem("inputs_landed")
        s_const = sem("constants_made")
        s_carry = [sem(f"waits_taken_{e}") for e in ("sp", "dve", "pool")]
        s_hi = sem("weight_hi_made")
        s_lo = sem("weight_lo_made")
        s_pe = sem("panels_multiplied")
        s_ev = sem("in_tiles_taken")
        s_m = sem("out_tiles_taken")
        s_xh = sem("operand_hi_made")
        s_xt = sem("operand_lo_made")
        s_h = sem("residual_updated")
        s_sa = sem("squares_made")
        s_pa = sem("squares_added")
        s_sq = sem("square_sums_made")
        s_stat = sem("token_sums_made")
        s_ms = sem("mean_squares_made")
        s_sqrt = sem("roots_made")
        s_diag = sem("diagonals_made")
        s_bc = sem("rstd_spread")
        s_rb = sem("rstd_kept")
        s_dve = sem("dve_chain")
        s_act = sem("act_chain")
        s_pool = sem("pool_chain")
        s_tap = sem("first_taps_made")
        s_cg = sem("gates_convolved")
        s_sg = sem("gates_silu")
        s_hid = sem("hidden_made")
        s_gate = sem("gates_sigmoid")
        s_gtp = sem("gates_turned")
        s_v = sem("v_panels_taken")
        s_swp = sem("halves_swapped")
        s_w1 = sem("compress_w1_landed")
        s_flat = sem("blocks_flattened")
        s_cm = sem("compress_matmuls")
        s_gelu = sem("compress_gelu")
        s_kv = sem("compressed_kept")
        s_qst = sem("q_staged")
        s_S = sem("scores_made")
        s_sc = sem("scores_masked")
        s_nb = sem("negative_max_made")
        s_e = sem("exps_made")
        s_P = sem("probs_scaled")
        s_T = sem("probs_turned")
        s_tv = sem("turned_kept_dve")
        s_ta = sem("turned_kept_act")
        s_pv = sem("pv_made")
        s_oh = sem("output_halves_hi")
        s_ol = sem("output_halves_taken")
        s_mod = sem("modulation_kept")
        s_ada_w = [sem(f"ada_w_landed{k}") for k in range(2)]
        s_ada = sem("ada_slices_summed")
        s_adap = sem("ada_slices_spread")
        s_csil = sem("c_silu")
        s_cacc = sem("conv_sums_made")
        s_cv = sem("conv_silu_made")
        s_dt = sem("dt_steps")
        s_dta = sem("dt_act_steps")
        s_dtp = sem("dt_turned")
        s_dtk = sem("dt_kept")
        s_xtp = sem("x_turned")
        s_xd = sem("x_dt_made")
        s_bt = sem("b_kept")
        s_ac = sem("cumsums_made")
        s_acv = sem("cumsums_kept")
        s_dec = sem("decays_made")
        s_xdec = sem("x_decayed")
        s_cb = sem("cb_made")
        s_cbk = sem("cb_kept")
        s_lb = sem("cumsums_spread")
        s_ein = sem("segments_made")
        s_ee = sem("segment_exps")
        s_xe = sem("spread_exps")
        s_w = sem("ssd_weights_made")
        s_cx = sem("c_scaled")
        s_y = sem("y_made")
        s_yk = sem("y_kept")
        s_st = sem("state_products")
        s_stk = sem("state_kept")
        s_out = sem("out_stored")

        def col(name, k=0, rows=P):
            c = COL[name] + k
            return par[0:rows, c:c + 1]

        block = ctx.enter_context(nc.Block())

        def psum_ap(t):
            return bank[t][:, :]

        @block.sync
        def _(sp):
            sp.dma_start(h[:, 0:4, :], xT[:, 0:4, :]).then_inc(s_in, 16)
            sp.dma_start(h[:, 4:8, :], xT[:, 4:8, :]).then_inc(s_in, 16)
            sp.dma_start(par[:, :], params).then_inc(s_in, 16)
            sp.dma_start(hpar[:, 0:2], heads).then_inc(s_in, 16)

            def load(name, c, i):
                g = START[name] + c
                nb = BLOCKS[name]
                if g >= 4 or not static(i):
                    sp.wait_ge(s_raw[g % 4], 16 * (g // 4) + 16 * i)
                    if not static(i):
                        sp.sem_inc(s_carry[0], 1)
                    sp.wait_ge(s_lo, g - 3 + 4 * i)
                    if not static(i):
                        sp.sem_inc(s_carry[0], 1)
                src = (w8 if nb == 8 else w11)[DRAM_AT[name] + c + 4 * i]
                sp.dma_start(raw[g % 4][:, 0:nb * P], src).then_inc(s_raw[g % 4], 16)

            for name, n, _, _ in PHASES:
                walk(sp, n, lambda c, i: load(name, c, i))
            sp.wait_ge(s_out, 16 * 8)

        @block.gpsimd
        def _(pool):
            chain = Chain(pool, s_pool)
            chain(pool.memset(ident[:, :], 0.0))
            chain(pool.memset(ones[:, :], 1.0))
            chain(pool.memset(epsc[:, :], EPS))
            chain(pool.memset(mbig[:, :], 0.0))
            chain(pool.memset(mcmp[:, :, :], 0.0))
            chain(pool.memset(rowok[:, :], 1.0))
            chain.wait()
            chain(pool.affine_select(out=ident[:, :], in_=ident[:, :], compare_op=ALU.not_equal, fill=1.0,
                                     base=0, pattern=[[-1, P]], channel_multiplier=1))
            chain(pool.affine_select(out=mbig[:, :], in_=mbig[:, :], compare_op=ALU.is_ge, fill=NEG,
                                     base=S - P, pattern=[[-1, S]], channel_multiplier=1))
            chain(pool.affine_select(out=mcmp[:, :, :], in_=mcmp[:, :, :], compare_op=ALU.is_ge, fill=NEG,
                                     base=-31, pattern=[[P, NT], [-16, NC]], channel_multiplier=1))
            chain(pool.affine_select(out=rowok[:, :], in_=rowok[:, :], compare_op=ALU.is_ge, fill=0.0,
                                     base=-31, pattern=[[0, 1]], channel_multiplier=1))
            chain.wait()
            pool.memset(small[:, 31:32], 0.0).then_inc(s_const, 1)

            squared, adds = [0], Chain(pool, s_pa)

            def add_squares(n):
                for j in range(1, n):
                    pool.wait_ge(s_sa, squared[0] + j + 1)
                    if j > 1:
                        adds.wait()
                    first = sqr[:, 0, :] if j == 1 else ssum[:, :]
                    adds(pool.tensor_tensor(ssum[:, :], first, sqr[:, j % 2, :], ALU.add))
                adds.wait()
                pool.memset(small[:, 31:32], 0.0).then_inc(s_sq, 1)
                squared[0] += n

            add_squares(KD)

            def ada_load(k, s):
                pool.dma_start(ada_w[:, k % 2, :], w_ada[s, k]).then_inc(s_ada_w[k % 2], 16)

            pool.wait_ge(s_csil, 1)
            before = chain.n
            per = 2 * KD - 1
            with pool.Fori(0, ADA_SLICES) as s:
                chain.off = s * per
                chain.wait()
                ada_load(0, s)
                ada_load(1, s)
                for k in range(KD):
                    pool.wait_ge(s_ada_w[k % 2], 16 * (k // 2 + 1) + 16 * (KD // 2) * s)
                    pool.sem_inc(s_carry[2], 1)
                    if k == 0:
                        done = chain(pool.tensor_scalar(ada_acc[:, :], ada_w[:, 0, :], csil[:, 0:1], 1.0,
                                                        ALU.mult, ALU.mult))
                    else:
                        chain(pool.tensor_scalar(ada_w[:, k % 2, :], ada_w[:, k % 2, :], csil[:, k:k + 1], 1.0,
                                                 ALU.mult, ALU.mult))
                        chain.wait()
                        ins = pool.tensor_tensor(ada_acc[:, :], ada_acc[:, :], ada_w[:, k % 2, :], ALU.add)
                        if k < KD - 1:
                            done = chain(ins)
                        else:
                            ins.then_inc(s_ada, 1)
                            pool.wait_ge(s_ada, s + 1)
                            pool.sem_inc(s_carry[2], 1)
                            chain(pool.memset(small[:, 31:32], 0.0))
                    if k + 2 < KD:
                        pool.wait_ge(s_pool, done)
                        ada_load(k + 2, s)
                pool.wait_ge(s_adap, s + 1)
            assert chain.n - before == per, (chain.n - before, per)
            chain.n = before + per * ADA_SLICES
            chain.off = 0

            add_squares(KD)
            add_squares(KD)

            pool.wait_ge(s_pe, START["SSD_IN"] + 41)
            chain(pool.memset(usum[:, :], 1.0))
            chain(pool.memset(smask[:, :], 0.0))
            chain.wait()
            chain(pool.affine_select(out=usum[:, :], in_=usum[:, :], compare_op=ALU.is_ge, fill=0.0,
                                     base=0, pattern=[[1, P]], channel_multiplier=-1))
            chain(pool.affine_select(out=smask[:, :], in_=smask[:, :], compare_op=ALU.is_ge, fill=NEG,
                                     base=0, pattern=[[1, P]], channel_multiplier=-1))
            chain.wait()
            pool.memset(small[:, 31:32], 0.0).then_inc(s_const, 1)

            for c in range(NT):
                tok = slice(c * P, (c + 1) * P)
                if c < NT - 1:
                    pool.wait_ge(s_xd, 4 * (c + 1))
                    pool.wait_ge(s_dec, c + 1)
                    if c > 0:
                        pool.wait_ge(s_st, 4 * c)
                    for k in range(4):
                        hs = slice(8 * k, 8 * k + 8)
                        pool.tensor_tensor(xdec[:, hs, :], xdt[:, hs, :],
                                           acs[:, 1, hs].unsqueeze(2).to_broadcast([P, 8, HD]),
                                           ALU.mult).then_inc(s_xdec, 1)
                if c > 0:
                    for u in range(8):
                        pool.wait_ge(s_xe, 8 * (c - 1) + u + 1)
                        pool.tensor_tensor(xbuf[:, u % 2, :].rearrange("p (a l) -> p a l", a=4),
                                           xbuf[:, u % 2, :].rearrange("p (a l) -> p a l", a=4),
                                           cv[:, 4 + u // 2, tok].unsqueeze(1).to_broadcast([P, 4, P]),
                                           ALU.mult).then_inc(s_cx, 1)
            for g in range(4):
                add_squares(4)
            add_squares(KD)
            add_squares(KD)
            add_squares(KD)

        @block.tensor
        def _(pe):
            def stats_a(q):
                pe.wait_ge(s_sq, q + 1)
                if q:
                    pe.wait_ge(s_ms, q)
                for t in range(NT):
                    mm = pe.matmul(stat_ps[:, t:t + 1], ssum[:, t * P:(t + 1) * P], ones[:, 0:1],
                                   start=True, stop=True)
                mm.then_inc(s_stat, 1)

            def stats_b(q):
                pe.wait_ge(s_diag, q + 1)
                if q:
                    pe.wait_ge(s_rb, q)
                pe.matmul(bc_ps[:, :], ones[:, :], tmp[:, 0, :], start=True, stop=True).then_inc(s_bc, 1)

            def gemm(name, hi, lo, taken, taken_at, q=None, panels=None, others=()):
                st, nb, per = START[name], BLOCKS[name], PER_TILE[name]
                n = panels or COUNT[name]
                nbank = 4 if per == 1 else 2
                for s_, v in others:
                    pe.wait_ge(s_, v)

                def weights(c, i):
                    pe.wait_ge(s_lo, st + c + 1 + 4 * i)

                def bank_free(c, i):
                    t = c // per
                    if not static(i) or t >= nbank:
                        pe.wait_ge(taken, taken_at + t - nbank + 1 + (4 // per) * i)

                def block_of(c, kb, bk):
                    w = (st + c) % 2
                    k = kb + nb * (c % per)
                    first, last = k == 0, k == nb * per - 1
                    cols = slice(kb * P, (kb + 1) * P)
                    pe.matmul(bk, whi[w][:, cols], hi[:, k, :], start=first, stop=False)
                    pe.matmul(bk, whi[w][:, cols], lo[:, k, :], start=False, stop=False)
                    return pe.matmul(bk, wlo[w][:, cols], hi[:, k, :], start=False, stop=last)

                def step(c, i):
                    bk = psum_ap((c // per) % nbank)
                    if c in (0, 1) and static(i) and per == 1:
                        if c == 0:
                            weights(1, 0)
                            for kb in range(nb):
                                pe.wait_ge(s_xt, XT[name] + kb + 1)
                                for cc_ in (0, 1):
                                    mm = block_of(cc_, kb, psum_ap(cc_))
                                    if kb == nb - 1:
                                        mm.then_inc(s_pe, 1)
                            if q is not None:
                                stats_a(q)
                        return
                    weights(c, i)
                    if c % per == 0:
                        bank_free(c, i)
                    for kb in range(nb):
                        if static(i) and c < per:
                            pe.wait_ge(s_xt, XT[name] + kb + nb * c + 1)
                        mm = block_of(c, kb, bk)
                    mm.then_inc(s_pe, 1)
                    if static(i) and c == 2 and q is not None:
                        stats_b(q)

                walk(pe, n, step)

            pe.wait_ge(s_const, 1)
            pe.wait_ge(s_in, 64)
            gemm("NSA_IN", xhi, xlo, s_ev, EV["NSA_IN"], Q_NSA_PRE, panels=17)
            pe.wait_ge(s_rb, 1)
            for c in range(17, 21):
                pe.wait_ge(s_lo, START["NSA_IN"] + c + 1)
                w = (START["NSA_IN"] + c) % 2
                for kk in range(2):
                    k = 2 * (c - 17) + kk
                    cols = slice(kk * S, (kk + 1) * S)
                    for t in range(NT):
                        tk = slice(t * P, (t + 1) * P)
                        bk = bank[4 + t][:, :]
                        pe.matmul(bk, xhi[:, k, tk], whi[w][:, cols], start=k == 0, stop=False)
                        pe.matmul(bk, xhi[:, k, tk], wlo[w][:, cols], start=False, stop=False)
                        mm = pe.matmul(bk, xlo[:, k, tk], whi[w][:, cols], start=False, stop=k == KD - 1)
                mm.then_inc(s_pe, 1)
            pe.wait_ge(s_gate, 1)
            pe.wait_ge(s_ev, 17)
            for t in range(NT):
                mm = pe.transpose(bank[1][:, t * 48:(t + 1) * 48], gt[:, t * P:(t + 1) * P], ident[0:48, 0:48])
            mm.then_inc(s_gtp, 1)
            for kv in range(2):
                pe.wait_ge(s_w1, 16 * (kv + 1))
                pe.wait_ge(s_flat, kv + 1)
                if kv:
                    pe.wait_ge(s_gelu, 1)
                for hh in range(2):
                    for m in range(16):
                        mm = pe.matmul(bank[0][:, hh * P:hh * P + 4 * NC], w1st[:, m, hh * P:(hh + 1) * P],
                                       flat[:, m, :, :].rearrange("p g c -> p (g c)"), start=m == 0, stop=m == 15)
                mm.then_inc(s_cm, 1)
                pe.wait_ge(s_gelu, kv + 1)
                w2 = par[:, COL["w2"] + kv * P:COL["w2"] + (kv + 1) * P].rearrange("p (a d) -> p a d", a=2)
                for g in range(4):
                    cs = slice(g * NC, (g + 1) * NC)
                    for hh in range(2):
                        if kv == 0:
                            o = bank[2][(g % 2) * HD:(g % 2 + 1) * HD, (g // 2) * NC:(g // 2 + 1) * NC]
                            mm = pe.matmul(o, w2[:, hh, :], hg[:, hh, cs], start=hh == 0, stop=hh == 1)
                        else:
                            o = bank[3][0:NC, g * HD:(g + 1) * HD]
                            mm = pe.matmul(o, hg[:, hh, cs], w2[:, hh, :], start=hh == 0, stop=hh == 1)
                mm.then_inc(s_cm, 1)

            pe.wait_ge(s_kv, 2)
            pe.wait_ge(s_v, 1)
            pe.wait_ge(s_gtp, 1)
            def scores(u, j, t):
                qt, a, U = u // 2, u % 2, u + 8 * t
                rows = slice(a * HD, (a + 1) * HD)
                n = (qt + 1) * P
                q_ = qst[rows, qt * P:(qt + 1) * P]
                if u == 0:
                    pe.wait_ge(s_qst, 1 + t)
                if some(U):
                    pe.wait_ge(s_sc, U)
                if u == 7:
                    spread_ada(t)
                pe.matmul(bank[0][:, 0:n], q_, qkv[rows, 12 + j, 0:n], start=True, stop=True)
                pe.matmul(bank[1][:, 0:n], q_, qkv[rows, 14 + j, 0:n], start=True, stop=True)
                if u == 7:
                    pe.wait_ge(s_mod, 1 + t)
                pe.matmul(bank[2][:, 0:NC], q_, kct[rows, j, :], start=True, stop=True).then_inc(s_S, 1)

            def turn(u, j, t):
                qt, U = u // 2, u + 8 * t
                pe.wait_ge(s_P, 1 + U)
                if some(U):
                    pe.wait_ge(s_tv, U)
                    pe.wait_ge(s_ta, U)
                for r in range(2):
                    for kb in range(qt + 1):
                        ks = slice(kb * P, (kb + 1) * P)
                        pe.transpose(bank[3 + r][:, ks], pbuf[:, u % 4, r, ks], ident[:, :])
                pe.transpose(bank[5][0:NC, 0:P], pcmp[:, u % 4, 0:NC], ident[:, :]).then_inc(s_T, 1)

            def pv(u, j, t):
                qt, a, U = u // 2, u % 2, u + 8 * t
                o = bank[6 + qt // 2][a * HD:(a + 1) * HD, (qt % 2) * P:(qt % 2 + 1) * P]
                pe.wait_ge(s_tv, 1 + U)
                pe.wait_ge(s_ta, 1 + U)
                if u == 0 and some(t):
                    pe.wait_ge(s_ol, t)
                if u == 4 and some(t):
                    pe.wait_ge(s_xt, XT["NSA_OUT"] + t)
                g = 2 * j + a
                for r in range(2):
                    for kb in range(qt + 1):
                        pe.matmul(o, vtok[:, kb, r * 256 + g * HD:r * 256 + (g + 1) * HD],
                                  pt[:, u % 2, r, kb * P:(kb + 1) * P], start=r == 0 and kb == 0, stop=False,
                                  skip_group_check=True)
                pe.matmul(o, vct[:, g, :], ptc[:, u % 2, :], start=False, stop=True,
                          skip_group_check=True).then_inc(s_pv, 1)

            def spread_ada(t):
                pe.wait_ge(s_ada, 1 + t)
                for f in range(ADA_SLICE // P):
                    mm = pe.matmul(bank[2][:, 256 + f:257 + f], ada_acc[:, f * P:(f + 1) * P], ones[:, 0:1],
                                   start=True, stop=True)
                mm.then_inc(s_adap, 1)

            def tile(t, j, jp):
                for k in range(8 if j is not None else 3):
                    for stage, lag in ((scores, 0), (turn, 2), (pv, 3)):
                        at_ = unit(k, lag, t, j, jp)
                        if at_:
                            stage(*at_)
            tiles_of_q(pe, tile)

            outs = [(s_ev, EV["UP1"]), (s_sc, 64), (s_tv, 64), (s_ta, 64), (s_mod, 8)]
            gemm("NSA_OUT", xhi, xlo, s_m, MV["NSA_OUT"], others=outs + [(s_ol, 8)])
            stats_a(Q_NSA_POST)
            stats_b(Q_NSA_POST)
            gemm("UP1", xhi, xlo, s_ev, EV["UP1"], Q_F1_PRE, others=[(s_m, 8)])
            gemm("DOWN1", hid_hi, hid_lo, s_m, MV["DOWN1"], others=[(s_ev, EV["SSD_IN"])])
            stats_a(Q_F1_POST)
            stats_b(Q_F1_POST)
            gemm("SSD_IN", xhi, xlo, s_ev, EV["SSD_IN"], Q_SSD_PRE, others=[(s_m, 16)])
            pe.wait_ge(s_dt, 8)
            pe.wait_ge(s_rb, Q_SSD_PRE + 1)
            for t in range(NT):
                for r in range(2):
                    mm = pe.transpose(bank[5][:, (2 * t + r) * SH:(2 * t + r + 1) * SH],
                                      dtt[:, r, t * P:(t + 1) * P], ident[0:SH, 0:SH])
            mm.then_inc(s_dtp, 1)
            pe.wait_ge(s_const, 2)
            pe.wait_ge(s_cv, 40)
            pe.wait_ge(s_ev, EV["UP2"])
            for c in range(NT):
                tok = slice(c * P, (c + 1) * P)
                if c:
                    pe.wait_ge(s_yk, 4 * c)
                    pe.wait_ge(s_w, 8 * c)
                    if c > 1:
                        pe.wait_ge(s_xe, 8 * (c - 1))
                for k in range(4):
                    for r in range(4):
                        mm = pe.transpose(bank[k][:, r * P:(r + 1) * P], cv[:, 8 + 4 * k + r, tok], ident[:, :])
                    mm.then_inc(s_xtp, 1)
                if c:
                    pe.wait_ge(s_bt, c)
                if c < NT - 1:
                    for g in range(4):
                        mm = pe.transpose(bank[4][:, g * P:(g + 1) * P], cv[:, g, tok], ident[:, :])
                    mm.then_inc(s_xtp, 1)
                pe.wait_ge(s_dtk, 1)
                dta = dtk[:, c, 1, :]
                pe.matmul(bank[5][:, 0:SH], usum[:, :], dta, start=True, stop=True)
                pe.matmul(bank[5][:, SH:2 * SH], ones[:, :], dta, start=True, stop=True).then_inc(s_ac, 1)
                pe.wait_ge(s_xd, 4 * (c + 1))
                for g in range(4):
                    G = 4 * c + g
                    if G:
                        pe.wait_ge(s_cbk, G)
                    pe.matmul(bank[6][:, 0:P], cv[:, g, tok], cv[:, 4 + g, tok], start=True, stop=True)\
                        .then_inc(s_cb, 1)
                    for v in range(2):
                        U = 2 * G + v
                        if U >= 2:
                            pe.wait_ge(s_ein, U - 1)
                        if c and U - 8 >= 2:
                            pe.wait_ge(s_xe, U - 8 - 1)
                        for k in range(4):
                            hd = 8 * g + 4 * v + k
                            mm = pe.matmul(bank[v][:, k * P:(k + 1) * P],
                                           dtk[:, c, 1, hd:hd + 1].to_broadcast([P, P]), usum[:, :],
                                           start=True, stop=True)
                        mm.then_inc(s_lb, 1)
                    yb = 2 + g % 2
                    if G >= 2:
                        pe.wait_ge(s_yk, G - 1)
                    for v in range(2):
                        U = 2 * G + v
                        pe.wait_ge(s_w, U + 1)
                        if c:
                            pe.wait_ge(s_cx, U - 8 + 1)
                            pe.wait_ge(s_stk, 4 * (c - 1) + g + 1)
                        for k in range(4):
                            hd = 8 * g + 4 * v + k
                            o = bank[yb][(hd % 2) * HD:(hd % 2 + 1) * HD, (hd // 2 % 4) * P:(hd // 2 % 4 + 1) * P]
                            mm = pe.matmul(o, xdt[:, hd, :], ebuf[:, v, k * P:(k + 1) * P],
                                           start=True, stop=c == 0, skip_group_check=True)
                            if c:
                                mm = pe.matmul(o, state[:, hd, :], xbuf[:, v, k * P:(k + 1) * P],
                                               start=False, stop=True, skip_group_check=True)
                        mm.then_inc(s_y, 1)
                    if c < NT - 1:
                        pe.wait_ge(s_xdec, 4 * c + g + 1)
                        if G:
                            pe.wait_ge(s_stk, G)
                        pe.wait_ge(s_bt, c + 1)
                        pe.matmul(bank[7][:, :], btok[:, g, :],
                                  xdec[:, 8 * g:8 * g + 8, :].rearrange("p h d -> p (h d)"),
                                  start=True, stop=True).then_inc(s_st, 1)
            pe.wait_ge(s_acv, NT)
            for g in range(4):
                stats_a(Q_GROUP + g)
                stats_b(Q_GROUP + g)
            gemm("SSD_OUT", yhi, ylo, s_m, MV["SSD_OUT"], others=[(s_yk, 16)])
            stats_a(Q_SSD_POST)
            stats_b(Q_SSD_POST)
            gemm("UP2", xhi, xlo, s_ev, EV["UP2"], Q_F2_PRE, others=[(s_m, 24)])
            gemm("DOWN2", hid_hi, hid_lo, s_m, MV["DOWN2"], others=[(s_ev, EV["CONV_IN"])])
            stats_a(Q_F2_POST)
            stats_b(Q_F2_POST)
            stats_a(Q_CONV_PRE)
            stats_b(Q_CONV_PRE)
            gemm("CONV_IN", xhi, xlo, s_ev, EV["CONV_IN"], others=[(s_m, 32)])
            gemm("CONV_OUT", yc_hi, yc_lo, s_m, MV["CONV_OUT"], others=[(s_ev, EV["UP3"])])
            stats_a(Q_CONV_POST)
            stats_b(Q_CONV_POST)
            stats_a(Q_F3_PRE)
            stats_b(Q_F3_PRE)
            gemm("UP3", xhi, xlo, s_ev, EV["UP3"], others=[(s_m, 40)])
            gemm("DOWN3", hid_hi, hid_lo, s_m, MV["DOWN3"], others=[(s_ev, EV["UP3"] + 44)])
            stats_a(Q_F3_POST)
            stats_b(Q_F3_POST)

        @block.scalar
        def _(act):
            chain = Chain(act, s_act)

            def weight_hi(g, i):
                if g >= TOTAL:
                    return
                n = PANEL_BLOCKS[g] * P
                act.wait_ge(s_raw[g % 4], 16 * (g // 4 + 1) + 16 * i)
                if g >= 2:
                    act.wait_ge(s_pe, g - 1 + 4 * i)
                act.activation(whi[g % 2][:, 0:n], raw[g % 4][:, 0:n], ACT.Copy).then_inc(s_hi, 1)

            def stats_root(q):
                act.wait_ge(s_ms, q + 1)
                act.activation(root, ms, ACT.Sqrt).then_inc(s_sqrt, 1)

            def stats_keep(q):
                act.wait_ge(s_bc, q + 1)
                act.activation(rstd_b[:, :], bc_ps[:, :], ACT.Copy).then_inc(s_rb, 1)

            added = [0]

            def square(src, j, n):
                need = added[0] + (max(1, j - 2) if j >= 2 else 0)
                if need:
                    act.wait_ge(s_pa, need)
                act.activation(sqr[:, j % 2, :], src, ACT.Square).then_inc(s_sa, 1)
                if j == n - 1:
                    added[0] += n - 1

            def project_in(name, post, q=None, panels=None):
                st = START[name]

                def step(c, i):
                    weight_hi(st + c + 2, i)
                    if q is not None and static(i) and c == 0:
                        stats_root(q)
                        return
                    if q is not None and static(i) and c == 1:
                        stats_keep(q)
                        post(0, 0)
                    post(c, i)
                walk(act, COUNT[name], step)

            def project_out(name, m):
                st, per = START[name], PER_TILE[name]

                def step(c, i):
                    weight_hi(st + c + 2, i)
                    if c % per == per - 1:
                        t = c // per
                        act.wait_ge(s_pe, st + c + 1 + 4 * i)
                        act.activation(m[:, t + (4 // per) * i, :], psum_ap(t % (4 if per == 1 else 2)), ACT.Copy)\
                            .then_inc(s_m, 1)
                walk(act, COUNT[name], step)

            def operands(name, gain, updated):
                for j in range(KD):
                    if updated is not None:
                        act.wait_ge(s_h, updated + j + 1)
                    act.activation(xhi[:, j, :], h[:, j, :], ACT.Copy, scale=gain(j)).then_inc(s_xh, 1)
                    square(h[:, j, :], j, KD)

            def ffn_up(name, layer, hidden_before, q):
                st, ev = START[name], EV[name]

                def first_tap(c, i):
                    k = layer * 44 + c + 4 * i
                    act.wait_ge(s_ev, ev + c + 1 + 4 * i)
                    act.activation(tmp[:, c % 2, :], upad[:, c % 2, 2:2 + S], ACT.Identity,
                                   scale=par[:, bass.ds(COL["ffn_w"] + 3 * k + 2, 1)],
                                   bias=par[:, bass.ds(COL["ffn_b"] + k, 1)]).then_inc(s_tap, 1)

                def post(c, i):
                    t = c // 2 + 2 * i
                    if c % 2 == 0:
                        act.wait_ge(s_cg, layer * KF + t + 1)
                        act.activation(sg[:, :], tmp[:, 0, :], ACT.Silu).then_inc(s_sg, 1)
                    else:
                        act.wait_ge(s_hid, hidden_before + t + 1)
                        act.activation(hid_hi[:, c // 2 + 2 * i, :], hid[:, :], ACT.Copy).then_inc(s_xh, 1)

                def step(c, i):
                    weight_hi(st + c + 2, i)
                    if static(i) and c == 0:
                        stats_root(q)
                        return
                    if static(i) and c == 1:
                        stats_keep(q)
                        first_tap(0, 0)
                    first_tap(c, i)
                    post(c - 1, i)
                walk(act, 44, step)
                post(43, 0)

            act.wait_ge(s_in, 64)
            act.wait_ge(s_const, 1)
            weight_hi(0, 0)
            weight_hi(1, 0)
            operands("NSA_IN", lambda j: col("gains", j), None)
            chain(act.activation(csil[:, :], par[:, COL["c"]:COL["c"] + KD], ACT.Silu))
            chain.wait()
            act.activation(csil[:, 0:1], csil[:, 0:1], ACT.Copy).then_inc(s_csil, 1)

            def nsa_post(c, i):
                if static(i) and c == 16:
                    act.wait_ge(s_ev, 12)
                    act.dma_start(swp[0:HD, :, :], qkv[HD:P, 8:12, :]).then_inc(s_swp, 16)
                    act.dma_start(swp[HD:P, :, :], qkv[0:HD, 8:12, :]).then_inc(s_swp, 16)
                    act.dma_start(w1st[:, :, :], w_cmp[0]).then_inc(s_w1, 16)
                if static(i) and c == 16:
                    act.wait_ge(s_ev, 17)
                    chain(act.activation(gt[:, :], gt[:, :], ACT.Sigmoid))
                    chain.wait()
                    act.activation(gt[0:1, 0:1], gt[0:1, 0:1], ACT.Copy).then_inc(s_gate, 1)

            project_in("NSA_IN", nsa_post, Q_NSA_PRE)
            for kv in range(2):
                act.wait_ge(s_cm, 2 * kv + 1)
                if kv == 0:
                    act.dma_start(w1st[:, :, :], w_cmp[1]).then_inc(s_w1, 16)
                else:
                    act.wait_ge(s_cm, 2)
                act.activation(hg[:, :, :], bank[0][:, 0:2 * P].rearrange("p (a c) -> p a c", a=2)[:, :, 0:4 * NC],
                               ACT.Gelu_apprx_tanh).then_inc(s_gelu, 1)
            act.wait_ge(s_cm, 4)
            def exps(u, j, t):
                qt, b, U = u // 2, u % 4, u + 8 * t
                n = (qt + 1) * P
                act.wait_ge(s_nb, 1 + U)
                for r in range(2):
                    act.activation(pbuf[:, b, r, 0:n], pbuf[:, b, r, 0:n], ACT.Exp, scale=QSCALE,
                                   bias=stat[:, b, 4 + r:5 + r], accum_out=stat[:, b, 8 + r:9 + r])\
                        .then_inc(s_e, 1)
                act.activation(pcmp[:, b, 0:NC], pcmp[:, b, 0:NC], ACT.Exp, scale=QSCALE,
                               bias=stat[:, b, 6:7], accum_out=stat[:, b, 10:11]).then_inc(s_e, 1)

            def keep_turned(u, j, t):
                n, U = (u // 2 + 1) * P, u + 8 * t
                act.wait_ge(s_T, 1 + U)
                if some(U - 1):
                    act.wait_ge(s_pv, U - 1)
                act.activation(ptc[:, u % 2, :], bank[5][0:NC, 0:P], ACT.Copy)
                act.activation(pt[:, u % 2, 1, 0:n], bank[4][:, 0:n], ACT.Copy).then_inc(s_ta, 1)

            def tile(t, j, jp):
                for k in range(8 if j is not None else 3):
                    for stage, lag in ((exps, 0), (keep_turned, 2)):
                        at_ = unit(k, lag, t, j, jp)
                        if at_:
                            stage(*at_)
                    if k == 7:
                        act.wait_ge(s_pv, 4 + 8 * t)
                        act.activation(xhi[:, t, 0:256], bank[6][:, 0:256], ACT.Copy).then_inc(s_oh, 1)
                    if (k == 3 or j is None and k == 2) and jp is not None:
                        act.wait_ge(s_pv, 8 * t)
                        act.activation(xhi[:, t - 1, 256:512], bank[7][:, 0:256], ACT.Copy).then_inc(s_xh, 1)
            tiles_of_q(act, tile)
            project_out("NSA_OUT", m_alt)
            stats_root(Q_NSA_POST)
            stats_keep(Q_NSA_POST)
            operands("UP1", lambda j: col("gains", 16 + j), 0)
            ffn_up("UP1", 0, 0, Q_F1_PRE)
            project_out("DOWN1", m_x)
            stats_root(Q_F1_POST)
            stats_keep(Q_F1_POST)
            operands("SSD_IN", lambda j: col("gains", 32 + j), 8)

            st = START["SSD_IN"]
            zone = {"z": False}

            def ssd_tap(c, i):
                k = c + 4 * i
                act.wait_ge(s_ev, EV["SSD_IN"] + c + 1 + 4 * i)
                if some(c - 1 + 4 * i):
                    act.wait_ge(s_cv, c - 1 + 4 * i)
                act.activation(cacc[:, c % 2, :], spad[:, 3:3 + S], ACT.Identity,
                               scale=par[:, bass.ds(COL["ssd_w"] + 4 * k + 3, 1)],
                               bias=par[:, bass.ds(COL["ssd_b"] + k, 1)]).then_inc(s_tap, 1)

            def ssd_silu(c, i, z):
                if z:
                    act.wait_ge(s_ev, EV["SSD_IN"] + c + 1 + 4 * i)
                    dst = zb[:, c - 24 + 4 * i, :]
                else:
                    act.wait_ge(s_cacc, c + 1 + 4 * i)
                    dst = cv[:, c + 4 * i, :]
                act.activation(dst, cacc[:, c % 2, :], ACT.Silu).then_inc(s_cv, 1)

            def ssd_step(c, i):
                z = zone["z"]
                weight_hi(st + c + 2, i)
                if static(i) and c == 0:
                    stats_root(Q_SSD_PRE)
                    return
                if static(i) and c == 1:
                    stats_keep(Q_SSD_PRE)
                    ssd_tap(0, 0)
                if c == 40:
                    return
                if z:
                    ssd_silu(c, i, True)
                    return
                ssd_tap(c, i)
                ssd_silu(c - 1, i, False)

            ssd_walk(act, ssd_step, zone, between=lambda: ssd_silu(23, 0, False))
            act.wait_ge(s_dt, 1)
            act.activation(dw[:, 1, :], dw[:, 0, :], ACT.Abs).then_inc(s_dta, 1)
            act.wait_ge(s_dta, 1)
            act.activation(dw[:, 1, :], dw[:, 1, :], ACT.Exp, scale=-1.0).then_inc(s_dta, 1)
            act.activation(hpar[:, 2:3], hpar[:, 1:2], ACT.Exp).then_inc(s_dta, 1)
            act.wait_ge(s_dt, 2)
            act.activation(dw[:, 3, :], dw[:, 2, :], ACT.Ln).then_inc(s_dta, 1)
            for c in range(NT):
                if c < NT - 1:
                    act.wait_ge(s_xtp, 5 * (c + 1))
                    if c:
                        act.wait_ge(s_st, 4 * c)
                    act.activation(btok[:, :, :].rearrange("p g n -> p (g n)"), bank[4][:, :], ACT.Copy)\
                        .then_inc(s_bt, 1)
                act.wait_ge(s_acv, c + 1)
                if c:
                    act.wait_ge(s_stk, 4 * c)
                act.activation(acs[:, 1:3, :], acs[:, 1:3, :], ACT.Exp).then_inc(s_dec, 1)
                for g in range(4):
                    G = 4 * c + g
                    act.wait_ge(s_cb, G + 1)
                    if G:
                        act.wait_ge(s_w, 2 * G)
                    act.activation(cbuf[:, :], bank[6][:, 0:P], ACT.Copy).then_inc(s_cbk, 1)
                    for v in range(2):
                        U = 2 * G + v
                        if c:
                            act.wait_ge(s_ein, U + 1)
                            if U - 8 >= 2:
                                act.wait_ge(s_y, U - 1)
                            act.activation(xbuf[:, v, :], bank[v][:, :], ACT.Exp).then_inc(s_xe, 1)
                        act.wait_ge(s_ein, U + 1)
                        act.activation(ebuf[:, v, :], ebuf[:, v, :], ACT.Exp).then_inc(s_ee, 1)
            def group_squares(g):
                act.wait_ge(s_yk, 12 + g + 1)
                for j in range(4):
                    square(zb[:, 4 * g + j, :], j, 4)

            group_squares(0)
            for g in range(4):
                stats_root(Q_GROUP + g)
                stats_keep(Q_GROUP + g)
                if g < 3:
                    group_squares(g + 1)
                for j in range(4 * g, 4 * g + 4):
                    act.wait_ge(s_hid, KF + j + 1)
                    act.activation(yhi[:, j, :], zb[:, j, :], ACT.Copy).then_inc(s_xh, 1)
            project_out("SSD_OUT", m_x)
            stats_root(Q_SSD_POST)
            stats_keep(Q_SSD_POST)
            operands("UP2", lambda j: col("gains", 48 + j), 16)
            ffn_up("UP2", 1, KF + NZ, Q_F2_PRE)
            project_out("DOWN2", m_x)
            stats_root(Q_F2_POST)
            stats_keep(Q_F2_POST)

            def modulated(updated, shift, made):
                for j in range(KD):
                    act.wait_ge(s_h, updated + j + 1)
                    square(h[:, j, :], j, KD)
                q = Q_CONV_PRE if shift == 0 else Q_F3_PRE
                stats_root(q)
                stats_keep(q)
                for j in range(KD):
                    act.wait_ge(s_hid, made + j + 1)
                    act.activation(xhi[:, j, :], tmp[:, j % 2, :], ACT.Identity,
                                   bias=mod[:, shift * KD + j:shift * KD + j + 1]).then_inc(s_xh, 1)

            modulated(24, 0, 2 * KF + NZ)

            def conv_post(c, i):
                if c >= 16:
                    act.wait_ge(s_hid, 2 * KF + NZ + KD + c - 16 + 1)
                    act.activation(yc_hi[:, c - 16, :], cyt[:, c % 2, :], ACT.Copy).then_inc(s_xh, 1)

            st = START["CONV_IN"]
            for c in range(24):
                weight_hi(st + c + 2, 0)
                conv_post(c, 0)
            project_out("CONV_OUT", m_conv)
            stats_root(Q_CONV_POST)
            stats_keep(Q_CONV_POST)
            modulated(32, 3, 2 * KF + NZ + 2 * KD)
            base_t = 2 * KF + NZ + 3 * KD

            def up3_post(c, i):
                if c % 2 == 0:
                    act.wait_ge(s_pe, START["UP3"] + c + 1 + 4 * i)
                    if not static(i) or c >= 2:
                        act.wait_ge(s_hid, base_t + c // 2 + 2 * i)
                    act.activation(sg[:, :], psum_ap(c % 4), ACT.Silu).then_inc(s_sg, 1)
                else:
                    act.wait_ge(s_hid, base_t + c // 2 + 1 + 2 * i)
                    act.activation(hid_hi[:, c // 2 + 2 * i, :], hid[:, :], ACT.Copy).then_inc(s_xh, 1)
            project_in("UP3", up3_post)
            project_out("DOWN3", m_x)
            stats_root(Q_F3_POST)
            stats_keep(Q_F3_POST)
            for j in range(KD):
                act.wait_ge(s_h, 40 + j + 1)
                act.dma_start(out[:, j, :], h[:, j, :]).then_inc(s_out, 16)
            act.wait_ge(s_out, 16 * 8)

        @block.vector
        def _(dve):
            chain = Chain(dve, s_dve)

            def weight_lo(g, i):
                if g >= TOTAL:
                    return
                n = PANEL_BLOCKS[g] * P
                dve.wait_ge(s_hi, g + 1 + 4 * i)
                dve.tensor_tensor(wlo[g % 2][:, 0:n], raw[g % 4][:, 0:n], whi[g % 2][:, 0:n].bitcast(F32),
                                  ALU.subtract).then_inc(s_lo, 1)

            def stats(q, width):
                dve.wait_ge(s_stat, q + 1)
                dve.tensor_scalar(ms, stat_ps[:, 0:4], 1.0 / width, EPS, ALU.mult, ALU.add).then_inc(s_ms, 1)
                dve.wait_ge(s_sqrt, q + 1)
                chain(dve.reciprocal(rt, root))
                chain.wait()
                dve.tensor_tensor(tmp[:, 0, :].rearrange("p (a b) -> p a b", a=NT),
                                  ident[:, :].unsqueeze(1).to_broadcast([P, NT, P]),
                                  rt.unsqueeze(2).to_broadcast([P, NT, P]), ALU.mult).then_inc(s_diag, 1)

            def operand_lo(name, j, gain):
                dve.wait_ge(s_xh, XT[name] + j + 1)
                dve.scalar_tensor_tensor(out=xlo[:, j, :], in0=h[:, j, :], scalar=gain(j),
                                         in1=xhi[:, j, :].bitcast(F32), op0=ALU.mult, op1=ALU.subtract)\
                    .then_inc(s_xt, 1)

            def update(q, m, post_gain, name=None, pre_gain=None):
                dve.wait_ge(s_rb, q + 1)
                for j in range(KD):
                    chain(dve.scalar_tensor_tensor(out=tmp[:, j % 2, :], in0=m[:, j, :], scalar=post_gain(j),
                                                   in1=rstd_b[:, :], op0=ALU.mult, op1=ALU.mult))
                    v = chain.n
                    if name and j:
                        operand_lo(name, j - 1, pre_gain)
                    chain.wait(v)
                    dve.tensor_tensor(h[:, j, :], tmp[:, j % 2, :], h[:, j, :], ALU.add).then_inc(s_h, 1)
                if name:
                    operand_lo(name, KD - 1, pre_gain)

            def project_out(name, m):
                st, per = START[name], PER_TILE[name]
                mv = MV[name]

                def step(c, i):
                    weight_lo(st + c + 2, i)
                    if c % per == per - 1:
                        t, ti = c // per, (4 // per) * i
                        dve.wait_ge(s_m, mv + t + 1 + ti)
                        mt = m[:, t + ti, :]
                        if t == 0 and static(i):
                            chain(dve.tensor_tensor(ssum[:, :], mt, mt, ALU.mult))
                            return
                        chain.wait()
                        chain(dve.tensor_tensor(tmp[:, 0, :], mt, mt, ALU.mult))
                        chain.wait()
                        ins = dve.tensor_tensor(ssum[:, :], ssum[:, :], tmp[:, 0, :], ALU.add)
                        if static(i) and t == KD - 1:
                            ins.then_inc(s_sq, 1)
                        else:
                            chain(ins)
                walk(dve, COUNT[name], step, chain, per=8 // per)

            def ffn_up(name, layer, xt_at, tile_at, q):
                st, ev = START[name], EV[name]

                def lo_of(c, i):
                    dve.wait_ge(s_xh, xt_at + c // 2 + 1 + 2 * i)
                    dve.tensor_tensor(hid_lo[:, c // 2 + 2 * i, :], hid[:, :],
                                      hid_hi[:, c // 2 + 2 * i, :].bitcast(F32), ALU.subtract).then_inc(s_xt, 1)

                def evacuate(c, i):
                    dve.wait_ge(s_pe, st + c + 1 + 4 * i)
                    dve.tensor_tensor(upad[:, c % 2, 2:2 + S], psum_ap(c % 4), rstd_b[:, :], ALU.mult)\
                        .then_inc(s_ev, 1)

                def convolve(c, i):
                    v = c % 2
                    k = layer * 44 + c + 4 * i
                    dve.wait_ge(s_tap, layer * (44 + CH) + c + 1 + 4 * i)
                    chain(dve.scalar_tensor_tensor(out=tmp[:, v, :], in0=upad[:, v, 1:1 + S],
                                                   scalar=par[:, bass.ds(COL["ffn_w"] + 3 * k + 1, 1)],
                                                   in1=tmp[:, v, :], op0=ALU.mult, op1=ALU.add))
                    chain.wait()
                    ins = dve.scalar_tensor_tensor(out=tmp[:, v, :], in0=upad[:, v, 0:S],
                                                   scalar=par[:, bass.ds(COL["ffn_w"] + 3 * k, 1)],
                                                   in1=tmp[:, v, :], op0=ALU.mult, op1=ALU.add)
                    if v == 0:
                        ins.then_inc(s_cg, 1)
                        if static(i) and c == 0:
                            return
                        lo_of(c - 2, i)
                    else:
                        chain(ins)
                        dve.wait_ge(s_sg, layer * KF + c // 2 + 1 + 2 * i)
                        chain.wait()
                        dve.tensor_tensor(hid[:, :], sg[:, :], tmp[:, 1, :], ALU.mult).then_inc(s_hid, 1)

                def step(c, i):
                    if static(i) and c == 0:
                        weight_lo(st + 2, 0)
                        stats(q, D)
                        return
                    if static(i) and c == 1:
                        dve.wait_ge(s_rb, q + 1)
                        evacuate(0, 0)
                    evacuate(c, i)
                    weight_lo(st + c + 2, i)
                    if static(i) and c == 1:
                        convolve(0, 0)
                    convolve(c, i)

                walk(dve, 44, step, chain, per=6)
                lo_of(42, 0)

            dve.wait_ge(s_in, 64)
            dve.wait_ge(s_const, 1)
            weight_lo(0, 0)
            weight_lo(1, 0)
            for j in range(KD):
                operand_lo("NSA_IN", j, lambda k: col("gains", k))

            def nsa_take(c, i):
                dve.wait_ge(s_pe, c + 1 + 4 * i)
                if static(i) and c == 16:
                    dve.tensor_tensor(gt[:, :], bank[0][0:48, :], rstd_b[0:48, :], ALU.mult).then_inc(s_ev, 1)
                else:
                    dve.tensor_tensor(qkv[:, c + 4 * i, :], psum_ap(c % 4), rstd_b[:, :], ALU.mult)\
                        .then_inc(s_ev, 1)

            def nsa_step(c, i):
                weight_lo(START["NSA_IN"] + c + 2, i)
                if static(i) and c == 0:
                    stats(Q_NSA_PRE, D)
                    return
                if static(i) and c == 1:
                    dve.wait_ge(s_rb, 1)
                    nsa_take(0, 0)
                if static(i) and c > 16:
                    return
                nsa_take(c, i)
            walk(dve, 21, nsa_step, chain, 0)
            dve.wait_ge(s_pe, 21)
            for t in range(NT):
                ins = dve.tensor_scalar(vtok[:, t, :], bank[4 + t][:, :], rt[:, t:t + 1], None, ALU.mult)
            ins.then_inc(s_v, 1)
            dve.wait_ge(s_swp, 32)
            dve.wait_ge(s_ev, 12)
            for kv in range(2):
                if kv:
                    dve.wait_ge(s_cm, 1)
                for a in range(2):
                    rows = slice(a * HD, (a + 1) * HD)
                    for b in range(2):
                        src = qkv[rows, 8 + 2 * kv:10 + 2 * kv, :] if a == b else swp[rows, 2 * kv:2 * kv + 2, :]
                        src = src.rearrange("p j (c r) -> p r j c", r=16)[:, a:16:2]
                        for mh in range(2):
                            pos = par[rows, COL["pos"] + 16 * kv + 8 * mh:COL["pos"] + 16 * kv + 8 * mh + 8]
                            for jt in range(2):
                                ins = dve.tensor_tensor(
                                    flat[rows, 8 * mh:8 * mh + 8, b + 2 * jt, :], src[:, :, jt, mh:mh + NC],
                                    pos.unsqueeze(2).to_broadcast([HD, 8, NC]), ALU.add)
                ins.then_inc(s_flat, 1)
            dve.wait_ge(s_gtp, 1)
            chain(dve.tensor_copy(gtok[:, :, :].rearrange("p t n -> p (t n)"), bank[1][:, 0:NT * 48]))
            dve.wait_ge(s_cm, 2)
            dve.tensor_copy(kct[:, :, :].rearrange("p j c -> p (j c)"), bank[2][:, 0:2 * NC]).then_inc(s_kv, 1)
            dve.wait_ge(s_cm, 4)
            dve.tensor_copy(vct[:, :, :].rearrange("p g d -> p (g d)"), bank[3][0:NC, 0:4 * HD]).then_inc(s_kv, 1)

            chain.wait()

            def masked(u, j, t):
                qt, b, U = u // 2, u % 4, u + 8 * t
                n = (qt + 1) * P
                if u == 0:
                    dve.tensor_copy(qst[:, :], qkv[:, t, :]).then_inc(s_qst, 1)
                dve.wait_ge(s_S, 1 + U)
                if some(U - 3):
                    dve.wait_ge(s_T, U - 3)
                dve.sem_inc(s_carry[1], 1)
                for r in range(2):
                    dve.tensor_tensor_reduce(pbuf[:, b, r, 0:n], bank[r][:, 0:n], mbig[:, S - n:S], 1.0,
                                             -3e38, ALU.add, ALU.max, stat[:, b, r:r + 1])
                dve.tensor_tensor_reduce(pcmp[:, b, 0:NC], bank[2][:, 0:NC], mcmp[:, qt, :], 1.0,
                                         -3e38, ALU.add, ALU.max, stat[:, b, 2:3]).then_inc(s_sc, 1)
                dve.wait_ge(s_sc, 1 + U)
                dve.tensor_scalar(stat[:, b, 4:7], stat[:, b, 0:3], -QSCALE, None, ALU.mult)\
                    .then_inc(s_nb, 1)

            def scaled(u, j, t):
                qt, b, U = u // 2, u % 4, u + 8 * t
                n = (qt + 1) * P
                dve.wait_ge(s_e, 3 + 3 * u + 24 * t)
                chain(dve.reciprocal(stat[:, b, 12:15], stat[:, b, 8:11]))
                gate = 3 * (4 * j + 4 * (u % 2))
                gsel = gtok[:, qt, bass.ds(gate + 3 * t + 1, 2)]
                gcmp = gtok[:, qt, bass.ds(gate + 3 * t, 1)]
                chain.wait()
                dve.tensor_tensor(stat[:, b, 16:18], stat[:, b, 12:14], gsel, ALU.mult)
                if qt == 0:
                    chain(dve.scalar_tensor_tensor(out=stat[:, b, 18:19], in0=stat[:, b, 14:15],
                                                   scalar=rowok[:, 0:1], in1=gcmp,
                                                   op0=ALU.mult, op1=ALU.mult))
                else:
                    chain(dve.tensor_tensor(stat[:, b, 18:19], stat[:, b, 14:15], gcmp, ALU.mult))
                chain.wait()
                chain(dve.tensor_scalar(pcmp[:, b, 0:NC], pcmp[:, b, 0:NC], stat[:, b, 18:19], None,
                                        ALU.mult))
                dve.tensor_scalar(pbuf[:, b, 0, 0:n], pbuf[:, b, 0, 0:n], stat[:, b, 16:17], None, ALU.mult)
                dve.tensor_scalar(pbuf[:, b, 1, 0:n], pbuf[:, b, 1, 0:n], stat[:, b, 17:18], None,
                                  ALU.mult).then_inc(s_P, 1)

            def keep_turned(u, j, t):
                n, U = (u // 2 + 1) * P, u + 8 * t
                dve.wait_ge(s_T, 1 + U)
                if some(U - 1):
                    dve.wait_ge(s_pv, U - 1)
                dve.tensor_copy(pt[:, u % 2, 0, 0:n], bank[3][:, 0:n]).then_inc(s_tv, 1)

            def tile(t, j, jp):
                for k in range(8 if j is not None else 3):
                    if k == 7:
                        dve.wait_ge(s_adap, 1 + t)
                        dve.tensor_copy(mod[:, bass.ds(6 * t, 6)], bank[2][:, 256:262]).then_inc(s_mod, 1)
                    for stage, lag in ((masked, 0), (scaled, 1), (keep_turned, 2)):
                        at_ = unit(k, lag, t, j, jp)
                        if at_:
                            stage(*at_)
                    if k == 0 and jp is not None:
                        dve.wait_ge(s_oh, t)
                        dve.tensor_tensor(xlo[:, t - 1, 0:256], bank[6][:, 0:256],
                                          xhi[:, t - 1, 0:256].bitcast(F32), ALU.subtract).then_inc(s_ol, 1)
                    if (k == 3 or j is None and k == 2) and jp is not None:
                        dve.wait_ge(s_xh, XT["NSA_OUT"] + t)
                        dve.tensor_tensor(xlo[:, t - 1, 256:512], bank[7][:, 0:256],
                                          xhi[:, t - 1, 256:512].bitcast(F32), ALU.subtract).then_inc(s_xt, 1)
            tiles_of_q(dve, tile, chain, 8 * 3)
            dve.wait_ge(s_mod, 8)
            chain(dve.tensor_tensor(mod[:, :], mod[:, :], par[:, COL["ada_b"]:COL["ada_b"] + 48], ALU.add))
            chain.wait()
            g2 = par[:, COL["gains2"]:COL["gains2"] + 32].rearrange("p (a k) -> p a k", a=4)
            md = mod[:, :].rearrange("p (a k) -> p a k", a=6)
            for f in range(2):
                chain(dve.tensor_scalar(gmod[:, 2 * f, :], md[:, 3 * f + 1, :], 1.0, None, ALU.add))
                chain.wait()
                chain(dve.tensor_tensor(gmod[:, 2 * f, :], gmod[:, 2 * f, :], g2[:, 2 * f, :], ALU.mult))
                chain(dve.tensor_tensor(gmod[:, 2 * f + 1, :], md[:, 3 * f + 2, :], g2[:, 2 * f + 1, :], ALU.mult))
                chain.wait()

            project_out("NSA_OUT", m_alt)
            stats(Q_NSA_POST, D)
            update(Q_NSA_POST, m_alt, lambda j: col("gains", 8 + j), "UP1", lambda j: col("gains", 16 + j))
            chain(dve.memset(upad[:, :, 0:2], 0.0))
            chain.wait()
            ffn_up("UP1", 0, XT["DOWN1"], 0, Q_F1_PRE)
            project_out("DOWN1", m_x)
            stats(Q_F1_POST, D)
            update(Q_F1_POST, m_x, lambda j: col("gains", 24 + j), "SSD_IN", lambda j: col("gains", 32 + j))
            st, ev = START["SSD_IN"], EV["SSD_IN"]
            chain(dve.memset(spad[:, 0:3], 0.0))
            chain.wait()
            zone = {"z": False}

            def ssd_evacuate(c, i, z):
                dve.wait_ge(s_pe, st + c + 1 + 4 * i)
                if z:
                    dve.wait_ge(s_cv, c - 1 + 4 * i)
                    out_ = cacc[:, c % 2, :]
                else:
                    out_ = spad[:, 3:3 + S]
                dve.tensor_tensor(out_, psum_ap(c % 4), rstd_b[:, :], ALU.mult).then_inc(s_ev, 1)

            def ssd_convolve(c, i):
                k = c + 4 * i
                dve.wait_ge(s_tap, 44 + c + 1 + 4 * i)
                for tap in (2, 1, 0):
                    ins = dve.scalar_tensor_tensor(
                        out=cacc[:, c % 2, :], in0=spad[:, tap:tap + S],
                        scalar=par[:, bass.ds(COL["ssd_w"] + 4 * k + tap, 1)],
                        in1=cacc[:, c % 2, :], op0=ALU.mult, op1=ALU.add)
                    if tap:
                        chain(ins)
                        chain.wait()
                    else:
                        ins.then_inc(s_cacc, 1)
                dve.wait_ge(s_cacc, c + 1 + 4 * i)

            def ssd_step(c, i):
                if static(i) and c == 0:
                    weight_lo(st + 2, 0)
                    stats(Q_SSD_PRE, D)
                    return
                if c == 40:
                    weight_lo(st + 42, 0)
                    dve.wait_ge(s_pe, st + 41)
                    dve.tensor_tensor(dw[:, 0, :], bank[0][0:SH, :], rstd_b[0:SH, :], ALU.mult).then_inc(s_ev, 1)
                    return
                if static(i) and c == 1:
                    dve.wait_ge(s_rb, Q_SSD_PRE + 1)
                    ssd_evacuate(0, 0, False)
                    weight_lo(st + 3, 0)
                    ssd_convolve(0, 0)
                    ssd_evacuate(1, 0, False)
                    ssd_convolve(1, 0)
                    return
                z = zone["z"]
                ssd_evacuate(c, i, z)
                weight_lo(st + c + 2, i)
                if not z:
                    ssd_convolve(c, i)

            ssd_walk(dve, ssd_step, zone, chain, 8, 0)
            dve.wait_ge(s_ev, EV["UP2"])
            chain(dve.tensor_scalar(dw[:, 4, :], dw[:, 0, :], hpar[:, 0:1], None, ALU.add))
            chain.wait()
            dve.tensor_copy(dw[:, 0, :], dw[:, 4, :]).then_inc(s_dt, 1)
            dve.wait_ge(s_dta, 3)
            dve.tensor_scalar(dw[:, 2, :], dw[:, 1, :], 1.0, None, ALU.add).then_inc(s_dt, 1)
            dve.wait_ge(s_dt, 2)
            chain(dve.tensor_scalar(dw[:, 4, :], dw[:, 2, :], 1.0, 1e-30, ALU.subtract, ALU.max))
            chain.wait()
            chain(dve.reciprocal(dw[:, 4, :], dw[:, 4, :]))
            chain.wait()
            dve.tensor_tensor(dw[:, 4, :], dw[:, 4, :], dw[:, 1, :], ALU.mult).then_inc(s_dt, 1)
            dve.wait_ge(s_dt, 3)
            dve.wait_ge(s_dta, 4)
            chain(dve.tensor_tensor(dw[:, 3, :], dw[:, 3, :], dw[:, 4, :], ALU.mult))
            chain(dve.tensor_scalar(dw[:, 2, :], dw[:, 2, :], 1.0, None, ALU.is_equal))
            chain.wait()
            dve.tensor_tensor(dw[:, 2, :], dw[:, 2, :], dw[:, 1, :], ALU.mult).then_inc(s_dt, 1)
            dve.wait_ge(s_dt, 4)
            dve.tensor_tensor(dw[:, 3, :], dw[:, 3, :], dw[:, 2, :], ALU.add).then_inc(s_dt, 1)
            dve.wait_ge(s_dt, 5)
            dve.scalar_tensor_tensor(out=dtt[:, 0, :], in0=dw[:, 0, :], scalar=0.0, in1=dw[:, 3, :],
                                     op0=ALU.max, op1=ALU.add).then_inc(s_dt, 1)
            dve.tensor_scalar(hpar[:, 3:4], hpar[:, 2:3], -1.0, None, ALU.mult).then_inc(s_dt, 1)
            dve.wait_ge(s_dt, 7)
            dve.tensor_scalar(dtt[:, 1, :], dtt[:, 0, :], hpar[:, 3:4], None, ALU.mult).then_inc(s_dt, 1)
            dve.wait_ge(s_dtp, 1)
            dve.tensor_copy(dtk[:, :, :, :].rearrange("p t r h -> p (t r h)"), bank[5][:, 0:NT * 2 * SH])\
                .then_inc(s_dtk, 1)
            dve.wait_ge(s_dtk, 1)
            dve.wait_ge(s_cv, 40)
            dve.wait_ge(s_const, 2)
            for c in range(NT):
                tok = slice(c * P, (c + 1) * P)
                if c:
                    dve.wait_ge(s_xdec, 4 * c)
                for k in range(4):
                    dve.wait_ge(s_xtp, (5 * c if c < NT else 0) + k + 1)
                    if c:
                        dve.wait_ge(s_y, 8 * c)
                    dve.tensor_tensor(xdt[:, 8 * k:8 * k + 8, :], bank[k][:, :].rearrange("p (h d) -> p h d", h=8),
                                      dtk[:, c, 0, 8 * k:8 * k + 8].unsqueeze(2).to_broadcast([P, 8, HD]),
                                      ALU.mult).then_inc(s_xd, 1)
                dve.wait_ge(s_ac, c + 1)
                if c:
                    dve.wait_ge(s_xdec, 4 * c)
                chain(dve.tensor_copy(acs[:, 0, :], bank[5][:, 0:SH]))
                chain(dve.tensor_copy(acs[:, 2, :], bank[5][:, SH:2 * SH]))
                chain.wait()
                dve.tensor_tensor(acs[:, 1, :], acs[:, 2, :], acs[:, 0, :], ALU.subtract).then_inc(s_acv, 1)
                dve.wait_ge(s_dec, c + 1)

                def segments(g, v):
                    U = 8 * c + 2 * g + v
                    dve.wait_ge(s_lb, U + 1)
                    if U >= 2:
                        dve.wait_ge(s_y, U - 1)
                    for k in range(4):
                        hd = 8 * g + 4 * v + k
                        ins = dve.scalar_tensor_tensor(
                            out=ebuf[:, v, k * P:(k + 1) * P], in0=bank[v][:, k * P:(k + 1) * P],
                            scalar=acs[:, 0, hd:hd + 1], in1=smask[:, :], op0=ALU.subtract, op1=ALU.add)
                    ins.then_inc(s_ein, 1)

                def weights(g, v):
                    U = 8 * c + 2 * g + v
                    dve.wait_ge(s_ee, U + 1)
                    dve.wait_ge(s_cbk, 4 * c + g + 1)
                    dve.tensor_tensor(ebuf[:, v, :].rearrange("p (a l) -> p a l", a=4),
                                      ebuf[:, v, :].rearrange("p (a l) -> p a l", a=4),
                                      cbuf[:, :].unsqueeze(1).to_broadcast([P, 4, P]), ALU.mult).then_inc(s_w, 1)

                for g in range(4):
                    G = 4 * c + g
                    segments(g, 0)
                    segments(g, 1)
                    weights(g, 0)
                    weights(g, 1)
                    dve.wait_ge(s_y, 2 * G + 2)
                    for r in range(4):
                        chain(dve.scalar_tensor_tensor(
                            out=tmp[:, 0, r * P:(r + 1) * P], in0=cv[:, 8 + 4 * g + r, tok],
                            scalar=col("dskip", 4 * g + r), in1=bank[2 + g % 2][:, r * P:(r + 1) * P],
                            op0=ALU.mult, op1=ALU.add))
                    chain.wait()
                    dve.tensor_tensor(zb[:, 4 * g:4 * g + 4, tok], zb[:, 4 * g:4 * g + 4, tok],
                                      tmp[:, 0, :].rearrange("p (r l) -> p r l", r=4), ALU.mult).then_inc(s_yk, 1)
                    if c < NT - 1:
                        dve.wait_ge(s_st, G + 1)
                        hs = slice(8 * g, 8 * g + 8)
                        pr = bank[7][:, :].rearrange("p (h d) -> p h d", h=8)
                        if c == 0:
                            dve.tensor_copy(state[:, hs, :], pr).then_inc(s_stk, 1)
                        else:
                            chain(dve.tensor_tensor(state[:, hs, :], state[:, hs, :],
                                                    acs[:, 2, hs].unsqueeze(2).to_broadcast([P, 8, HD]), ALU.mult))
                            chain.wait()
                            dve.tensor_tensor(state[:, hs, :], state[:, hs, :], pr, ALU.add).then_inc(s_stk, 1)
            for g in range(4):
                stats(Q_GROUP + g, 4 * P)
                dve.wait_ge(s_rb, Q_GROUP + g + 1)
                for j in range(4 * g, 4 * g + 4):
                    dve.scalar_tensor_tensor(out=zb[:, j, :], in0=zb[:, j, :], scalar=col("norm_w", j),
                                             in1=rstd_b[:, :], op0=ALU.mult, op1=ALU.mult).then_inc(s_hid, 1)
                for j in range(4 * g, 4 * g + 4):
                    dve.wait_ge(s_xh, XT["SSD_OUT"] + j + 1)
                    dve.tensor_tensor(ylo[:, j, :], zb[:, j, :], yhi[:, j, :].bitcast(F32), ALU.subtract)\
                        .then_inc(s_xt, 1)
            project_out("SSD_OUT", m_x)
            stats(Q_SSD_POST, D)
            update(Q_SSD_POST, m_x, lambda j: col("gains", 40 + j), "UP2", lambda j: col("gains", 48 + j))
            chain(dve.memset(upad[:, :, 0:2], 0.0))
            chain.wait()
            ffn_up("UP2", 1, XT["DOWN2"], KF, Q_F2_PRE)
            project_out("DOWN2", m_x)
            stats(Q_F2_POST, D)
            update(Q_F2_POST, m_x, lambda j: col("gains", 56 + j))

            def modulated(q, f, name):
                stats(q, D)
                dve.wait_ge(s_rb, q + 1)

                def low(j):
                    dve.wait_ge(s_xh, XT[name] + j + 1)
                    dve.scalar_tensor_tensor(out=xlo[:, j, :], in0=tmp[:, j % 2, :],
                                             scalar=mod[:, 24 * f + j:24 * f + j + 1],
                                             in1=xhi[:, j, :].bitcast(F32), op0=ALU.add, op1=ALU.subtract)\
                        .then_inc(s_xt, 1)
                for j in range(KD):
                    if j >= 2:
                        dve.wait_ge(s_xt, XT[name] + j - 1)
                    dve.scalar_tensor_tensor(out=tmp[:, j % 2, :], in0=h[:, j, :], scalar=gmod[:, 2 * f, j:j + 1],
                                             in1=rstd_b[:, :], op0=ALU.mult, op1=ALU.mult).then_inc(s_hid, 1)
                    if j:
                        low(j - 1)
                low(KD - 1)

            modulated(Q_CONV_PRE, 0, "CONV_IN")
            chain(dve.memset(cpad[:, 0:2], 0.0))
            chain.wait()
            st, ev = START["CONV_IN"], EV["CONV_IN"]

            def conv_low(t):
                dve.wait_ge(s_xh, XT["CONV_OUT"] + t + 1)
                dve.tensor_tensor(yc_lo[:, t, :], cyt[:, t % 2, :], yc_hi[:, t, :].bitcast(F32), ALU.subtract)\
                    .then_inc(s_xt, 1)

            for c in range(24):
                weight_lo(st + c + 2, 0)
                dve.wait_ge(s_pe, st + c + 1)
                t = c % 8
                if c < 8:
                    dve.tensor_copy(cc[:, t, :], psum_ap(c % 4)).then_inc(s_ev, 1)
                elif c < 16:
                    dve.wait_ge(s_ev, ev + 8)
                    chain.wait()
                    dve.tensor_tensor(cpad[:, 2:2 + S], psum_ap(c % 4), cc[:, t, :], ALU.mult).then_inc(s_ev, 1)
                    dve.wait_ge(s_ev, ev + c + 1)
                    chain(dve.tensor_scalar(cy[:, t, :], cpad[:, 2:2 + S], col("cw", 3 * t + 2), None, ALU.mult))
                    for tap in (1, 0):
                        chain.wait()
                        chain(dve.scalar_tensor_tensor(out=cy[:, t, :], in0=cpad[:, tap:tap + S],
                                                       scalar=col("cw", 3 * t + tap), in1=cy[:, t, :],
                                                       op0=ALU.mult, op1=ALU.add))
                else:
                    chain.wait()
                    if t >= 2:
                        dve.wait_ge(s_xt, XT["CONV_OUT"] + t - 1)
                    chain(dve.tensor_tensor(cyt[:, t % 2, :], psum_ap(c % 4), cy[:, t, :], ALU.mult))
                    chain.wait()
                    dve.tensor_copy(small[:, 28:29], rt[:, 0:1]).then_inc(s_ev, 1)
                    dve.tensor_copy(small[:, 27:28], rt[:, 0:1]).then_inc(s_hid, 1)
                    if t:
                        conv_low(t - 1)
            conv_low(7)
            project_out("CONV_OUT", m_conv)
            stats(Q_CONV_POST, D)
            update(Q_CONV_POST, m_conv, lambda j: gmod[:, 1, j:j + 1])
            modulated(Q_F3_PRE, 1, "UP3")
            st, ev = START["UP3"], EV["UP3"]

            def low3(c, i):
                t = c // 2 + 2 * i
                dve.wait_ge(s_xh, XT["DOWN3"] + 1 + t)
                dve.tensor_tensor(hid_lo[:, t, :], hid[:, :], hid_hi[:, t, :].bitcast(F32), ALU.subtract)\
                    .then_inc(s_xt, 1)

            def step3(c, i):
                weight_lo(st + c + 2, i)
                if c % 2 == 0:
                    if not static(i) or c:
                        low3(c - 2, i)
                    dve.wait_ge(s_sg, 2 * KF + c // 2 + 1 + 2 * i)
                    dve.tensor_copy(small[:, 28:29], rt[:, 0:1]).then_inc(s_ev, 1)
                else:
                    dve.wait_ge(s_pe, st + c + 1 + 4 * i)
                    dve.wait_ge(s_xt, XT["DOWN3"] + c // 2 + 2 * i)
                    chain(dve.tensor_tensor(hid[:, :], psum_ap(c % 4), sg[:, :], ALU.mult))
                    chain.wait()
                    dve.tensor_copy(small[:, 28:29], rt[:, 0:1]).then_inc(s_ev, 1)
                    dve.tensor_copy(small[:, 27:28], rt[:, 0:1]).then_inc(s_hid, 1)
            walk(dve, 44, step3, chain, 2)
            low3(42, 0)
            project_out("DOWN3", m_x)
            stats(Q_F3_POST, D)
            update(Q_F3_POST, m_x, lambda j: gmod[:, 3, j:j + 1])


def pack(inputs):
    v = {k: np.asarray(a) for k, a in inputs.items()}

    def panels(w):
        k, f = w.shape
        return w.reshape(k // P, P, f // P, P).transpose(2, 1, 0, 3).reshape(f // P, P, k)

    def halves(w):
        k, f = w.shape
        w = w.reshape(2, k // 2 // P, P, f // P, P).transpose(3, 0, 2, 1, 4)
        return w.reshape(2 * f // P, P, k // 2)

    def paired(a, b):
        return np.stack([panels(a), panels(b)], 1).reshape(2 * a.shape[1] // P, P, a.shape[0])

    w = v["nsa_w_in"][0]
    q = w[:, :D].reshape(D, 2, 2, 4, HD).transpose(0, 1, 3, 2, 4).reshape(D, D)
    kv = w[:, D:D + 6 * 256].reshape(D, 6, 256)
    gates = w[:, D + 6 * 256:]
    vv = np.concatenate([kv[:, 3], kv[:, 5]], 1).reshape(4, 2, P, 512).transpose(0, 2, 1, 3).reshape(4, P, 1024)
    nsa_out = v["nsa_w_out"][0].reshape(2, 2, 4, HD, D).transpose(0, 2, 1, 3, 4).reshape(D, D)
    sw = v["ssd_w_in"][0]
    di = NZ * P
    order = np.concatenate([np.arange(di, di + 1024), np.arange(di)])
    dt = sw[:, 2 * di + 1024:]
    cw = v["conv_w_in_2"][0]
    up, down = v["ffn_w_up"], v["ffn_w_down"]
    gu = v["ffn_w_gate_up_2"][0]
    w8 = np.concatenate(
        [panels(q)] + [panels(kv[:, n]) for n in (0, 1, 2, 4)]
        + [panels(np.concatenate([gates, gates, gates[:, :32]], 1)), vv, panels(nsa_out),
           paired(up[0][:, FH:], up[0][:, :FH]),
           panels(sw[:, di:2 * di + 1024][:, order]), panels(sw[:, :di]), panels(np.concatenate([dt] * 4, 1)),
           halves(v["ssd_w_out"][0]), paired(up[1][:, FH:], up[1][:, :FH]),
           panels(cw[:, D:2 * D]), panels(cw[:, 2 * D:]), panels(cw[:, :D]), panels(v["conv_w_out_2"][0]),
           paired(gu[:, :FH], gu[:, FH:])])
    w11 = np.concatenate([halves(down[0]), halves(down[1]), halves(v["ffn_w_down_2"][0])])

    def cols(a):
        return a.reshape(-1, P).T

    def taps(a, tiles):
        return a.reshape(a.shape[0], tiles, P).transpose(2, 1, 0).reshape(P, -1)

    def pair_cols(a):
        return np.stack([a[..., FH:].reshape(-1, KF, P), a[..., :FH].reshape(-1, KF, P)], 2).reshape(-1, 2 * FH)

    par = np.concatenate(
        [cols(v["norm_gains"]), cols(v["norm_gains_2"]), taps(v["ssd_conv_w"][0][:, order], CH),
         cols(v["ssd_conv_b"][0][order])]
        + [taps(pair_cols(v["ffn_conv_w"][n]), 44) for n in range(2)]
        + [cols(pair_cols(v["ffn_conv_b"][n])) for n in range(2)]
        + [cols(np.repeat(v["ssd_d"][0], HD)), cols(v["ssd_norm_w"][0]), cols(v["c_2"][0]), cols(v["ada_b_2"][0]),
           v["nsa_cmp_pos"][0].reshape(2, 16, 2, HD).transpose(2, 3, 0, 1).reshape(P, 32),
           v["nsa_cmp_w2"][0].reshape(2, 2, P, HD).transpose(2, 0, 1, 3).reshape(P, 256),
           taps(v["conv_w_2"][0], KD)], 1)
    return {
        "w8": w8, "w11": w11, "xT": v["x"][0].T.reshape(KD, P, S).transpose(1, 0, 2), "params": par,
        "heads": np.stack([v["ssd_dt_bias"][0], v["ssd_a_log"][0]], 1),
        "w_cmp": v["nsa_cmp_w1"][0].reshape(2, 16, P, 256).transpose(0, 2, 1, 3),
        "w_ada": v["ada_w_2"][0].reshape(KD, P, ADA_SLICES, ADA_SLICE).transpose(2, 0, 1, 3),
    }


def kernel(**inputs):
    import concourse.bacc as bacc
    from concourse.bass_utils import run_bass_kernel_spmd as run

    nc = bacc.Bacc("TRN2", target_bir_lowering=False, num_devices=1)
    arrays, args = {}, []
    for name, a in pack(inputs).items():
        arrays[name] = np.ascontiguousarray(a)
        args.append(nc.dram_tensor(name, arrays[name].shape, F32, kind="ExternalInput").ap())
    out = nc.dram_tensor("out_t", (P, KD, S), F32, kind="ExternalOutput").ap()
    build(nc, *args, out)
    r = run(nc, [arrays], core_ids=[0])
    return r.results[0]["out_t"].transpose(2, 1, 0).reshape(1, S, D)
```

```python
from contextlib import ExitStack

import numpy as np

import concourse.bass as bass
from concourse import mybir

F32 = mybir.dt.float32
F32R = mybir.dt.float32r
ALU = mybir.AluOpType
ACT = mybir.ActivationFunctionType
AX = mybir.AxisListType

P = 128
S = 512
NT = S // P
D = 1024
KD = D // P
FH = 2816
KF = FH // P
HALF_F = KF // 2
HD = 64
NQ = 8
NC = (S - 32) // 16 + 1
SH = 32
CH = 24
NZ = 16
EPS = 1e-6
NEG = -1e30
QSCALE = HD ** -0.5
ADA_SLICE = 768
ADA_SLICES = 6 * D // ADA_SLICE

PHASES = [
    ("NSA_IN", 21, 8, 1), ("NSA_OUT", 8, 8, 1), ("UP1", 44, 8, 1), ("DOWN1", 16, HALF_F, 2),
    ("SSD_IN", 41, 8, 1), ("SSD_OUT", 16, 8, 2), ("UP2", 44, 8, 1), ("DOWN2", 16, HALF_F, 2),
    ("CONV_IN", 24, 8, 1), ("CONV_OUT", 8, 8, 1), ("UP3", 44, 8, 1), ("DOWN3", 16, HALF_F, 2),
]
START, COUNT, BLOCKS, PER_TILE, DRAM_AT = {}, {}, {}, {}, {}
PANEL_BLOCKS = []
_at8 = _at11 = 0
for _name, _n, _nb, _pt in PHASES:
    START[_name], COUNT[_name], BLOCKS[_name], PER_TILE[_name] = len(PANEL_BLOCKS), _n, _nb, _pt
    if _nb == 8:
        DRAM_AT[_name] = _at8
        _at8 += _n
    else:
        DRAM_AT[_name] = _at11
        _at11 += _n
    PANEL_BLOCKS += [_nb] * _n
TOTAL = len(PANEL_BLOCKS)
N8, N11 = _at8, _at11

OPERANDS = [("NSA_IN", 8), ("NSA_OUT", 8), ("UP1", 8), ("DOWN1", KF), ("SSD_IN", 8), ("SSD_OUT", NZ),
            ("UP2", 8), ("DOWN2", KF), ("CONV_IN", 8), ("CONV_OUT", 8), ("UP3", 8), ("DOWN3", KF)]
XT = {}
_n = 0
for _name, _k in OPERANDS:
    XT[_name] = _n
    _n += _k
EV, MV = {}, {}
_n = 0
for _name, _k in [("NSA_IN", 17), ("UP1", 44), ("SSD_IN", 41), ("UP2", 44), ("CONV_IN", 24), ("UP3", 44)]:
    EV[_name] = _n
    _n += _k
_n = 0
for _name in ["NSA_OUT", "DOWN1", "SSD_OUT", "DOWN2", "CONV_OUT", "DOWN3"]:
    MV[_name] = _n
    _n += 8
(Q_NSA_PRE, Q_NSA_POST, Q_F1_PRE, Q_F1_POST, Q_SSD_PRE, Q_SSD_POST, Q_F2_PRE, Q_F2_POST,
 Q_CONV_PRE, Q_CONV_POST, Q_F3_PRE, Q_F3_POST) = range(12)
KEPT = {q: n + 1 for n, q in enumerate([Q_NSA_PRE, Q_F1_PRE, Q_SSD_PRE, Q_F2_PRE])}
LAST = {q: n + 1 for n, q in enumerate([Q_NSA_POST, Q_F1_POST, Q_SSD_POST, Q_F2_POST, Q_CONV_POST, Q_F3_POST])}

PARAMS = [("gains", 64), ("gains2", 32), ("ssd_w", CH * 4), ("ssd_b", CH), ("ffn_w", 2 * 44 * 3), ("ffn_b", 2 * 44),
          ("dskip", NZ), ("norm_w", NZ), ("c", KD), ("ada_b", 48), ("pos", 32), ("w2", 256), ("cw", 8 * 3)]
COL = {}
_n = 0
for _name, _k in PARAMS:
    COL[_name] = _n
    _n += _k
NPAR = _n


class Chain:

    def __init__(self, eng, sem):
        self.eng, self.sem, self.n, self.off = eng, sem, 0, 0

    def __call__(self, ins):
        ins.then_inc(self.sem, 1)
        self.n += 1
        return self.n + self.off

    def wait(self, value=None):
        self.eng.wait_ge(self.sem, self.n + self.off if value is None else value)


def static(i):
    return isinstance(i, int)


def walk(eng, n, step, chain=None, per=0):
    groups = n // 4
    for c in range(4):
        step(c, 0)
    if groups > 2:
        before = chain.n if chain else 0
        with eng.Fori(1, groups - 1) as i:
            if chain:
                chain.off = (i - 1) * per
            for c in range(4):
                step(c, i)
        if chain:
            assert chain.n - before == per, (chain.n - before, per)
            chain.n = before + per * (groups - 2)
            chain.off = 0
    for c in range(4 * (groups - 1), n):
        step(c, 0)


def ssd_walk(eng, step, zone, chain=None, per_conv=0, per_z=0, between=None):
    for c in range(4):
        step(c, 0)
    for is_z, (a, b), per in ((False, (1, 6), per_conv), (True, (6, 10), per_z)):
        zone["z"] = is_z
        before = chain.n if chain else 0
        with eng.Fori(a, b) as i:
            if chain:
                chain.off = (i - a) * per
            for c in range(4):
                step(c, i)
        if chain:
            assert chain.n - before == per, (chain.n - before, per)
            chain.n, chain.off = before + per * (b - a), 0
        if between and not is_z:
            between()
    zone["z"] = False
    step(40, 0)


def some(value):
    return not static(value) or value > 0


def unit(k, lag, t, j, jp):
    k -= lag
    if k < 0:
        return None if jp is None else (k + 8, jp, t - 1)
    return None if j is None else (k, j, t)


def tiles_of_q(eng, body, chain=None, per=0):
    body(0, 0, None)
    for j in range(2):
        a = 4 * j + 1
        before = chain.n if chain else 0
        with eng.Fori(a, a + 3) as t:
            if chain:
                chain.off = (t - a) * per
            body(t, j, j)
        if chain:
            assert chain.n - before == per, (chain.n - before, per)
            chain.n, chain.off = before + 3 * per, 0
        body(a + 3, 1 if j == 0 else None, j)


def build(nc, w8, w11, xT, params, heads, w_cmp, w_ada, out, stop=None):
    with ExitStack() as ctx:
        def sem(name):
            return ctx.enter_context(nc.semaphore(name))

        base = [16512]

        def sb(name, shape, dt=F32, at=None):
            size = 4 * int(np.prod(shape[1:]))
            size = (size + 31) // 32 * 32
            if at is None:
                at = base[0]
                base[0] += size
            assert at + size <= 229344, (name, at + size)
            t = nc.alloc_sbuf_tensor_at(name, shape, dt, offset=at)
            ends[name] = at + size
            return t

        ends = {}
        h = sb("h", [P, KD, S])
        RAWW = HALF_F * P
        raw = [sb(f"raw{k}", [P, RAWW]) for k in range(4)]
        whi = [sb(f"whi{k}", [P, RAWW], F32R) for k in range(2)]
        wlo = [sb(f"wlo{k}", [P, RAWW], F32R) for k in range(2)]
        rstd_b = sb("rstd_b", [P, S])
        ssum = sb("ssum", [P, S])
        sqr = sb("sqr", [P, 2, S])
        tmp = sb("tmp", [P, 2, S])
        ident = sb("ident", [P, P])
        ones = sb("ones", [P, P])
        par = sb("par", [P, NPAR])
        hpar = sb("hpar", [SH, 4])
        small = sb("small", [P, 32])
        csil = sb("csil", [P, KD])
        mod = sb("mod", [P, 48])
        gmod = sb("gmod", [P, 4, KD])
        epsc = sb("epsc", [P, 1])
        ms, root, rt = small[:, 0:4], small[:, 4:8], small[:, 8:12]
        arena = base[0]

        def at(kb):
            return arena + int(kb * 1024)

        xhi = sb("xhi", [P, KD, S], F32R, at(0))
        xlo = sb("xlo", [P, KD, S], F32R, at(16))
        m_x = sb("m_x", [P, KD, S], F32, at(0))
        hid_hi = sb("hid_hi", [P, KF, S], F32R, at(32))
        hid_lo = sb("hid_lo", [P, KF, S], F32R, at(76))
        UP = 516
        upad = sb("upad", [P, 2, UP], F32, at(120))
        sg = sb("sg", [P, S], F32, at(124.125))
        hid = sb("hid", [P, S], F32, at(126.125))
        qkv = sb("qkv", [P, 16, S], F32, at(32))
        m_alt = sb("m_alt", [P, KD, S], F32, at(32))
        vtok = sb("vtok", [P, NT, S], F32, at(64))
        swp = sb("swp", [P, 4, S], F32, at(72))
        flat = sb("flat", [P, 16, 4, NC], F32, at(80))
        w1st = sb("w1st", [P, 16, 256], F32, at(88))
        pbuf = sb("pbuf", [P, 4, 2, S], F32, at(80))
        pt = sb("pt", [P, 2, 2, S], F32, at(96))
        hg = sb("hg", [P, 2, 4 * NC], F32, at(104))
        kct = sb("kct", [P, 2, NC], F32, at(105))
        vct = sb("vct", [NC, 4, HD], F32, at(105.5))
        pcmp = sb("pcmp", [P, 4, 32], F32, at(106.5))
        ptc = sb("ptc", [NC, 2, P], F32, at(107))
        gt = sb("gt", [48, S], F32, at(108))
        qst = sb("qst", [P, S], F32, at(108))
        gtok = sb("gtok", [P, NT, 48], F32, at(110))
        mbig = sb("mbig", [P, S], F32, at(111))
        mcmp = sb("mcmp", [P, NT, NC], F32, at(113))
        stat = sb("stat", [P, 4, 32], F32, at(123.25))
        ada_acc = sb("ada_acc", [P, ADA_SLICE], F32, at(114))
        ada_w = sb("ada_w", [P, 2, ADA_SLICE], F32, at(117))
        rowok = sb("rowok", [P, 1], F32, at(123))
        cv = sb("cv", [P, CH, S], F32, at(32))
        zb = sb("zb", [P, NZ, S], F32, at(80))
        yhi = sb("yhi", [P, NZ, S], F32R, at(48))
        ylo = sb("ylo", [P, NZ, S], F32R, at(16))
        xdt = sb("xdt", [P, SH, HD], F32, at(0))
        xdec = sb("xdec", [P, SH, HD], F32, at(8))
        state = sb("state", [P, SH, HD], F32, at(16))
        btok = sb("btok", [P, 4, P], F32, at(24))
        ebuf = sb("ebuf", [P, 2, S], F32, at(26))
        usum = sb("usum", [P, P], F32, at(30))
        smask = sb("smask", [P, P], F32, at(30.5))
        cbuf = sb("cbuf", [P, 2, P], F32, at(31))
        xbuf = sb("xbuf", [P, 4, S], F32, at(112))
        spad = sb("spad", [P, UP], F32, at(116))
        cacc = sb("cacc", [P, 2, S], F32, at(118.25))
        dtt = sb("dtt", [SH, 2, S], F32, at(122.25))
        dtk = sb("dtk", [P, NT, 2, SH], F32, at(126.25))
        acs = sb("acs", [P, 3, NT, SH], F32, at(122.25))
        gst = sb("gst", [P, 3, 4 * NT], F32, at(124))
        dw = sb("dw", [SH, 5, S], F32, at(0))
        cc = sb("cc", [P, KD, S], F32, at(32))
        cy = sb("cy", [P, KD, S], F32, at(48))
        yc_hi = sb("yc_hi", [P, KD, S], F32R, at(64))
        yc_lo = sb("yc_lo", [P, KD, S], F32R, at(80))
        m_conv = sb("m_conv", [P, KD, S], F32, at(96))
        cpad = sb("cpad", [P, UP], F32, at(112))
        cyt = sb("cyt", [P, 2, S], F32, at(115))

        bank = [ctx.enter_context(nc.psum_tensor(f"bank{k}", [P, 512], F32)) for k in range(8)]
        stat_ps, bc_ps = bank[5], bank[4]

        s_raw = [sem(f"raw_landed{k}") for k in range(4)]
        s_in = sem("inputs_landed")
        s_const = sem("constants_made")
        s_carry = [sem(f"waits_taken_{e}") for e in ("sp", "dve", "pool")]
        s_hi = sem("weight_hi_made")
        s_lo = sem("weight_lo_made")
        s_pe = sem("panels_multiplied")
        s_ev = sem("in_tiles_taken")
        s_m = sem("out_tiles_taken")
        s_xh = sem("operand_hi_made")
        s_xt = sem("operand_lo_made")
        s_h = sem("residual_updated")
        s_sa = sem("squares_made")
        s_pa = sem("squares_added")
        s_sq = sem("square_sums_made")
        s_stat = sem("token_sums_made")
        s_ms = sem("mean_squares_made")
        s_sqrt = sem("roots_made")
        s_rt = sem("token_rstd_made")
        s_last = sem("last_squares_made")
        s_add = sem("updates_scaled")
        s_bc = sem("rstd_spread")
        s_rb = sem("rstd_kept")
        s_dve = sem("dve_chain")
        s_act = sem("act_chain")
        s_pool = sem("pool_chain")
        s_tap = sem("first_taps_made")
        s_cg = sem("gates_convolved")
        s_sg = sem("gates_silu")
        s_hid = sem("hidden_made")
        s_gate = sem("gates_sigmoid")
        s_gtp = sem("gates_turned")
        s_v = sem("v_panels_taken")
        s_swp = sem("halves_swapped")
        s_w1 = sem("compress_w1_landed")
        s_flat = sem("blocks_flattened")
        s_cm = sem("compress_matmuls")
        s_gelu = sem("compress_gelu")
        s_kv = sem("compressed_kept")
        s_qst = sem("q_staged")
        s_S = sem("scores_made")
        s_sc = sem("scores_masked")
        s_nb = sem("negative_max_made")
        s_e = sem("exps_made")
        s_P = sem("probs_scaled")
        s_T = sem("probs_turned")
        s_tv = sem("turned_kept_dve")
        s_ta = sem("turned_kept_act")
        s_pv = sem("pv_made")
        s_oh = sem("output_halves_hi")
        s_ol = sem("output_halves_taken")
        s_mod = sem("modulation_kept")
        s_ada_w = [sem(f"ada_w_landed{k}") for k in range(2)]
        s_ada = sem("ada_slices_summed")
        s_adap = sem("ada_slices_spread")
        s_csil = sem("c_silu")
        s_cacc = sem("conv_sums_made")
        s_cv = sem("conv_silu_made")
        s_dt = sem("dt_steps")
        s_dta = sem("dt_act_steps")
        s_dtp = sem("dt_turned")
        s_dtk = sem("dt_kept")
        s_xtp = sem("x_turned")
        s_xd = sem("x_dt_made")
        s_bt = sem("b_kept")
        s_ac = sem("cumsums_made")
        s_acv = sem("cumsums_kept")
        s_dec = sem("decays_made")
        s_xdec = sem("x_decayed")
        s_cb = sem("cb_made")
        s_cbk = sem("cb_kept")
        s_lb = sem("cumsums_spread")
        s_ein = sem("segments_made")
        s_ee = sem("segment_exps")
        s_xe = sem("spread_exps")
        s_w = sem("ssd_weights_made")
        s_cx = sem("c_scaled")
        s_y = sem("y_made")
        s_gq = sem("group_squares_made")
        s_gs = sem("group_sums_made")
        s_gn = sem("group_norm_steps")
        s_gr = sem("group_roots_made")
        s_gb = sem("group_rstd_spread")
        s_yk = sem("y_kept")
        s_st = sem("state_products")
        s_stk = sem("state_kept")
        s_out = sem("out_stored")

        def col(name, k=0, rows=P):
            c = COL[name] + k
            return par[0:rows, c:c + 1]

        block = ctx.enter_context(nc.Block())

        def segs(U):
            return (ebuf, sqr)[U // 2 % 2][:, U % 2, :]

        def psum_ap(t):
            return bank[t][:, :]

        @block.sync
        def _(sp):
            sp.dma_start(h[:, 0:4, :], xT[:, 0:4, :]).then_inc(s_in, 16)
            sp.dma_start(h[:, 4:8, :], xT[:, 4:8, :]).then_inc(s_in, 16)
            sp.dma_start(par[:, :], params).then_inc(s_in, 16)
            sp.dma_start(hpar[:, 0:2], heads).then_inc(s_in, 16)

            def load(name, c, i):
                g = START[name] + c
                nb = BLOCKS[name]
                if g >= 4 or not static(i):
                    sp.wait_ge(s_raw[g % 4], 16 * (g // 4) + 16 * i)
                    if not static(i):
                        sp.sem_inc(s_carry[0], 1)
                    sp.wait_ge(s_lo, g - 3 + 4 * i)
                    if not static(i):
                        sp.sem_inc(s_carry[0], 1)
                src = (w8 if nb == 8 else w11)[DRAM_AT[name] + c + 4 * i]
                sp.dma_start(raw[g % 4][:, 0:nb * P], src).then_inc(s_raw[g % 4], 16)

            for name, n, _, _ in PHASES:
                walk(sp, n, lambda c, i: load(name, c, i))
            sp.wait_ge(s_out, 16 * 8)

        @block.gpsimd
        def _(pool):
            chain = Chain(pool, s_pool)
            chain(pool.memset(ident[:, :], 0.0))
            chain(pool.memset(ones[:, :], 1.0))
            chain(pool.memset(epsc[:, :], EPS))
            chain(pool.memset(mbig[:, :], 0.0))
            chain(pool.memset(mcmp[:, :, :], 0.0))
            chain(pool.memset(rowok[:, :], 1.0))
            chain.wait()
            chain(pool.affine_select(out=ident[:, :], in_=ident[:, :], compare_op=ALU.not_equal, fill=1.0,
                                     base=0, pattern=[[-1, P]], channel_multiplier=1))
            chain(pool.affine_select(out=mbig[:, :], in_=mbig[:, :], compare_op=ALU.is_ge, fill=NEG,
                                     base=S - P, pattern=[[-1, S]], channel_multiplier=1))
            chain(pool.affine_select(out=mcmp[:, :, :], in_=mcmp[:, :, :], compare_op=ALU.is_ge, fill=NEG,
                                     base=-31, pattern=[[P, NT], [-16, NC]], channel_multiplier=1))
            chain(pool.affine_select(out=rowok[:, :], in_=rowok[:, :], compare_op=ALU.is_ge, fill=0.0,
                                     base=-31, pattern=[[0, 1]], channel_multiplier=1))
            chain.wait()
            pool.memset(small[:, 31:32], 0.0).then_inc(s_const, 1)

            squared, added = [0], [0]

            def add_squares():
                for j in range(1, KD):
                    pool.wait_ge(s_sa, squared[0] + j + 1)
                    if added[0] and j > 1:
                        pool.wait_ge(s_pa, added[0])
                    first = sqr[:, 0, :] if j == 1 else ssum[:, :]
                    pool.tensor_tensor(ssum[:, :], first, sqr[:, j % 2, :], ALU.add).then_inc(s_pa, 1)
                    added[0] += 1
                pool.wait_ge(s_pa, added[0])
                pool.memset(small[:, 31:32], 0.0).then_inc(s_sq, 1)
                squared[0] += KD

            def add_update(scaled_before):
                for j in range(KD):
                    pool.wait_ge(s_add, scaled_before + j + 1)
                    pool.tensor_tensor(h[:, j, :], tmp[:, j % 2, :], h[:, j, :], ALU.add).then_inc(s_h, 1)
                squared[0] += KD
                added[0] += KD - 1

            add_squares()

            def ada_load(k, s):
                pool.dma_start(ada_w[:, k % 2, :], w_ada[s, k]).then_inc(s_ada_w[k % 2], 16)

            pool.wait_ge(s_csil, 1)
            before = chain.n
            per = 2 * KD - 1
            with pool.Fori(0, ADA_SLICES) as s:
                chain.off = s * per
                chain.wait()
                ada_load(0, s)
                ada_load(1, s)
                for k in range(KD):
                    pool.wait_ge(s_ada_w[k % 2], 16 * (k // 2 + 1) + 16 * (KD // 2) * s)
                    pool.sem_inc(s_carry[2], 1)
                    if k == 0:
                        done = chain(pool.tensor_scalar(ada_acc[:, :], ada_w[:, 0, :], csil[:, 0:1], 1.0,
                                                        ALU.mult, ALU.mult))
                    else:
                        chain(pool.tensor_scalar(ada_w[:, k % 2, :], ada_w[:, k % 2, :], csil[:, k:k + 1], 1.0,
                                                 ALU.mult, ALU.mult))
                        chain.wait()
                        ins = pool.tensor_tensor(ada_acc[:, :], ada_acc[:, :], ada_w[:, k % 2, :], ALU.add)
                        if k < KD - 1:
                            done = chain(ins)
                        else:
                            ins.then_inc(s_ada, 1)
                            pool.wait_ge(s_ada, s + 1)
                            pool.sem_inc(s_carry[2], 1)
                            chain(pool.memset(small[:, 31:32], 0.0))
                    if k + 2 < KD:
                        pool.wait_ge(s_pool, done)
                        ada_load(k + 2, s)
                pool.wait_ge(s_adap, s + 1)
            assert chain.n - before == per, (chain.n - before, per)
            chain.n = before + per * ADA_SLICES
            chain.off = 0

            add_update(0)
            add_update(KD)

            pool.wait_ge(s_pe, START["SSD_IN"] + 41)
            chain(pool.memset(usum[:, :], 1.0))
            chain(pool.memset(smask[:, :], 0.0))
            chain.wait()
            chain(pool.affine_select(out=usum[:, :], in_=usum[:, :], compare_op=ALU.is_ge, fill=0.0,
                                     base=0, pattern=[[1, P]], channel_multiplier=-1))
            chain(pool.affine_select(out=smask[:, :], in_=smask[:, :], compare_op=ALU.is_ge, fill=NEG,
                                     base=0, pattern=[[1, P]], channel_multiplier=-1))
            chain.wait()
            pool.memset(small[:, 31:32], 0.0).then_inc(s_const, 1)

            for c in range(NT):
                tok = slice(c * P, (c + 1) * P)
                for g in range(4):
                    for u in (2 * g, 2 * g + 1) if c else ():
                        pool.wait_ge(s_xe, 8 * (c - 1) + u + 1)
                        b = xbuf[:, u % 4, :].rearrange("p (a l) -> p a l", a=4)
                        pool.tensor_tensor(b, b, cv[:, 4 + g, tok].unsqueeze(1).to_broadcast([P, 4, P]),
                                           ALU.mult).then_inc(s_cx, 1)
                    if c < NT - 1:
                        pool.wait_ge(s_xd, 4 * c + g + 1)
                        pool.wait_ge(s_dec, 1)
                        if c > 0:
                            pool.wait_ge(s_st, 4 * (c - 1) + g + 1)
                        hs = slice(8 * g, 8 * g + 8)
                        pool.tensor_tensor(xdec[:, hs, :], xdt[:, hs, :],
                                           acs[:, 1, c, hs].unsqueeze(2).to_broadcast([P, 8, HD]),
                                           ALU.mult).then_inc(s_xdec, 1)
            add_update(2 * KD)
            add_squares()
            add_squares()

        @block.tensor
        def _(pe):
            def token_sums(src, first, last):
                for t in range(NT):
                    mm = pe.matmul(stat_ps[:, t:t + 1], src[:, t * P:(t + 1) * P], ones[:, 0:1],
                                   start=first and t == 0, stop=last, skip_group_check=True)
                return mm

            def stats_a(q):
                pe.wait_ge(s_sq, q + 1)
                if q in LAST:
                    pe.wait_ge(s_last, LAST[q])
                    token_sums(sqr[:, 0, :], False, True).then_inc(s_stat, 1)
                    return
                if q:
                    pe.wait_ge(s_ms, q)
                token_sums(ssum, True, True).then_inc(s_stat, 1)

            def stats_b(q):
                pe.wait_ge(s_rt, q + 1)
                for t in range(NT):
                    mm = pe.matmul(bc_ps[:, t * P:(t + 1) * P], rt[:, t:t + 1].to_broadcast([P, P]), ident[:, :],
                                   start=True, stop=True)
                mm.then_inc(s_bc, 1)

            def gemm(name, hi, lo, taken, taken_at, q=None, panels=None, others=(), post=None):
                st, nb, per = START[name], BLOCKS[name], PER_TILE[name]
                n = panels or COUNT[name]
                nbank = 4 if per == 1 else 2
                for s_, v in others:
                    pe.wait_ge(s_, v)

                def weights(c, i):
                    pe.wait_ge(s_lo, st + c + 1 + 4 * i)

                def bank_free(c, i):
                    t = c // per
                    if not static(i) or t >= nbank:
                        pe.wait_ge(taken, taken_at + t - nbank + 1 + (4 // per) * i)

                def block_of(c, kb, bk):
                    w = (st + c) % 2
                    k = kb + nb * (c % per)
                    first, last = k == 0, k == nb * per - 1
                    cols = slice(kb * P, (kb + 1) * P)
                    pe.matmul(bk, whi[w][:, cols], hi[:, k, :], start=first, stop=False)
                    pe.matmul(bk, whi[w][:, cols], lo[:, k, :], start=False, stop=False)
                    return pe.matmul(bk, wlo[w][:, cols], hi[:, k, :], start=False, stop=last)

                def step(c, i):
                    bk = psum_ap((c // per) % nbank)
                    if c in (0, 1) and static(i) and per == 1:
                        if c == 0:
                            weights(1, 0)
                            for kb in range(nb):
                                pe.wait_ge(s_xt, XT[name] + kb + 1)
                                for cc_ in (0, 1):
                                    mm = block_of(cc_, kb, psum_ap(cc_))
                                    if kb == nb - 1:
                                        mm.then_inc(s_pe, 1)
                            if q is not None:
                                stats_a(q)
                        return
                    weights(c, i)
                    if c % per == 0:
                        bank_free(c, i)
                    for kb in range(nb):
                        if post is not None and static(i) and c == n - 1 and kb == nb // 2:
                            pe.wait_ge(s_sq, post + 1)
                            pe.wait_ge(s_ms, post)
                            token_sums(ssum, True, False)
                        if static(i) and c < per:
                            pe.wait_ge(s_xt, XT[name] + kb + nb * c + 1)
                        mm = block_of(c, kb, bk)
                    mm.then_inc(s_pe, 1)
                    if static(i) and c == 2 and q is not None:
                        stats_b(q)

                walk(pe, n, step)

            pe.wait_ge(s_const, 1)
            pe.wait_ge(s_in, 64)
            gemm("NSA_IN", xhi, xlo, s_ev, EV["NSA_IN"], Q_NSA_PRE, panels=17)
            pe.wait_ge(s_rb, 1)
            for c in range(17, 21):
                pe.wait_ge(s_lo, START["NSA_IN"] + c + 1)
                w = (START["NSA_IN"] + c) % 2
                for kk in range(2):
                    k = 2 * (c - 17) + kk
                    cols = slice(kk * S, (kk + 1) * S)
                    for t in range(NT):
                        tk = slice(t * P, (t + 1) * P)
                        bk = bank[4 + t][:, :]
                        pe.matmul(bk, xhi[:, k, tk], whi[w][:, cols], start=k == 0, stop=False)
                        pe.matmul(bk, xhi[:, k, tk], wlo[w][:, cols], start=False, stop=False)
                        mm = pe.matmul(bk, xlo[:, k, tk], whi[w][:, cols], start=False, stop=k == KD - 1)
                mm.then_inc(s_pe, 1)
            pe.wait_ge(s_gate, 1)
            pe.wait_ge(s_ev, 17)
            for t in range(NT):
                mm = pe.transpose(bank[1][:, t * 48:(t + 1) * 48], gt[:, t * P:(t + 1) * P], ident[0:48, 0:48])
            mm.then_inc(s_gtp, 1)
            for kv in range(2):
                pe.wait_ge(s_w1, 16 * (kv + 1))
                pe.wait_ge(s_flat, kv + 1)
                if kv:
                    pe.wait_ge(s_gelu, 1)
                for hh in range(2):
                    for m in range(16):
                        mm = pe.matmul(bank[0][:, hh * P:hh * P + 4 * NC], w1st[:, m, hh * P:(hh + 1) * P],
                                       flat[:, m, :, :].rearrange("p g c -> p (g c)"), start=m == 0, stop=m == 15)
                mm.then_inc(s_cm, 1)
                pe.wait_ge(s_gelu, kv + 1)
                w2 = par[:, COL["w2"] + kv * P:COL["w2"] + (kv + 1) * P].rearrange("p (a d) -> p a d", a=2)
                for g in range(4):
                    cs = slice(g * NC, (g + 1) * NC)
                    for hh in range(2):
                        if kv == 0:
                            o = bank[2][(g % 2) * HD:(g % 2 + 1) * HD, (g // 2) * NC:(g // 2 + 1) * NC]
                            mm = pe.matmul(o, w2[:, hh, :], hg[:, hh, cs], start=hh == 0, stop=hh == 1)
                        else:
                            o = bank[3][0:NC, g * HD:(g + 1) * HD]
                            mm = pe.matmul(o, hg[:, hh, cs], w2[:, hh, :], start=hh == 0, stop=hh == 1)
                mm.then_inc(s_cm, 1)

            pe.wait_ge(s_kv, 2)
            pe.wait_ge(s_v, 1)
            pe.wait_ge(s_gtp, 1)
            def scores(u, j, t):
                qt, a, U = u // 2, u % 2, u + 8 * t
                rows = slice(a * HD, (a + 1) * HD)
                n = (qt + 1) * P
                q_ = qst[rows, qt * P:(qt + 1) * P]
                if u == 0:
                    pe.wait_ge(s_qst, 1 + t)
                if some(U):
                    pe.wait_ge(s_sc, U)
                if u == 7:
                    spread_ada(t)
                pe.matmul(bank[0][:, 0:n], q_, qkv[rows, 12 + j, 0:n], start=True, stop=True)
                pe.matmul(bank[1][:, 0:n], q_, qkv[rows, 14 + j, 0:n], start=True, stop=True)
                if u == 7:
                    pe.wait_ge(s_mod, 1 + t)
                pe.matmul(bank[2][:, 0:NC], q_, kct[rows, j, :], start=True, stop=True).then_inc(s_S, 1)

            def turn(u, j, t):
                qt, U = u // 2, u + 8 * t
                pe.wait_ge(s_P, 1 + U)
                if some(U):
                    pe.wait_ge(s_tv, U)
                    pe.wait_ge(s_ta, U)
                for r in range(2):
                    for kb in range(qt + 1):
                        ks = slice(kb * P, (kb + 1) * P)
                        pe.transpose(bank[3 + r][:, ks], pbuf[:, u % 4, r, ks], ident[:, :])
                pe.transpose(bank[5][0:NC, 0:P], pcmp[:, u % 4, 0:NC], ident[:, :]).then_inc(s_T, 1)

            def pv(u, j, t):
                qt, a, U = u // 2, u % 2, u + 8 * t
                o = bank[6 + qt // 2][a * HD:(a + 1) * HD, (qt % 2) * P:(qt % 2 + 1) * P]
                pe.wait_ge(s_tv, 1 + U)
                pe.wait_ge(s_ta, 1 + U)
                if u == 0 and some(t):
                    pe.wait_ge(s_ol, t)
                if u == 4 and some(t):
                    pe.wait_ge(s_xt, XT["NSA_OUT"] + t)
                g = 2 * j + a
                for r in range(2):
                    for kb in range(qt + 1):
                        pe.matmul(o, vtok[:, kb, r * 256 + g * HD:r * 256 + (g + 1) * HD],
                                  pt[:, u % 2, r, kb * P:(kb + 1) * P], start=r == 0 and kb == 0, stop=False,
                                  skip_group_check=True)
                pe.matmul(o, vct[:, g, :], ptc[:, u % 2, :], start=False, stop=True,
                          skip_group_check=True).then_inc(s_pv, 1)

            def spread_ada(t):
                pe.wait_ge(s_ada, 1 + t)
                for f in range(ADA_SLICE // P):
                    mm = pe.matmul(bank[2][:, 256 + f:257 + f], ada_acc[:, f * P:(f + 1) * P], ones[:, 0:1],
                                   start=True, stop=True)
                mm.then_inc(s_adap, 1)

            def tile(t, j, jp):
                for k in range(8 if j is not None else 3):
                    for stage, lag in ((scores, 0), (turn, 2), (pv, 3)):
                        at_ = unit(k, lag, t, j, jp)
                        if at_:
                            stage(*at_)
            tiles_of_q(pe, tile)

            outs = [(s_ev, EV["UP1"]), (s_sc, 64), (s_tv, 64), (s_ta, 64), (s_mod, 8)]
            gemm("NSA_OUT", xhi, xlo, s_m, MV["NSA_OUT"], others=outs + [(s_ol, 8)], post=Q_NSA_POST)
            stats_a(Q_NSA_POST)
            stats_b(Q_NSA_POST)
            gemm("UP1", xhi, xlo, s_ev, EV["UP1"], Q_F1_PRE, others=[(s_m, 8)])
            gemm("DOWN1", hid_hi, hid_lo, s_m, MV["DOWN1"], others=[(s_ev, EV["SSD_IN"])], post=Q_F1_POST)
            stats_a(Q_F1_POST)
            stats_b(Q_F1_POST)
            gemm("SSD_IN", xhi, xlo, s_ev, EV["SSD_IN"], Q_SSD_PRE, others=[(s_m, 16)])
            pe.wait_ge(s_dt, 8)
            pe.wait_ge(s_rb, KEPT[Q_SSD_PRE])
            for t in range(NT):
                for r in range(2):
                    mm = pe.transpose(bank[5][:, (2 * t + r) * SH:(2 * t + r + 1) * SH],
                                      dtt[:, r, t * P:(t + 1) * P], ident[0:SH, 0:SH])
            mm.then_inc(s_dtp, 1)
            pe.wait_ge(s_const, 2)
            pe.wait_ge(s_cv, 40)
            pe.wait_ge(s_ev, EV["UP2"])
            pe.wait_ge(s_dtk, 1)
            for c in range(NT):
                dta = dtk[:, c, 1, :]
                pe.matmul(bank[5][:, c * SH:(c + 1) * SH], usum[:, :], dta, start=True, stop=True)
                mm = pe.matmul(bank[5][:, (NT + c) * SH:(NT + c + 1) * SH], ones[:, :], dta, start=True, stop=True)
            mm.then_inc(s_ac, 1)

            def turn_x(c, k):
                if c and k < 2:
                    pe.wait_ge(s_ein, 8 * c - 1 + k)
                    if c > 1:
                        pe.wait_ge(s_xe, 8 * (c - 1) - 1 + k)
                elif c:
                    pe.wait_ge(s_yk, 4 * (c - 1) + k + 1)
                for r in range(4):
                    mm = pe.transpose(bank[k][:, r * P:(r + 1) * P],
                                      cv[:, 8 + 4 * k + r, c * P:(c + 1) * P], ident[:, :])
                mm.then_inc(s_xtp, 1)

            def turn_b(c):
                if c:
                    pe.wait_ge(s_bt, c)
                for g in range(4):
                    mm = pe.transpose(bank[4][:, g * P:(g + 1) * P], cv[:, g, c * P:(c + 1) * P], ident[:, :])
                mm.then_inc(s_xtp, 1)

            def spread(G):
                c, g = G // 4, G % 4
                tok = slice(c * P, (c + 1) * P)
                if G:
                    pe.wait_ge(s_cbk, G)
                pe.matmul(bank[6][:, 0:P], cv[:, g, tok], cv[:, 4 + g, tok], start=True, stop=True)\
                    .then_inc(s_cb, 1)
                for v in range(2):
                    U = 2 * G + v
                    if g == 0:
                        pe.wait_ge(s_xd, 4 * c + v + 1)
                    if U >= 2:
                        pe.wait_ge(s_ein, U - 1)
                    if c and U - 8 >= 2:
                        pe.wait_ge(s_xe, U - 8 - 1)
                    for k in range(4):
                        hd = 8 * g + 4 * v + k
                        mm = pe.matmul(bank[v][:, k * P:(k + 1) * P],
                                       dtk[:, c, 1, hd:hd + 1].to_broadcast([P, P]), usum[:, :],
                                       start=True, stop=True)
                    mm.then_inc(s_lb, 1)

            def outputs(G):
                c, g = G // 4, G % 4
                yb = 2 + g % 2
                pe.wait_ge(s_xd, 4 * c + min(3 + g, 4))
                if G >= 2:
                    pe.wait_ge(s_yk, G - 1)
                for v in range(2):
                    U = 2 * G + v
                    pe.wait_ge(s_w, U + 1)
                    if c:
                        pe.wait_ge(s_cx, U - 8 + 1)
                        pe.wait_ge(s_stk, 4 * (c - 1) + g + 1)
                    for k in range(4):
                        hd = 8 * g + 4 * v + k
                        o = bank[yb][(hd % 2) * HD:(hd % 2 + 1) * HD, (hd // 2 % 4) * P:(hd // 2 % 4 + 1) * P]
                        mm = pe.matmul(o, xdt[:, hd, :], segs(U)[:, k * P:(k + 1) * P],
                                       start=True, stop=c == 0, skip_group_check=True)
                        if c:
                            mm = pe.matmul(o, state[:, hd, :], xbuf[:, U % 4, k * P:(k + 1) * P],
                                           start=False, stop=True, skip_group_check=True)
                    mm.then_inc(s_y, 1)

            def states(G):
                c, g = G // 4, G % 4
                pe.wait_ge(s_xdec, G + 1)
                if G:
                    pe.wait_ge(s_stk, G)
                pe.wait_ge(s_bt, c + 1)
                pe.matmul(bank[7][:, :], btok[:, g, :],
                          xdec[:, 8 * g:8 * g + 8, :].rearrange("p h d -> p (h d)"),
                          start=True, stop=True).then_inc(s_st, 1)

            def group_sums(G):
                c, g = G // 4, G % 4
                pe.wait_ge(s_gq, G + 1)
                if G == 0:
                    pe.wait_ge(s_acv, 1)
                for r in range(4):
                    mm = pe.matmul(stat_ps[:, 4 * g + c:4 * g + c + 1], tmp[:, 1, r * P:(r + 1) * P], ones[:, 0:1],
                                   start=r == 0, stop=r == 3)
                mm.then_inc(s_gs, 1)

            for k in range(4):
                turn_x(0, k)
            turn_b(0)
            spread(0)
            for G in range(4 * NT):
                c, g = G // 4, G % 4
                if g < 3:
                    spread(G + 1)
                elif c < NT - 1:
                    turn_x(c + 1, 0)
                    turn_x(c + 1, 1)
                outputs(G)
                if g == 3 and c < NT - 1:
                    spread(G + 1)
                if c < NT - 1:
                    states(G)
                    if g == 3:
                        turn_x(c + 1, 2)
                        turn_x(c + 1, 3)
                        if c + 1 < NT - 1:
                            turn_b(c + 1)
                if G >= 2:
                    group_sums(G - 2)
            group_sums(4 * NT - 2)
            group_sums(4 * NT - 1)
            pe.wait_ge(s_gn, 2)
            pe.wait_ge(s_yk, 4 * NT)
            for g in range(4):
                for t in range(NT):
                    mm = pe.matmul(bank[2 + g if g < 3 else 6][:, t * P:(t + 1) * P],
                                   gst[:, 2, 4 * g + t:4 * g + t + 1].to_broadcast([P, P]), ident[:, :],
                                   start=True, stop=True)
                mm.then_inc(s_gb, 1)
            gemm("SSD_OUT", yhi, ylo, s_m, MV["SSD_OUT"], others=[(s_yk, 16)], post=Q_SSD_POST)
            stats_a(Q_SSD_POST)
            stats_b(Q_SSD_POST)
            gemm("UP2", xhi, xlo, s_ev, EV["UP2"], Q_F2_PRE, others=[(s_m, 24)])
            gemm("DOWN2", hid_hi, hid_lo, s_m, MV["DOWN2"], others=[(s_ev, EV["CONV_IN"])], post=Q_F2_POST)
            stats_a(Q_F2_POST)
            stats_b(Q_F2_POST)
            stats_a(Q_CONV_PRE)
            stats_b(Q_CONV_PRE)
            gemm("CONV_IN", xhi, xlo, s_ev, EV["CONV_IN"], others=[(s_m, 32)])
            gemm("CONV_OUT", yc_hi, yc_lo, s_m, MV["CONV_OUT"], others=[(s_ev, EV["UP3"])], post=Q_CONV_POST)
            stats_a(Q_CONV_POST)
            stats_b(Q_CONV_POST)
            stats_a(Q_F3_PRE)
            stats_b(Q_F3_PRE)
            gemm("UP3", xhi, xlo, s_ev, EV["UP3"], others=[(s_m, 40)])
            gemm("DOWN3", hid_hi, hid_lo, s_m, MV["DOWN3"], others=[(s_ev, EV["UP3"] + 44)], post=Q_F3_POST)
            stats_a(Q_F3_POST)
            stats_b(Q_F3_POST)

        @block.scalar
        def _(act):
            chain = Chain(act, s_act)

            def weight_hi(g, i):
                if g >= TOTAL:
                    return
                n = PANEL_BLOCKS[g] * P
                act.wait_ge(s_raw[g % 4], 16 * (g // 4 + 1) + 16 * i)
                if g >= 2:
                    act.wait_ge(s_pe, g - 1 + 4 * i)
                act.activation(whi[g % 2][:, 0:n], raw[g % 4][:, 0:n], ACT.Copy).then_inc(s_hi, 1)

            def stats_root(q):
                act.wait_ge(s_ms, q + 1)
                act.activation(root, ms, ACT.Sqrt).then_inc(s_sqrt, 1)

            def stats_keep(q):
                act.wait_ge(s_bc, q + 1)
                act.activation(rstd_b[:, :], bc_ps[:, :], ACT.Copy).then_inc(s_rb, 1)

            added = [0]

            def square(src, j, n):
                need = added[0] + (max(1, j - 2) if j >= 2 else 0)
                if need:
                    act.wait_ge(s_pa, need)
                act.activation(sqr[:, j % 2, :], src, ACT.Square).then_inc(s_sa, 1)
                if j == n - 1:
                    added[0] += n - 1

            def project_in(name, post, q=None, panels=None):
                st = START[name]

                def step(c, i):
                    weight_hi(st + c + 2, i)
                    if q is not None and static(i) and c == 0:
                        stats_root(q)
                        return
                    if q is not None and static(i) and c == 1:
                        stats_keep(q)
                        post(0, 0)
                    post(c, i)
                walk(act, COUNT[name], step)

            def project_out(name, m, q):
                st, per, n = START[name], PER_TILE[name], COUNT[name]

                def step(c, i):
                    if static(i) and c == n - 1:
                        act.wait_ge(s_pe, st + n)
                        act.activation(sqr[:, 0, :], psum_ap(3 if per == 1 else 1), ACT.Square).then_inc(s_last, 1)
                        act.activation(m[:, KD - 1, :], psum_ap(3 if per == 1 else 1), ACT.Copy).then_inc(s_m, 1)
                        stats_root(q)
                        weight_hi(st + n + 1, 0)
                        return
                    weight_hi(st + c + 2, i)
                    if c % per == per - 1:
                        t = c // per
                        act.wait_ge(s_pe, st + c + 1 + 4 * i)
                        act.activation(m[:, t + (4 // per) * i, :], psum_ap(t % (4 if per == 1 else 2)), ACT.Copy)\
                            .then_inc(s_m, 1)
                walk(act, COUNT[name], step)

            def operands(name, gain, updated):
                for j in range(KD):
                    if updated is not None:
                        act.wait_ge(s_h, updated + j + 1)
                    act.activation(xhi[:, j, :], h[:, j, :], ACT.Copy, scale=gain(j)).then_inc(s_xh, 1)
                for j in range(KD):
                    square(h[:, j, :], j, KD)

            def ffn_up(name, layer, hidden_before, q):
                st, ev = START[name], EV[name]

                def first_tap(c, i):
                    k = layer * 44 + c + 4 * i
                    act.wait_ge(s_ev, ev + c + 1 + 4 * i)
                    act.activation(tmp[:, c % 2, :], upad[:, c % 2, 2:2 + S], ACT.Identity,
                                   scale=par[:, bass.ds(COL["ffn_w"] + 3 * k + 2, 1)],
                                   bias=par[:, bass.ds(COL["ffn_b"] + k, 1)]).then_inc(s_tap, 1)

                def post(c, i):
                    t = c // 2 + 2 * i
                    if c % 2 == 0:
                        act.wait_ge(s_cg, layer * KF + t + 1)
                        act.activation(sg[:, :], tmp[:, 0, :], ACT.Silu).then_inc(s_sg, 1)
                    else:
                        act.wait_ge(s_hid, hidden_before + t + 1)
                        act.activation(hid_hi[:, c // 2 + 2 * i, :], hid[:, :], ACT.Copy).then_inc(s_xh, 1)

                def step(c, i):
                    weight_hi(st + c + 2, i)
                    if static(i) and c == 0:
                        stats_root(q)
                        return
                    if static(i) and c == 1:
                        stats_keep(q)
                        first_tap(0, 0)
                    first_tap(c, i)
                    post(c - 1, i)
                walk(act, 44, step)
                post(43, 0)

            act.wait_ge(s_in, 64)
            act.wait_ge(s_const, 1)
            weight_hi(0, 0)
            weight_hi(1, 0)
            operands("NSA_IN", lambda j: col("gains", j), None)
            chain(act.activation(csil[:, :], par[:, COL["c"]:COL["c"] + KD], ACT.Silu))
            chain.wait()
            act.activation(csil[:, 0:1], csil[:, 0:1], ACT.Copy).then_inc(s_csil, 1)

            def nsa_post(c, i):
                if static(i) and c == 16:
                    act.wait_ge(s_ev, 12)
                    act.dma_start(swp[0:HD, :, :], qkv[HD:P, 8:12, :]).then_inc(s_swp, 16)
                    act.dma_start(swp[HD:P, :, :], qkv[0:HD, 8:12, :]).then_inc(s_swp, 16)
                    act.dma_start(w1st[:, :, :], w_cmp[0]).then_inc(s_w1, 16)
                if static(i) and c == 16:
                    act.wait_ge(s_ev, 17)
                    chain(act.activation(gt[:, :], gt[:, :], ACT.Sigmoid))
                    chain.wait()
                    act.activation(gt[0:1, 0:1], gt[0:1, 0:1], ACT.Copy).then_inc(s_gate, 1)

            project_in("NSA_IN", nsa_post, Q_NSA_PRE)
            for kv in range(2):
                act.wait_ge(s_cm, 2 * kv + 1)
                if kv == 0:
                    act.dma_start(w1st[:, :, :], w_cmp[1]).then_inc(s_w1, 16)
                else:
                    act.wait_ge(s_cm, 2)
                act.activation(hg[:, :, :], bank[0][:, 0:2 * P].rearrange("p (a c) -> p a c", a=2)[:, :, 0:4 * NC],
                               ACT.Gelu_apprx_tanh).then_inc(s_gelu, 1)
            act.wait_ge(s_cm, 4)
            def exps(u, j, t):
                qt, b, U = u // 2, u % 4, u + 8 * t
                n = (qt + 1) * P
                act.wait_ge(s_nb, 1 + U)
                for r in range(2):
                    act.activation(pbuf[:, b, r, 0:n], pbuf[:, b, r, 0:n], ACT.Exp, scale=QSCALE,
                                   bias=stat[:, b, 4 + r:5 + r], accum_out=stat[:, b, 8 + r:9 + r])\
                        .then_inc(s_e, 1)
                act.activation(pcmp[:, b, 0:NC], pcmp[:, b, 0:NC], ACT.Exp, scale=QSCALE,
                               bias=stat[:, b, 6:7], accum_out=stat[:, b, 10:11]).then_inc(s_e, 1)

            def keep_turned(u, j, t):
                n, U = (u // 2 + 1) * P, u + 8 * t
                act.wait_ge(s_T, 1 + U)
                if some(U - 1):
                    act.wait_ge(s_pv, U - 1)
                act.activation(ptc[:, u % 2, :], bank[5][0:NC, 0:P], ACT.Copy)
                act.activation(pt[:, u % 2, 1, 0:n], bank[4][:, 0:n], ACT.Copy).then_inc(s_ta, 1)

            def tile(t, j, jp):
                for k in range(8 if j is not None else 3):
                    for stage, lag in ((exps, 0), (keep_turned, 2)):
                        at_ = unit(k, lag, t, j, jp)
                        if at_:
                            stage(*at_)
                    if k == 7:
                        act.wait_ge(s_pv, 4 + 8 * t)
                        act.activation(xhi[:, t, 0:256], bank[6][:, 0:256], ACT.Copy).then_inc(s_oh, 1)
                    if (k == 3 or j is None and k == 2) and jp is not None:
                        act.wait_ge(s_pv, 8 * t)
                        act.activation(xhi[:, t - 1, 256:512], bank[7][:, 0:256], ACT.Copy).then_inc(s_xh, 1)
            tiles_of_q(act, tile)
            project_out("NSA_OUT", m_alt, Q_NSA_POST)
            operands("UP1", lambda j: col("gains", 16 + j), 0)
            ffn_up("UP1", 0, 0, Q_F1_PRE)
            project_out("DOWN1", m_x, Q_F1_POST)
            operands("SSD_IN", lambda j: col("gains", 32 + j), 8)

            st = START["SSD_IN"]
            zone = {"z": False}

            def ssd_tap(c, i):
                k = c + 4 * i
                act.wait_ge(s_ev, EV["SSD_IN"] + c + 1 + 4 * i)
                if some(c - 1 + 4 * i):
                    act.wait_ge(s_cv, c - 1 + 4 * i)
                act.activation(cacc[:, c % 2, :], spad[:, 3:3 + S], ACT.Identity,
                               scale=par[:, bass.ds(COL["ssd_w"] + 4 * k + 3, 1)],
                               bias=par[:, bass.ds(COL["ssd_b"] + k, 1)]).then_inc(s_tap, 1)

            def ssd_silu(c, i, z):
                if z:
                    act.wait_ge(s_ev, EV["SSD_IN"] + c + 1 + 4 * i)
                    dst = zb[:, c - 24 + 4 * i, :]
                else:
                    act.wait_ge(s_cacc, c + 1 + 4 * i)
                    dst = cv[:, c + 4 * i, :]
                act.activation(dst, cacc[:, c % 2, :], ACT.Silu).then_inc(s_cv, 1)

            def ssd_step(c, i):
                z = zone["z"]
                weight_hi(st + c + 2, i)
                if static(i) and c == 0:
                    stats_root(Q_SSD_PRE)
                    return
                if static(i) and c == 1:
                    stats_keep(Q_SSD_PRE)
                    ssd_tap(0, 0)
                if c == 40:
                    return
                if z:
                    ssd_silu(c, i, True)
                    return
                ssd_tap(c, i)
                ssd_silu(c - 1, i, False)

            ssd_walk(act, ssd_step, zone, between=lambda: ssd_silu(23, 0, False))
            act.wait_ge(s_dt, 1)
            act.activation(dw[:, 1, :], dw[:, 0, :], ACT.Abs).then_inc(s_dta, 1)
            act.wait_ge(s_dta, 1)
            act.activation(dw[:, 1, :], dw[:, 1, :], ACT.Exp, scale=-1.0).then_inc(s_dta, 1)
            act.activation(hpar[:, 2:3], hpar[:, 1:2], ACT.Exp).then_inc(s_dta, 1)
            act.wait_ge(s_dt, 2)
            act.activation(dw[:, 3, :], dw[:, 2, :], ACT.Ln).then_inc(s_dta, 1)
            act.wait_ge(s_acv, 1)
            act.activation(acs[:, 1:3, :, :], acs[:, 1:3, :, :], ACT.Exp).then_inc(s_dec, 1)

            def group_square(G):
                c, g = G // 4, G % 4
                act.wait_ge(s_yk, G + 1)
                if G:
                    act.wait_ge(s_gs, G)
                act.activation(tmp[:, 1, :].rearrange("p (r l) -> p r l", r=4),
                               zb[:, 4 * g:4 * g + 4, c * P:(c + 1) * P], ACT.Square).then_inc(s_gq, 1)

            for G in range(4 * NT):
                c, g = G // 4, G % 4
                act.wait_ge(s_cb, G + 1)
                if G >= 2:
                    act.wait_ge(s_w, 2 * G - 2)
                act.activation(cbuf[:, G % 2, :], bank[6][:, 0:P], ACT.Copy).then_inc(s_cbk, 1)
                for v in range(2):
                    U = 2 * G + v
                    act.wait_ge(s_ein, U + 1)
                    if c:
                        if U - 8 >= 4:
                            act.wait_ge(s_y, U - 3)
                        act.activation(xbuf[:, U % 4, :], bank[v][:, :], ACT.Exp).then_inc(s_xe, 1)
                    act.activation(segs(U), segs(U), ACT.Exp).then_inc(s_ee, 1)
                if g == 0 and c < NT - 1:
                    act.wait_ge(s_xtp, 5 * (c + 1))
                    if c:
                        act.wait_ge(s_st, 4 * c)
                    act.activation(btok[:, :, :].rearrange("p g n -> p (g n)"), bank[4][:, :], ACT.Copy)\
                        .then_inc(s_bt, 1)
                if G >= 2:
                    group_square(G - 2)
            group_square(4 * NT - 2)
            group_square(4 * NT - 1)
            act.wait_ge(s_gn, 1)
            act.activation(gst[:, 1, :], gst[:, 0, :], ACT.Sqrt).then_inc(s_gr, 1)
            for j in range(NZ):
                act.wait_ge(s_hid, KF + j + 1)
                act.activation(yhi[:, j, :], zb[:, j, :], ACT.Copy).then_inc(s_xh, 1)
            project_out("SSD_OUT", m_x, Q_SSD_POST)
            operands("UP2", lambda j: col("gains", 48 + j), 16)
            ffn_up("UP2", 1, KF + NZ, Q_F2_PRE)
            project_out("DOWN2", m_x, Q_F2_POST)

            def modulated(updated, shift, made):
                for j in range(KD):
                    act.wait_ge(s_h, updated + j + 1)
                    square(h[:, j, :], j, KD)
                stats_root(Q_CONV_PRE if shift == 0 else Q_F3_PRE)
                for j in range(KD):
                    act.wait_ge(s_hid, made + j + 1)
                    act.activation(xhi[:, j, :], tmp[:, j % 2, :], ACT.Identity,
                                   bias=mod[:, shift * KD + j:shift * KD + j + 1]).then_inc(s_xh, 1)

            modulated(24, 0, 2 * KF + NZ)

            def conv_post(c, i):
                if c >= 16:
                    act.wait_ge(s_hid, 2 * KF + NZ + KD + c - 16 + 1)
                    act.activation(yc_hi[:, c - 16, :], cyt[:, c % 2, :], ACT.Copy).then_inc(s_xh, 1)

            st = START["CONV_IN"]
            for c in range(24):
                weight_hi(st + c + 2, 0)
                conv_post(c, 0)
            project_out("CONV_OUT", m_conv, Q_CONV_POST)
            modulated(32, 3, 2 * KF + NZ + 2 * KD)
            base_t = 2 * KF + NZ + 3 * KD

            def up3_post(c, i):
                if c % 2 == 0:
                    act.wait_ge(s_pe, START["UP3"] + c + 1 + 4 * i)
                    if not static(i) or c >= 2:
                        act.wait_ge(s_hid, base_t + c // 2 + 2 * i)
                    act.activation(sg[:, :], psum_ap(c % 4), ACT.Silu).then_inc(s_sg, 1)
                else:
                    act.wait_ge(s_hid, base_t + c // 2 + 1 + 2 * i)
                    act.activation(hid_hi[:, c // 2 + 2 * i, :], hid[:, :], ACT.Copy).then_inc(s_xh, 1)
            project_in("UP3", up3_post)
            project_out("DOWN3", m_x, Q_F3_POST)
            for j in range(KD):
                act.wait_ge(s_h, 40 + j + 1)
                act.dma_start(out[:, j, :], h[:, j, :]).then_inc(s_out, 16)
            act.wait_ge(s_out, 16 * 8)

        @block.vector
        def _(dve):
            chain = Chain(dve, s_dve)

            def weight_lo(g, i):
                if g >= TOTAL:
                    return
                n = PANEL_BLOCKS[g] * P
                dve.wait_ge(s_hi, g + 1 + 4 * i)
                dve.tensor_tensor(wlo[g % 2][:, 0:n], raw[g % 4][:, 0:n], whi[g % 2][:, 0:n].bitcast(F32),
                                  ALU.subtract).then_inc(s_lo, 1)

            def stats(q, width):
                dve.wait_ge(s_stat, q + 1)
                dve.tensor_scalar(ms, stat_ps[:, 0:4], 1.0 / width, EPS, ALU.mult, ALU.add).then_inc(s_ms, 1)
                dve.wait_ge(s_sqrt, q + 1)
                dve.reciprocal(rt, root).then_inc(s_rt, 1)

            def operand_lo(name, j, gain):
                dve.wait_ge(s_xh, XT[name] + j + 1)
                dve.scalar_tensor_tensor(out=xlo[:, j, :], in0=h[:, j, :], scalar=gain(j),
                                         in1=xhi[:, j, :].bitcast(F32), op0=ALU.mult, op1=ALU.subtract)\
                    .then_inc(s_xt, 1)

            def update(q, m, post_gain):
                dve.wait_ge(s_bc, q + 1)
                for j in range(KD):
                    chain(dve.scalar_tensor_tensor(out=tmp[:, j % 2, :], in0=m[:, j, :], scalar=post_gain(j),
                                                   in1=bc_ps[:, :], op0=ALU.mult, op1=ALU.mult))
                    chain.wait()
                    dve.tensor_tensor(h[:, j, :], tmp[:, j % 2, :], h[:, j, :], ALU.add).then_inc(s_h, 1)

            def update_ahead(q, m, post_gain, name, pre_gain, updated, squared):
                dve.wait_ge(s_bc, q + 1)
                for j in range(KD):
                    if j >= 2:
                        dve.wait_ge(s_h, updated + j - 1)
                    dve.scalar_tensor_tensor(out=tmp[:, j % 2, :], in0=m[:, j, :], scalar=post_gain(j),
                                             in1=bc_ps[:, :], op0=ALU.mult, op1=ALU.mult).then_inc(s_add, 1)
                    if j >= 2:
                        operand_lo(name, j - 2, pre_gain)
                operand_lo(name, KD - 2, pre_gain)
                operand_lo(name, KD - 1, pre_gain)
                for j in range(1, KD):
                    n = squared // KD * (KD - 1) + j
                    dve.wait_ge(s_sa, squared + j + 1)
                    if j > 1:
                        dve.wait_ge(s_pa, n - 1)
                    first = sqr[:, 0, :] if j == 1 else ssum[:, :]
                    ins = dve.tensor_tensor(ssum[:, :], first, sqr[:, j % 2, :], ALU.add)
                    ins.then_inc(s_pa, 1)
                dve.wait_ge(s_pa, n)
                dve.sem_inc(s_sq, 1)

            def project_out(name, m, q):
                st, per, n = START[name], PER_TILE[name], COUNT[name]
                mv = MV[name]

                def step(c, i):
                    if static(i) and c == n - 1:
                        stats(q, D)
                        weight_lo(st + n + 1, 0)
                        dve.wait_ge(s_m, mv + KD)
                        return
                    weight_lo(st + c + 2, i)
                    if c % per == per - 1:
                        t, ti = c // per, (4 // per) * i
                        dve.wait_ge(s_m, mv + t + 1 + ti)
                        mt = m[:, t + ti, :]
                        if t == 0 and static(i):
                            chain(dve.tensor_tensor(ssum[:, :], mt, mt, ALU.mult))
                            return
                        chain.wait()
                        chain(dve.tensor_tensor(tmp[:, 0, :], mt, mt, ALU.mult))
                        chain.wait()
                        ins = dve.tensor_tensor(ssum[:, :], ssum[:, :], tmp[:, 0, :], ALU.add)
                        if static(i) and t == KD - 2:
                            ins.then_inc(s_sq, 1)
                        else:
                            chain(ins)
                walk(dve, n, step, chain, per=8 // per)

            def ffn_up(name, layer, xt_at, tile_at, q):
                st, ev = START[name], EV[name]

                def lo_of(c, i):
                    dve.wait_ge(s_xh, xt_at + c // 2 + 1 + 2 * i)
                    dve.tensor_tensor(hid_lo[:, c // 2 + 2 * i, :], hid[:, :],
                                      hid_hi[:, c // 2 + 2 * i, :].bitcast(F32), ALU.subtract).then_inc(s_xt, 1)

                def evacuate(c, i):
                    dve.wait_ge(s_pe, st + c + 1 + 4 * i)
                    dve.tensor_tensor(upad[:, c % 2, 2:2 + S], psum_ap(c % 4), rstd_b[:, :], ALU.mult)\
                        .then_inc(s_ev, 1)

                def convolve(c, i):
                    v = c % 2
                    k = layer * 44 + c + 4 * i
                    dve.wait_ge(s_tap, layer * (44 + CH) + c + 1 + 4 * i)
                    chain(dve.scalar_tensor_tensor(out=tmp[:, v, :], in0=upad[:, v, 1:1 + S],
                                                   scalar=par[:, bass.ds(COL["ffn_w"] + 3 * k + 1, 1)],
                                                   in1=tmp[:, v, :], op0=ALU.mult, op1=ALU.add))
                    chain.wait()
                    ins = dve.scalar_tensor_tensor(out=tmp[:, v, :], in0=upad[:, v, 0:S],
                                                   scalar=par[:, bass.ds(COL["ffn_w"] + 3 * k, 1)],
                                                   in1=tmp[:, v, :], op0=ALU.mult, op1=ALU.add)
                    if v == 0:
                        ins.then_inc(s_cg, 1)
                        if static(i) and c == 0:
                            return
                        lo_of(c - 2, i)
                    else:
                        chain(ins)
                        dve.wait_ge(s_sg, layer * KF + c // 2 + 1 + 2 * i)
                        chain.wait()
                        dve.tensor_tensor(hid[:, :], sg[:, :], tmp[:, 1, :], ALU.mult).then_inc(s_hid, 1)

                def step(c, i):
                    if static(i) and c == 0:
                        weight_lo(st + 2, 0)
                        stats(q, D)
                        return
                    if static(i) and c == 1:
                        weight_lo(st + 3, 0)
                        dve.wait_ge(s_rb, KEPT[q])
                        evacuate(0, 0)
                        evacuate(1, 0)
                        convolve(0, 0)
                        convolve(1, 0)
                        return
                    evacuate(c, i)
                    weight_lo(st + c + 2, i)
                    convolve(c, i)

                walk(dve, 44, step, chain, per=6)
                lo_of(42, 0)

            dve.wait_ge(s_in, 64)
            dve.wait_ge(s_const, 1)
            weight_lo(0, 0)
            weight_lo(1, 0)
            for j in range(KD):
                operand_lo("NSA_IN", j, lambda k: col("gains", k))

            def nsa_take(c, i):
                dve.wait_ge(s_pe, c + 1 + 4 * i)
                if static(i) and c == 16:
                    dve.tensor_tensor(gt[:, :], bank[0][0:48, :], rstd_b[0:48, :], ALU.mult).then_inc(s_ev, 1)
                else:
                    dve.tensor_tensor(qkv[:, c + 4 * i, :], psum_ap(c % 4), rstd_b[:, :], ALU.mult)\
                        .then_inc(s_ev, 1)

            def nsa_step(c, i):
                weight_lo(START["NSA_IN"] + c + 2, i)
                if static(i) and c == 0:
                    stats(Q_NSA_PRE, D)
                    return
                if static(i) and c == 1:
                    dve.wait_ge(s_rb, 1)
                    nsa_take(0, 0)
                if static(i) and c > 16:
                    return
                nsa_take(c, i)
            walk(dve, 21, nsa_step, chain, 0)
            dve.wait_ge(s_pe, 21)
            for t in range(NT):
                ins = dve.tensor_scalar(vtok[:, t, :], bank[4 + t][:, :], rt[:, t:t + 1], None, ALU.mult)
            ins.then_inc(s_v, 1)
            dve.wait_ge(s_swp, 32)
            dve.wait_ge(s_ev, 12)
            for kv in range(2):
                if kv:
                    dve.wait_ge(s_cm, 1)
                for a in range(2):
                    rows = slice(a * HD, (a + 1) * HD)
                    for b in range(2):
                        src = qkv[rows, 8 + 2 * kv:10 + 2 * kv, :] if a == b else swp[rows, 2 * kv:2 * kv + 2, :]
                        src = src.rearrange("p j (c r) -> p r j c", r=16)[:, a:16:2]
                        for mh in range(2):
                            pos = par[rows, COL["pos"] + 16 * kv + 8 * mh:COL["pos"] + 16 * kv + 8 * mh + 8]
                            for jt in range(2):
                                ins = dve.tensor_tensor(
                                    flat[rows, 8 * mh:8 * mh + 8, b + 2 * jt, :], src[:, :, jt, mh:mh + NC],
                                    pos.unsqueeze(2).to_broadcast([HD, 8, NC]), ALU.add)
                ins.then_inc(s_flat, 1)
            dve.wait_ge(s_gtp, 1)
            chain(dve.tensor_copy(gtok[:, :, :].rearrange("p t n -> p (t n)"), bank[1][:, 0:NT * 48]))
            dve.wait_ge(s_cm, 2)
            dve.tensor_copy(kct[:, :, :].rearrange("p j c -> p (j c)"), bank[2][:, 0:2 * NC]).then_inc(s_kv, 1)
            dve.wait_ge(s_cm, 4)
            dve.tensor_copy(vct[:, :, :].rearrange("p g d -> p (g d)"), bank[3][0:NC, 0:4 * HD]).then_inc(s_kv, 1)

            chain.wait()

            def masked(u, j, t):
                qt, b, U = u // 2, u % 4, u + 8 * t
                n = (qt + 1) * P
                if u == 0:
                    dve.tensor_copy(qst[:, :], qkv[:, t, :]).then_inc(s_qst, 1)
                dve.wait_ge(s_S, 1 + U)
                if some(U - 3):
                    dve.wait_ge(s_T, U - 3)
                dve.sem_inc(s_carry[1], 1)
                for r in range(2):
                    dve.tensor_tensor_reduce(pbuf[:, b, r, 0:n], bank[r][:, 0:n], mbig[:, S - n:S], 1.0,
                                             -3e38, ALU.add, ALU.max, stat[:, b, r:r + 1])
                dve.tensor_tensor_reduce(pcmp[:, b, 0:NC], bank[2][:, 0:NC], mcmp[:, qt, :], 1.0,
                                         -3e38, ALU.add, ALU.max, stat[:, b, 2:3]).then_inc(s_sc, 1)
                dve.wait_ge(s_sc, 1 + U)
                dve.tensor_scalar(stat[:, b, 4:7], stat[:, b, 0:3], -QSCALE, None, ALU.mult)\
                    .then_inc(s_nb, 1)

            def scaled(u, j, t):
                qt, b, U = u // 2, u % 4, u + 8 * t
                n = (qt + 1) * P
                dve.wait_ge(s_e, 3 + 3 * u + 24 * t)
                chain(dve.reciprocal(stat[:, b, 12:15], stat[:, b, 8:11]))
                gate = 3 * (4 * j + 4 * (u % 2))
                gsel = gtok[:, qt, bass.ds(gate + 3 * t + 1, 2)]
                gcmp = gtok[:, qt, bass.ds(gate + 3 * t, 1)]
                chain.wait()
                dve.tensor_tensor(stat[:, b, 16:18], stat[:, b, 12:14], gsel, ALU.mult)
                if qt == 0:
                    chain(dve.scalar_tensor_tensor(out=stat[:, b, 18:19], in0=stat[:, b, 14:15],
                                                   scalar=rowok[:, 0:1], in1=gcmp,
                                                   op0=ALU.mult, op1=ALU.mult))
                else:
                    chain(dve.tensor_tensor(stat[:, b, 18:19], stat[:, b, 14:15], gcmp, ALU.mult))
                chain.wait()
                chain(dve.tensor_scalar(pcmp[:, b, 0:NC], pcmp[:, b, 0:NC], stat[:, b, 18:19], None,
                                        ALU.mult))
                dve.tensor_scalar(pbuf[:, b, 0, 0:n], pbuf[:, b, 0, 0:n], stat[:, b, 16:17], None, ALU.mult)
                dve.tensor_scalar(pbuf[:, b, 1, 0:n], pbuf[:, b, 1, 0:n], stat[:, b, 17:18], None,
                                  ALU.mult).then_inc(s_P, 1)

            def keep_turned(u, j, t):
                n, U = (u // 2 + 1) * P, u + 8 * t
                dve.wait_ge(s_T, 1 + U)
                if some(U - 1):
                    dve.wait_ge(s_pv, U - 1)
                dve.tensor_copy(pt[:, u % 2, 0, 0:n], bank[3][:, 0:n]).then_inc(s_tv, 1)

            def tile(t, j, jp):
                for k in range(8 if j is not None else 3):
                    if k == 7:
                        dve.wait_ge(s_adap, 1 + t)
                        dve.tensor_copy(mod[:, bass.ds(6 * t, 6)], bank[2][:, 256:262]).then_inc(s_mod, 1)
                    for stage, lag in ((masked, 0), (scaled, 1), (keep_turned, 2)):
                        at_ = unit(k, lag, t, j, jp)
                        if at_:
                            stage(*at_)
                    if k == 0 and jp is not None:
                        dve.wait_ge(s_oh, t)
                        dve.tensor_tensor(xlo[:, t - 1, 0:256], bank[6][:, 0:256],
                                          xhi[:, t - 1, 0:256].bitcast(F32), ALU.subtract).then_inc(s_ol, 1)
                    if (k == 3 or j is None and k == 2) and jp is not None:
                        dve.wait_ge(s_xh, XT["NSA_OUT"] + t)
                        dve.tensor_tensor(xlo[:, t - 1, 256:512], bank[7][:, 0:256],
                                          xhi[:, t - 1, 256:512].bitcast(F32), ALU.subtract).then_inc(s_xt, 1)
            tiles_of_q(dve, tile, chain, 8 * 3)
            dve.wait_ge(s_mod, 8)
            chain(dve.tensor_tensor(mod[:, :], mod[:, :], par[:, COL["ada_b"]:COL["ada_b"] + 48], ALU.add))
            chain.wait()
            g2 = par[:, COL["gains2"]:COL["gains2"] + 32].rearrange("p (a k) -> p a k", a=4)
            md = mod[:, :].rearrange("p (a k) -> p a k", a=6)
            for f in range(2):
                chain(dve.tensor_scalar(gmod[:, 2 * f, :], md[:, 3 * f + 1, :], 1.0, None, ALU.add))
                chain.wait()
                chain(dve.tensor_tensor(gmod[:, 2 * f, :], gmod[:, 2 * f, :], g2[:, 2 * f, :], ALU.mult))
                chain(dve.tensor_tensor(gmod[:, 2 * f + 1, :], md[:, 3 * f + 2, :], g2[:, 2 * f + 1, :], ALU.mult))
                chain.wait()

            project_out("NSA_OUT", m_alt, Q_NSA_POST)
            update_ahead(Q_NSA_POST, m_alt, lambda j: col("gains", 8 + j), "UP1", lambda j: col("gains", 16 + j),
                         0 * KD, 1 * KD)
            chain(dve.memset(upad[:, :, 0:2], 0.0))
            chain.wait()
            ffn_up("UP1", 0, XT["DOWN1"], 0, Q_F1_PRE)
            project_out("DOWN1", m_x, Q_F1_POST)
            update_ahead(Q_F1_POST, m_x, lambda j: col("gains", 24 + j), "SSD_IN", lambda j: col("gains", 32 + j),
                         1 * KD, 2 * KD)
            st, ev = START["SSD_IN"], EV["SSD_IN"]
            chain(dve.memset(spad[:, 0:3], 0.0))
            chain.wait()
            zone = {"z": False}

            def ssd_evacuate(c, i, z):
                dve.wait_ge(s_pe, st + c + 1 + 4 * i)
                if z:
                    dve.wait_ge(s_cv, c - 1 + 4 * i)
                    out_ = cacc[:, c % 2, :]
                else:
                    out_ = spad[:, 3:3 + S]
                dve.tensor_tensor(out_, psum_ap(c % 4), rstd_b[:, :], ALU.mult).then_inc(s_ev, 1)

            def ssd_convolve(c, i):
                k = c + 4 * i
                dve.wait_ge(s_tap, 44 + c + 1 + 4 * i)
                for tap in (2, 1, 0):
                    ins = dve.scalar_tensor_tensor(
                        out=cacc[:, c % 2, :], in0=spad[:, tap:tap + S],
                        scalar=par[:, bass.ds(COL["ssd_w"] + 4 * k + tap, 1)],
                        in1=cacc[:, c % 2, :], op0=ALU.mult, op1=ALU.add)
                    if tap:
                        chain(ins)
                        chain.wait()
                    else:
                        ins.then_inc(s_cacc, 1)
                dve.wait_ge(s_cacc, c + 1 + 4 * i)

            def ssd_step(c, i):
                if static(i) and c == 0:
                    weight_lo(st + 2, 0)
                    stats(Q_SSD_PRE, D)
                    return
                if c == 40:
                    weight_lo(st + 42, 0)
                    dve.wait_ge(s_pe, st + 41)
                    dve.tensor_tensor(dw[:, 0, :], bank[0][0:SH, :], rstd_b[0:SH, :], ALU.mult).then_inc(s_ev, 1)
                    return
                if static(i) and c == 1:
                    weight_lo(st + 3, 0)
                    dve.wait_ge(s_rb, KEPT[Q_SSD_PRE])
                    ssd_evacuate(0, 0, False)
                    ssd_convolve(0, 0)
                    ssd_evacuate(1, 0, False)
                    ssd_convolve(1, 0)
                    return
                z = zone["z"]
                ssd_evacuate(c, i, z)
                weight_lo(st + c + 2, i)
                if not z:
                    ssd_convolve(c, i)

            ssd_walk(dve, ssd_step, zone, chain, 8, 0)
            dve.wait_ge(s_ev, EV["UP2"])
            chain(dve.tensor_scalar(dw[:, 4, :], dw[:, 0, :], hpar[:, 0:1], None, ALU.add))
            chain.wait()
            dve.tensor_copy(dw[:, 0, :], dw[:, 4, :]).then_inc(s_dt, 1)
            dve.wait_ge(s_dta, 3)
            dve.tensor_scalar(dw[:, 2, :], dw[:, 1, :], 1.0, None, ALU.add).then_inc(s_dt, 1)
            dve.wait_ge(s_dt, 2)
            chain(dve.tensor_scalar(dw[:, 4, :], dw[:, 2, :], 1.0, 1e-30, ALU.subtract, ALU.max))
            chain.wait()
            chain(dve.reciprocal(dw[:, 4, :], dw[:, 4, :]))
            chain.wait()
            dve.tensor_tensor(dw[:, 4, :], dw[:, 4, :], dw[:, 1, :], ALU.mult).then_inc(s_dt, 1)
            dve.wait_ge(s_dt, 3)
            dve.wait_ge(s_dta, 4)
            chain(dve.tensor_tensor(dw[:, 3, :], dw[:, 3, :], dw[:, 4, :], ALU.mult))
            chain(dve.tensor_scalar(dw[:, 2, :], dw[:, 2, :], 1.0, None, ALU.is_equal))
            chain.wait()
            dve.tensor_tensor(dw[:, 2, :], dw[:, 2, :], dw[:, 1, :], ALU.mult).then_inc(s_dt, 1)
            dve.wait_ge(s_dt, 4)
            dve.tensor_tensor(dw[:, 3, :], dw[:, 3, :], dw[:, 2, :], ALU.add).then_inc(s_dt, 1)
            dve.wait_ge(s_dt, 5)
            dve.scalar_tensor_tensor(out=dtt[:, 0, :], in0=dw[:, 0, :], scalar=0.0, in1=dw[:, 3, :],
                                     op0=ALU.max, op1=ALU.add).then_inc(s_dt, 1)
            dve.tensor_scalar(hpar[:, 3:4], hpar[:, 2:3], -1.0, None, ALU.mult).then_inc(s_dt, 1)
            dve.wait_ge(s_dt, 7)
            dve.tensor_scalar(dtt[:, 1, :], dtt[:, 0, :], hpar[:, 3:4], None, ALU.mult).then_inc(s_dt, 1)
            dve.wait_ge(s_dtp, 1)
            dve.tensor_copy(dtk[:, :, :, :].rearrange("p t r h -> p (t r h)"), bank[5][:, 0:NT * 2 * SH])\
                .then_inc(s_dtk, 1)
            dve.wait_ge(s_dtk, 1)
            dve.wait_ge(s_cv, 40)
            dve.wait_ge(s_const, 2)
            dve.wait_ge(s_ac, 1)
            sums = bank[5][:, 0:2 * NT * SH].rearrange("p (a c h) -> p a c h", a=2, c=NT)
            chain(dve.tensor_copy(acs[:, 0, :, :], sums[:, 0, :, :]))
            chain(dve.tensor_copy(acs[:, 2, :, :], sums[:, 1, :, :]))
            chain.wait()
            dve.tensor_tensor(acs[:, 1, :, :], acs[:, 2, :, :], acs[:, 0, :, :], ALU.subtract).then_inc(s_acv, 1)

            def x_dt(c, k):
                dve.wait_ge(s_xtp, 5 * c + k + 1)
                if c:
                    dve.wait_ge(s_y, 8 * (c - 1) + 2 * k + 2)
                    dve.wait_ge(s_xdec, 4 * (c - 1) + k + 1)
                dve.tensor_tensor(xdt[:, 8 * k:8 * k + 8, :], bank[k][:, :].rearrange("p (h d) -> p h d", h=8),
                                  dtk[:, c, 0, 8 * k:8 * k + 8].unsqueeze(2).to_broadcast([P, 8, HD]),
                                  ALU.mult).then_inc(s_xd, 1)

            def segments(G):
                c, g = G // 4, G % 4
                for v in range(2):
                    U = 2 * G + v
                    dve.wait_ge(s_lb, U + 1)
                    if U >= 4:
                        dve.wait_ge(s_y, U - 3)
                    for k in range(4):
                        hd = 8 * g + 4 * v + k
                        ins = dve.scalar_tensor_tensor(
                            out=segs(U)[:, k * P:(k + 1) * P], in0=bank[v][:, k * P:(k + 1) * P],
                            scalar=acs[:, 0, c, hd:hd + 1], in1=smask[:, :], op0=ALU.subtract, op1=ALU.add)
                    ins.then_inc(s_ein, 1)

            def weights(G):
                dve.wait_ge(s_cbk, G + 1)
                for v in range(2):
                    U = 2 * G + v
                    dve.wait_ge(s_ee, U + 1)
                    b = segs(U).rearrange("p (a l) -> p a l", a=4)
                    dve.tensor_tensor(b, b, cbuf[:, G % 2, :].unsqueeze(1).to_broadcast([P, 4, P]), ALU.mult)\
                        .then_inc(s_w, 1)

            def gated(G):
                c, g = G // 4, G % 4
                tok = slice(c * P, (c + 1) * P)
                dve.wait_ge(s_y, 2 * G + 2)
                if G:
                    dve.wait_ge(s_yk, G)
                for r in range(4):
                    chain(dve.scalar_tensor_tensor(
                        out=tmp[:, 0, r * P:(r + 1) * P], in0=cv[:, 8 + 4 * g + r, tok],
                        scalar=col("dskip", 4 * g + r), in1=bank[2 + g % 2][:, r * P:(r + 1) * P],
                        op0=ALU.mult, op1=ALU.add))
                chain.wait()
                dve.tensor_tensor(zb[:, 4 * g:4 * g + 4, tok], zb[:, 4 * g:4 * g + 4, tok],
                                  tmp[:, 0, :].rearrange("p (r l) -> p r l", r=4), ALU.mult).then_inc(s_yk, 1)
                if c < NT - 1:
                    dve.wait_ge(s_st, G + 1)
                    hs = slice(8 * g, 8 * g + 8)
                    pr = bank[7][:, :].rearrange("p (h d) -> p h d", h=8)
                    if c == 0:
                        dve.tensor_copy(state[:, hs, :], pr).then_inc(s_stk, 1)
                    else:
                        chain(dve.tensor_tensor(state[:, hs, :], state[:, hs, :],
                                                acs[:, 2, c, hs].unsqueeze(2).to_broadcast([P, 8, HD]), ALU.mult))
                        chain.wait()
                        dve.tensor_tensor(state[:, hs, :], state[:, hs, :], pr, ALU.add).then_inc(s_stk, 1)

            for k in range(4):
                x_dt(0, k)
            segments(0)
            weights(0)
            dve.wait_ge(s_dec, 1)
            for G in range(4 * NT):
                c, g = G // 4, G % 4
                if g < 3:
                    segments(G + 1)
                    if g:
                        gated(G - 1)
                    weights(G + 1)
                    continue
                gated(G - 1)
                if c < NT - 1:
                    x_dt(c + 1, 0)
                    x_dt(c + 1, 1)
                gated(G)
                if c < NT - 1:
                    segments(G + 1)
                    x_dt(c + 1, 2)
                    weights(G + 1)
                    x_dt(c + 1, 3)
            dve.wait_ge(s_gs, 4 * NT)
            dve.tensor_scalar(gst[:, 0, :], stat_ps[:, 0:4 * NT], 1.0 / (4 * P), EPS, ALU.mult, ALU.add)\
                .then_inc(s_gn, 1)
            dve.wait_ge(s_gr, 1)
            dve.reciprocal(gst[:, 2, :], gst[:, 1, :]).then_inc(s_gn, 1)

            def y_lo(j):
                dve.wait_ge(s_xh, XT["SSD_OUT"] + j + 1)
                dve.tensor_tensor(ylo[:, j, :], zb[:, j, :], yhi[:, j, :].bitcast(F32), ALU.subtract)\
                    .then_inc(s_xt, 1)

            for j in range(NZ):
                g = j // 4
                dve.wait_ge(s_gb, g + 1)
                dve.scalar_tensor_tensor(out=zb[:, j, :], in0=zb[:, j, :], scalar=col("norm_w", j),
                                         in1=bank[2 + g if g < 3 else 6][:, :], op0=ALU.mult, op1=ALU.mult)\
                    .then_inc(s_hid, 1)
                if j:
                    y_lo(j - 1)
            y_lo(NZ - 1)
            project_out("SSD_OUT", m_x, Q_SSD_POST)
            update_ahead(Q_SSD_POST, m_x, lambda j: col("gains", 40 + j), "UP2", lambda j: col("gains", 48 + j),
                         2 * KD, 3 * KD)
            chain(dve.memset(upad[:, :, 0:2], 0.0))
            chain.wait()
            ffn_up("UP2", 1, XT["DOWN2"], KF, Q_F2_PRE)
            project_out("DOWN2", m_x, Q_F2_POST)
            update(Q_F2_POST, m_x, lambda j: col("gains", 56 + j))

            def modulated(q, f, name):
                stats(q, D)
                dve.wait_ge(s_bc, q + 1)

                def low(j):
                    dve.wait_ge(s_xh, XT[name] + j + 1)
                    dve.scalar_tensor_tensor(out=xlo[:, j, :], in0=tmp[:, j % 2, :],
                                             scalar=mod[:, 24 * f + j:24 * f + j + 1],
                                             in1=xhi[:, j, :].bitcast(F32), op0=ALU.add, op1=ALU.subtract)\
                        .then_inc(s_xt, 1)
                for j in range(KD):
                    if j >= 2:
                        dve.wait_ge(s_xt, XT[name] + j - 1)
                    dve.scalar_tensor_tensor(out=tmp[:, j % 2, :], in0=h[:, j, :], scalar=gmod[:, 2 * f, j:j + 1],
                                             in1=bc_ps[:, :], op0=ALU.mult, op1=ALU.mult).then_inc(s_hid, 1)
                    if j:
                        low(j - 1)
                low(KD - 1)

            modulated(Q_CONV_PRE, 0, "CONV_IN")
            chain(dve.memset(cpad[:, 0:2], 0.0))
            chain.wait()
            st, ev = START["CONV_IN"], EV["CONV_IN"]

            def conv_low(t):
                dve.wait_ge(s_xh, XT["CONV_OUT"] + t + 1)
                dve.tensor_tensor(yc_lo[:, t, :], cyt[:, t % 2, :], yc_hi[:, t, :].bitcast(F32), ALU.subtract)\
                    .then_inc(s_xt, 1)

            for c in range(24):
                weight_lo(st + c + 2, 0)
                dve.wait_ge(s_pe, st + c + 1)
                t = c % 8
                if c < 8:
                    dve.tensor_copy(cc[:, t, :], psum_ap(c % 4)).then_inc(s_ev, 1)
                elif c < 16:
                    dve.wait_ge(s_ev, ev + 8)
                    chain.wait()
                    dve.tensor_tensor(cpad[:, 2:2 + S], psum_ap(c % 4), cc[:, t, :], ALU.mult).then_inc(s_ev, 1)
                    dve.wait_ge(s_ev, ev + c + 1)
                    chain(dve.tensor_scalar(cy[:, t, :], cpad[:, 2:2 + S], col("cw", 3 * t + 2), None, ALU.mult))
                    for tap in (1, 0):
                        chain.wait()
                        chain(dve.scalar_tensor_tensor(out=cy[:, t, :], in0=cpad[:, tap:tap + S],
                                                       scalar=col("cw", 3 * t + tap), in1=cy[:, t, :],
                                                       op0=ALU.mult, op1=ALU.add))
                else:
                    chain.wait()
                    if t >= 2:
                        dve.wait_ge(s_xt, XT["CONV_OUT"] + t - 1)
                    chain(dve.tensor_tensor(cyt[:, t % 2, :], psum_ap(c % 4), cy[:, t, :], ALU.mult))
                    chain.wait()
                    dve.tensor_copy(small[:, 28:29], rt[:, 0:1]).then_inc(s_ev, 1)
                    dve.tensor_copy(small[:, 27:28], rt[:, 0:1]).then_inc(s_hid, 1)
                    if t:
                        conv_low(t - 1)
            conv_low(7)
            project_out("CONV_OUT", m_conv, Q_CONV_POST)
            update(Q_CONV_POST, m_conv, lambda j: gmod[:, 1, j:j + 1])
            modulated(Q_F3_PRE, 1, "UP3")
            st, ev = START["UP3"], EV["UP3"]

            def low3(c, i):
                t = c // 2 + 2 * i
                dve.wait_ge(s_xh, XT["DOWN3"] + 1 + t)
                dve.tensor_tensor(hid_lo[:, t, :], hid[:, :], hid_hi[:, t, :].bitcast(F32), ALU.subtract)\
                    .then_inc(s_xt, 1)

            def step3(c, i):
                weight_lo(st + c + 2, i)
                if c % 2 == 0:
                    if not static(i) or c:
                        low3(c - 2, i)
                    dve.wait_ge(s_sg, 2 * KF + c // 2 + 1 + 2 * i)
                    dve.tensor_copy(small[:, 28:29], rt[:, 0:1]).then_inc(s_ev, 1)
                else:
                    dve.wait_ge(s_pe, st + c + 1 + 4 * i)
                    dve.wait_ge(s_xt, XT["DOWN3"] + c // 2 + 2 * i)
                    chain(dve.tensor_tensor(hid[:, :], psum_ap(c % 4), sg[:, :], ALU.mult))
                    chain.wait()
                    dve.tensor_copy(small[:, 28:29], rt[:, 0:1]).then_inc(s_ev, 1)
                    dve.tensor_copy(small[:, 27:28], rt[:, 0:1]).then_inc(s_hid, 1)
            walk(dve, 44, step3, chain, 2)
            low3(42, 0)
            project_out("DOWN3", m_x, Q_F3_POST)
            update(Q_F3_POST, m_x, lambda j: gmod[:, 3, j:j + 1])


def pack(inputs):
    v = {k: np.asarray(a) for k, a in inputs.items()}

    def panels(w):
        k, f = w.shape
        return w.reshape(k // P, P, f // P, P).transpose(2, 1, 0, 3).reshape(f // P, P, k)

    def halves(w):
        k, f = w.shape
        w = w.reshape(2, k // 2 // P, P, f // P, P).transpose(3, 0, 2, 1, 4)
        return w.reshape(2 * f // P, P, k // 2)

    def paired(a, b):
        return np.stack([panels(a), panels(b)], 1).reshape(2 * a.shape[1] // P, P, a.shape[0])

    w = v["nsa_w_in"][0]
    q = w[:, :D].reshape(D, 2, 2, 4, HD).transpose(0, 1, 3, 2, 4).reshape(D, D)
    kv = w[:, D:D + 6 * 256].reshape(D, 6, 256)
    gates = w[:, D + 6 * 256:]
    vv = np.concatenate([kv[:, 3], kv[:, 5]], 1).reshape(4, 2, P, 512).transpose(0, 2, 1, 3).reshape(4, P, 1024)
    nsa_out = v["nsa_w_out"][0].reshape(2, 2, 4, HD, D).transpose(0, 2, 1, 3, 4).reshape(D, D)
    sw = v["ssd_w_in"][0]
    di = NZ * P
    order = np.concatenate([np.arange(di, di + 1024), np.arange(di)])
    dt = sw[:, 2 * di + 1024:]
    cw = v["conv_w_in_2"][0]
    up, down = v["ffn_w_up"], v["ffn_w_down"]
    gu = v["ffn_w_gate_up_2"][0]
    w8 = np.concatenate(
        [panels(q)] + [panels(kv[:, n]) for n in (0, 1, 2, 4)]
        + [panels(np.concatenate([gates, gates, gates[:, :32]], 1)), vv, panels(nsa_out),
           paired(up[0][:, FH:], up[0][:, :FH]),
           panels(sw[:, di:2 * di + 1024][:, order]), panels(sw[:, :di]), panels(np.concatenate([dt] * 4, 1)),
           halves(v["ssd_w_out"][0]), paired(up[1][:, FH:], up[1][:, :FH]),
           panels(cw[:, D:2 * D]), panels(cw[:, 2 * D:]), panels(cw[:, :D]), panels(v["conv_w_out_2"][0]),
           paired(gu[:, :FH], gu[:, FH:])])
    w11 = np.concatenate([halves(down[0]), halves(down[1]), halves(v["ffn_w_down_2"][0])])

    def cols(a):
        return a.reshape(-1, P).T

    def taps(a, tiles):
        return a.reshape(a.shape[0], tiles, P).transpose(2, 1, 0).reshape(P, -1)

    def pair_cols(a):
        return np.stack([a[..., FH:].reshape(-1, KF, P), a[..., :FH].reshape(-1, KF, P)], 2).reshape(-1, 2 * FH)

    par = np.concatenate(
        [cols(v["norm_gains"]), cols(v["norm_gains_2"]), taps(v["ssd_conv_w"][0][:, order], CH),
         cols(v["ssd_conv_b"][0][order])]
        + [taps(pair_cols(v["ffn_conv_w"][n]), 44) for n in range(2)]
        + [cols(pair_cols(v["ffn_conv_b"][n])) for n in range(2)]
        + [cols(np.repeat(v["ssd_d"][0], HD)), cols(v["ssd_norm_w"][0]), cols(v["c_2"][0]), cols(v["ada_b_2"][0]),
           v["nsa_cmp_pos"][0].reshape(2, 16, 2, HD).transpose(2, 3, 0, 1).reshape(P, 32),
           v["nsa_cmp_w2"][0].reshape(2, 2, P, HD).transpose(2, 0, 1, 3).reshape(P, 256),
           taps(v["conv_w_2"][0], KD)], 1)
    return {
        "w8": w8, "w11": w11, "xT": v["x"][0].T.reshape(KD, P, S).transpose(1, 0, 2), "params": par,
        "heads": np.stack([v["ssd_dt_bias"][0], v["ssd_a_log"][0]], 1),
        "w_cmp": v["nsa_cmp_w1"][0].reshape(2, 16, P, 256).transpose(0, 2, 1, 3),
        "w_ada": v["ada_w_2"][0].reshape(KD, P, ADA_SLICES, ADA_SLICE).transpose(2, 0, 1, 3),
    }


def kernel(**inputs):
    import concourse.bacc as bacc
    from concourse.bass_utils import run_bass_kernel_spmd as run

    nc = bacc.Bacc("TRN2", target_bir_lowering=False, num_devices=1)
    arrays, args = {}, []
    for name, a in pack(inputs).items():
        arrays[name] = np.ascontiguousarray(a)
        args.append(nc.dram_tensor(name, arrays[name].shape, F32, kind="ExternalInput").ap())
    out = nc.dram_tensor("out_t", (P, KD, S), F32, kind="ExternalOutput").ap()
    build(nc, *args, out)
    r = run(nc, [arrays], core_ids=[0])
    return r.results[0]["out_t"].transpose(2, 1, 0).reshape(1, S, D)
```
